# Optimizing a Trainium2 kernel written in Bass

```python
import math
import jax, jax.numpy as jnp
from jax import lax
import numpy as np

D_MODEL = 1024
BATCH = 1
SEQ = 256
DEPTH = 2

N_MEM = 256
N_MIXERS = 2
D_MIX = D_MODEL
ML_HEADS = 4
ML_HEAD_DIM = 192
ML_WIDTH = ML_HEADS * ML_HEAD_DIM
ML_CHUNK = 64
RG_WIDTH = 768
RG_BLOCKS = 8
RG_BLOCK_DIM = RG_WIDTH // RG_BLOCKS
RG_CONV = 4
RG_C = 8.0
XA_HEADS = 4
XA_HEAD_DIM = 64
XA_WIDTH = XA_HEADS * XA_HEAD_DIM
PEER_HEADS = 8
PEER_KEYS = 128
PEER_EXPERTS = PEER_KEYS * PEER_KEYS
PEER_HALF = 128
PEER_QDIM = 2 * PEER_HALF
PEER_TOPK = 16
PEER_TOK_BLOCK = 128
DN_ALPHA = (2 * DEPTH) ** 0.25
DN_BETA = (8 * DEPTH) ** -0.25
LN_EPS = 1e-5
N_A = (DEPTH + 1) // 2
N_B = DEPTH // 2
ML_IN = 4 * ML_WIDTH + 2 * ML_HEADS + XA_WIDTH
RG_IN = 2 * RG_WIDTH + XA_WIDTH


def layer_norm(x, g, b):
    xf = x.astype(jnp.float32)
    mu = jnp.mean(xf, axis=-1, keepdims=True)
    var = jnp.mean(jnp.square(xf - mu), axis=-1, keepdims=True)
    y = (xf - mu) * lax.rsqrt(var + LN_EPS) * g.astype(jnp.float32) + b.astype(jnp.float32)
    return y.astype(x.dtype)

def cross_attention(xq, mem, w_kv):
    B, S, _ = xq.shape
    M = mem.shape[1]
    q = xq.reshape(B, S, XA_HEADS, XA_HEAD_DIM).astype(jnp.float32)
    kv = (mem @ w_kv).astype(jnp.float32)
    k = kv[..., :XA_WIDTH].reshape(B, M, XA_HEADS, XA_HEAD_DIM)
    v = kv[..., XA_WIDTH:].reshape(B, M, XA_HEADS, XA_HEAD_DIM)
    s = jnp.einsum('bshd,bmhd->bhsm', q, k) * (XA_HEAD_DIM ** -0.5)
    p = jax.nn.softmax(s, axis=-1)
    o = jnp.einsum('bhsm,bmhd->bshd', p, v)
    return o.reshape(B, S, XA_WIDTH).astype(xq.dtype)

def mlstm_mixer(zm, b_gates, norm_g):
    B, S, _ = zm.shape
    H, dh, L = ML_HEADS, ML_HEAD_DIM, ML_CHUNK
    nc = S // L
    W = ML_WIDTH
    q, k, v, o, g = jnp.split(zm, [W, 2 * W, 3 * W, 4 * W], axis=-1)
    g = g.astype(jnp.float32) + b_gates.astype(jnp.float32)
    ig = g[..., :H]
    lf = jax.nn.log_sigmoid(g[..., H:])

    def to_chunks(t):
        return t.astype(jnp.float32).reshape(B, nc, L, H, dh).transpose(1, 0, 3, 2, 4)

    def gate_chunks(t):
        return t.reshape(B, nc, L, H).transpose(1, 0, 3, 2)

    qc = to_chunks(q)
    kc = to_chunks(k) * (dh ** -0.5)
    vc = to_chunks(v)
    causal = jnp.tril(jnp.ones((L, L), dtype=bool))

    def step(carry, inp):
        C, n, m = carry
        qq, kk, vv, ii, ff = inp
        b = jnp.cumsum(ff, axis=-1)
        dmat = b[..., :, None] - b[..., None, :] + ii[..., None, :]
        dmat = jnp.where(causal, dmat, -jnp.inf)
        inter = b + m[..., None]
        mj = jnp.maximum(jnp.max(dmat, axis=-1), inter)
        w = jnp.exp(dmat - mj[..., None])
        s = jnp.einsum('bhld,bhsd->bhls', qq, kk) * w
        sc = jnp.exp(inter - mj)
        num = sc[..., None] * jnp.einsum('bhld,bhde->bhle', qq, C) + jnp.einsum('bhls,bhse->bhle', s, vv)
        den = sc * jnp.einsum('bhld,bhd->bhl', qq, n) + jnp.sum(s, axis=-1)
        h = num / jnp.maximum(jnp.abs(den), jnp.exp(-mj))[..., None]
        bl = b[..., -1]
        gl = bl[..., None] - b + ii
        m_new = jnp.maximum(bl + m, jnp.max(gl, axis=-1))
        wg = jnp.exp(gl - m_new[..., None])
        decay = jnp.exp(bl + m - m_new)
        C_new = decay[..., None, None] * C + jnp.einsum('bhl,bhld,bhle->bhde', wg, kk, vv)
        n_new = decay[..., None] * n + jnp.einsum('bhl,bhld->bhd', wg, kk)
        return (C_new, n_new, m_new), h

    init = (jnp.zeros((B, H, dh, dh), jnp.float32), jnp.zeros((B, H, dh), jnp.float32),
            jnp.zeros((B, H), jnp.float32))
    _, hc = lax.scan(step, init, (qc, kc, vc, gate_chunks(ig), gate_chunks(lf)))
    h = hc.transpose(1, 0, 3, 2, 4).reshape(B, S, H, dh)
    mu = jnp.mean(h, axis=-1, keepdims=True)
    var = jnp.mean(jnp.square(h - mu), axis=-1, keepdims=True)
    hn = (h - mu) * lax.rsqrt(var + LN_EPS) * norm_g.astype(jnp.float32).reshape(H, dh)
    y = hn.reshape(B, S, W) * jax.nn.sigmoid(o.astype(jnp.float32))
    return y.astype(zm.dtype)

def rglru_mixer(zr, conv_w, conv_b, w_a, b_a, w_x, b_x, lam):
    B, S, _ = zr.shape
    gate = zr[..., :RG_WIDTH]
    xr = zr[..., RG_WIDTH:]
    xr = lax.conv_general_dilated(xr, conv_w[:, None, :], window_strides=(1,),
                                  padding=[(RG_CONV - 1, 0)],
                                  dimension_numbers=('NWC', 'WIO', 'NWC'),
                                  feature_group_count=RG_WIDTH) + conv_b
    xb = xr.reshape(B, S, RG_BLOCKS, RG_BLOCK_DIM)
    r = jax.nn.sigmoid((jnp.einsum('bsgi,gij->bsgj', xb, w_a).reshape(B, S, RG_WIDTH) + b_a).astype(jnp.float32))
    i = jax.nn.sigmoid((jnp.einsum('bsgi,gij->bsgj', xb, w_x).reshape(B, S, RG_WIDTH) + b_x).astype(jnp.float32))
    log_a = -RG_C * r * jax.nn.softplus(-lam.astype(jnp.float32))
    a = jnp.exp(log_a)
    u = jnp.sqrt(-jnp.expm1(2.0 * log_a)) * (i * xr.astype(jnp.float32))

    def combine(e1, e2):
        a1, b1 = e1
        a2, b2 = e2
        return a1 * a2, a2 * b1 + b2

    _, h = lax.associative_scan(combine, (a, u), axis=1)
    y = h * jax.nn.gelu(gate.astype(jnp.float32), approximate=False)
    return y.astype(zr.dtype)

def peer_ffn(x, w_q, subkeys, u_tab, v_tab):
    B, S, D = x.shape
    n = PEER_TOK_BLOCK
    xt = x.reshape((B * S) // n, n, D)
    sk = subkeys.astype(jnp.float32)

    def block(xb):
        q = (xb @ w_q).reshape(n, PEER_HEADS, 2, PEER_HALF).astype(jnp.float32)
        s = jnp.einsum('nhpc,pkc->nhpk', q, sk)
        sv, si = lax.top_k(s, PEER_TOPK)
        cand = sv[:, :, 0, :, None] + sv[:, :, 1, None, :]
        cand_id = si[:, :, 0, :, None] * PEER_KEYS + si[:, :, 1, None, :]
        fv, fi = lax.top_k(cand.reshape(n, PEER_HEADS, PEER_TOPK * PEER_TOPK), PEER_TOPK)
        eid = jnp.take_along_axis(cand_id.reshape(n, PEER_HEADS, PEER_TOPK * PEER_TOPK), fi, axis=-1)
        gw = jax.nn.softmax(fv, axis=-1)
        u = u_tab[eid]
        act = jax.nn.gelu(jnp.einsum('nhkd,nd->nhk', u, xb).astype(jnp.float32), approximate=False)
        coef = (gw * act).astype(x.dtype)
        return jnp.einsum('nhk,nhkd->nd', coef, v_tab[eid])

    y = lax.map(block, xt)
    return y.reshape(B, S, D)

def first_inputs(seed: int = 0) -> dict:
    key = jax.random.key(seed)
    ks = jax.random.split(key, 24)
    D = D_MODEL
    nrm = jax.random.normal
    x = nrm(ks[0], (BATCH, SEQ, D), jnp.float32)
    mem = nrm(ks[1], (BATCH, N_MEM, D), jnp.float32)
    mlstm_w_in = nrm(ks[2], (N_A, D, ML_IN), jnp.float32) * D ** -0.5
    f_bias = jnp.linspace(3.0, 6.0, ML_HEADS, dtype=jnp.float32)
    mlstm_b_gates = jnp.concatenate([
        0.1 * nrm(ks[3], (N_A, ML_HEADS), jnp.float32),
        f_bias[None, :] + 0.1 * nrm(ks[4], (N_A, ML_HEADS), jnp.float32)], axis=-1)
    mlstm_norm_g = 1.0 + 0.02 * nrm(ks[5], (N_A, ML_WIDTH), jnp.float32)
    rglru_w_in = nrm(ks[6], (N_B, D, RG_IN), jnp.float32) * D ** -0.5
    rglru_conv_w = nrm(ks[7], (N_B, RG_CONV, RG_WIDTH), jnp.float32) * RG_CONV ** -0.5
    rglru_conv_b = 0.01 * nrm(ks[8], (N_B, RG_WIDTH), jnp.float32)
    rglru_w_a = nrm(ks[9], (N_B, RG_BLOCKS, RG_BLOCK_DIM, RG_BLOCK_DIM), jnp.float32) * RG_BLOCK_DIM ** -0.5
    rglru_b_a = 0.01 * nrm(ks[10], (N_B, RG_WIDTH), jnp.float32)
    rglru_w_x = nrm(ks[11], (N_B, RG_BLOCKS, RG_BLOCK_DIM, RG_BLOCK_DIM), jnp.float32) * RG_BLOCK_DIM ** -0.5
    rglru_b_x = 0.01 * nrm(ks[12], (N_B, RG_WIDTH), jnp.float32)
    a0 = jax.random.uniform(ks[13], (N_B, RG_WIDTH), jnp.float32, 0.9, 0.999)
    p = a0 ** (1.0 / RG_C)
    rglru_lam = jnp.log(p) - jnp.log1p(-p)
    xattn_w_kv = nrm(ks[14], (DEPTH, D, 2 * XA_WIDTH), jnp.float32) * D ** -0.5
    w_out = nrm(ks[15], (DEPTH, D_MIX, D), jnp.float32) * (D_MIX ** -0.5) * DN_BETA
    ln1_g = 1.0 + 0.02 * nrm(ks[16], (DEPTH, D), jnp.float32)
    ln1_b = 0.01 * nrm(ks[17], (DEPTH, D), jnp.float32)
    peer_w_q = nrm(ks[18], (DEPTH, D, PEER_HEADS * PEER_QDIM), jnp.float32) * D ** -0.5
    peer_subkeys = nrm(ks[19], (DEPTH, 2, PEER_KEYS, PEER_HALF), jnp.float32) * PEER_HALF ** -0.5
    peer_u = nrm(ks[20], (DEPTH, PEER_EXPERTS, D), jnp.float32) * D ** -0.5
    peer_v = nrm(ks[21], (DEPTH, PEER_EXPERTS, D), jnp.float32) * (D ** -0.5) * DN_BETA
    ln2_g = 1.0 + 0.02 * nrm(ks[22], (DEPTH, D), jnp.float32)
    ln2_b = 0.01 * nrm(ks[23], (DEPTH, D), jnp.float32)
    return {"x": x, "mem": mem,
            "mlstm_w_in": mlstm_w_in, "mlstm_b_gates": mlstm_b_gates, "mlstm_norm_g": mlstm_norm_g,
            "rglru_w_in": rglru_w_in, "rglru_conv_w": rglru_conv_w, "rglru_conv_b": rglru_conv_b,
            "rglru_w_a": rglru_w_a, "rglru_b_a": rglru_b_a, "rglru_w_x": rglru_w_x, "rglru_b_x": rglru_b_x,
            "rglru_lam": rglru_lam, "xattn_w_kv": xattn_w_kv, "w_out": w_out,
            "ln1_g": ln1_g, "ln1_b": ln1_b, "peer_w_q": peer_w_q, "peer_subkeys": peer_subkeys,
            "peer_u": peer_u, "peer_v": peer_v, "ln2_g": ln2_g, "ln2_b": ln2_b}

def first_block(x, mem, mlstm_w_in, mlstm_b_gates, mlstm_norm_g, rglru_w_in, rglru_conv_w, rglru_conv_b,
              rglru_w_a, rglru_b_a, rglru_w_x, rglru_b_x, rglru_lam, xattn_w_kv, w_out,
              ln1_g, ln1_b, peer_w_q, peer_subkeys, peer_u, peer_v, ln2_g, ln2_b):
    for i in range(DEPTH):
        j = i // N_MIXERS
        if i % N_MIXERS == 0:
            z = x @ mlstm_w_in[j]
            hm = mlstm_mixer(z[..., :ML_IN - XA_WIDTH], mlstm_b_gates[j], mlstm_norm_g[j])
            xq = z[..., ML_IN - XA_WIDTH:]
        else:
            z = x @ rglru_w_in[j]
            hm = rglru_mixer(z[..., :RG_IN - XA_WIDTH], rglru_conv_w[j], rglru_conv_b[j],
                             rglru_w_a[j], rglru_b_a[j], rglru_w_x[j], rglru_b_x[j], rglru_lam[j])
            xq = z[..., RG_IN - XA_WIDTH:]
        ha = cross_attention(xq, mem, xattn_w_kv[i])
        mix = jnp.concatenate([hm, ha], axis=-1) @ w_out[i]
        x = layer_norm(DN_ALPHA * x + mix, ln1_g[i], ln1_b[i])
        y = peer_ffn(x, peer_w_q[i], peer_subkeys[i], peer_u[i], peer_v[i])
        x = layer_norm(DN_ALPHA * x + y, ln2_g[i], ln2_b[i])
    return x


N_MIXERS_2 = 4
D_FF = 2816
EPS = 1e-6
S5_GROUP = 16
S5_GROUPS = D_MODEL // S5_GROUP
S5_STATE = 64
DT_MIN = 1e-3
DT_MAX = 1e-1
CONV_W = 31
GM_CHUNK = 128
GM_E = 2 * D_MODEL
GM_HEADS = 8
HEAD_DIM = 64
AT_HEADS = D_MODEL // HEAD_DIM
PATTERNS = ((128, 1), (512, 4), (2048, 16))
N_PATTERNS = len(PATTERNS)
BLOCK = 128
NUM_BUCKETS = 32
MAX_DISTANCE = 2048


def rmsnorm(x, g):
    xf = x.astype(jnp.float32)
    y = xf * lax.rsqrt(jnp.mean(xf * xf, axis=-1, keepdims=True) + EPS)
    return (y * g.astype(jnp.float32)).astype(x.dtype)

def layernorm(x, g, b):
    xf = x.astype(jnp.float32)
    mu = jnp.mean(xf, axis=-1, keepdims=True)
    var = jnp.mean(jnp.square(xf - mu), axis=-1, keepdims=True)
    y = (xf - mu) * lax.rsqrt(var + EPS)
    return (y * g.astype(jnp.float32) + b.astype(jnp.float32)).astype(x.dtype)

def swiglu(h, w1, w3, w2):
    return (jax.nn.silu(h @ w1) * (h @ w3)) @ w2

def _complex_scan_op(left, right):
    a1r, a1i, b1r, b1i = left
    a2r, a2i, b2r, b2i = right
    return (a2r * a1r - a2i * a1i,
            a2r * a1i + a2i * a1r,
            a2r * b1r - a2i * b1i + b2r,
            a2r * b1i + a2i * b1r + b2i)

def s5_mixer(h, w_in, a_re, a_im, log_dt, b_re, b_im, c_re, c_im, d_skip, w_glu, b_glu, w_out):
    bsz, seq, _ = h.shape
    u = (h @ w_in).astype(jnp.float32).reshape(bsz, seq, S5_GROUPS, S5_GROUP)
    ar = a_re.astype(jnp.float32)
    ai = a_im.astype(jnp.float32)
    dt = jnp.exp(log_dt.astype(jnp.float32))[:, None]
    mag = jnp.exp(dt * ar)
    abar_re = mag * jnp.cos(dt * ai)
    abar_im = mag * jnp.sin(dt * ai)
    den = ar * ar + ai * ai
    nr = abar_re - 1.0
    f_re = (nr * ar + abar_im * ai) / den
    f_im = (abar_im * ar - nr * ai) / den
    br = b_re.astype(jnp.float32)
    bi = b_im.astype(jnp.float32)
    bb_re = f_re[..., None] * br - f_im[..., None] * bi
    bb_im = f_re[..., None] * bi + f_im[..., None] * br
    bu_re = jnp.einsum('blgh,gph->blgp', u, bb_re)
    bu_im = jnp.einsum('blgh,gph->blgp', u, bb_im)
    elems = (jnp.broadcast_to(abar_re, bu_re.shape), jnp.broadcast_to(abar_im, bu_re.shape), bu_re, bu_im)
    _, _, st_re, st_im = lax.associative_scan(_complex_scan_op, elems, axis=1)
    y = (jnp.einsum('blgp,ghp->blgh', st_re, c_re.astype(jnp.float32))
         - jnp.einsum('blgp,ghp->blgh', st_im, c_im.astype(jnp.float32))
         + d_skip.astype(jnp.float32).reshape(S5_GROUPS, S5_GROUP) * u)
    y = jax.nn.gelu(y.reshape(bsz, seq, D_MODEL)).astype(h.dtype)
    z = y * jax.nn.sigmoid(y @ w_glu + b_glu)
    return z @ w_out

def conv_mixer(h, w_in, b_in, dw, dw_b, ln_g, ln_b, w_out, b_out):
    z = h @ w_in + b_in
    a, g = jnp.split(z, 2, axis=-1)
    z = a * jax.nn.sigmoid(g)
    z = lax.conv_general_dilated(z, dw[:, None, :].astype(z.dtype), window_strides=(1,),
                                 padding=[(CONV_W - 1, 0)],
                                 dimension_numbers=('NWC', 'WIO', 'NWC'),
                                 feature_group_count=D_MODEL) + dw_b
    z = jax.nn.silu(layernorm(z, ln_g, ln_b))
    return z @ w_out + b_out

def gmlp_mixer(h, w_in, b_in, ln_g, ln_b, w_s, b_s, w_out, b_out):
    bsz, seq, _ = h.shape
    z = jax.nn.gelu(h @ w_in + b_in)
    u, v = jnp.split(z, 2, axis=-1)
    v = layernorm(v, ln_g, ln_b)
    vc = v.reshape(bsz, seq // GM_CHUNK, GM_CHUNK, GM_HEADS, GM_E // GM_HEADS)
    causal = jnp.tril(jnp.ones((GM_CHUNK, GM_CHUNK), jnp.float32))
    s = jnp.einsum('hts,bnshc->bnthc', w_s * causal, vc) + b_s.T[None, None, :, :, None]
    s = s.reshape(bsz, seq, GM_E).astype(u.dtype)
    return (u * s) @ w_out + b_out

def t5_bucket(dist):
    max_exact = NUM_BUCKETS // 2
    distf = jnp.maximum(dist, 1).astype(jnp.float32)
    large = max_exact + (jnp.log(distf / max_exact) / math.log(MAX_DISTANCE / max_exact)
                         * (NUM_BUCKETS - max_exact)).astype(jnp.int32)
    large = jnp.minimum(large, NUM_BUCKETS - 1)
    return jnp.where(dist < max_exact, dist, large)

def _band_delta():
    return (jnp.arange(BLOCK)[:, None] + BLOCK) - jnp.arange(2 * BLOCK)[None, :]

def rel_bias_block(table, dilation):
    dist = jnp.maximum(_band_delta(), 0) * dilation
    return table.astype(jnp.float32)[t5_bucket(dist)].transpose(2, 0, 1)

def dilated_window_attention(q, k, v, bias, window, dilation):
    bsz, seq, heads, hd = q.shape
    span = BLOCK * dilation
    seq_p = -(-seq // span) * span
    n_sub = seq_p // dilation
    n_blk = n_sub // BLOCK

    def to_blocks(t):
        t = jnp.pad(t.astype(jnp.float32), ((0, 0), (0, seq_p - seq), (0, 0), (0, 0)))
        t = t.reshape(bsz, n_sub, dilation, heads, hd).transpose(0, 2, 1, 3, 4)
        return t.reshape(bsz, dilation, n_blk, BLOCK, heads, hd)

    def with_prev(t):
        prev = jnp.pad(t, ((0, 0), (0, 0), (1, 0), (0, 0), (0, 0), (0, 0)))[:, :, :-1]
        return jnp.concatenate([prev, t], axis=3)

    qb = to_blocks(q)
    kk = with_prev(to_blocks(k))
    vv = with_prev(to_blocks(v))
    logits = jnp.einsum('brnqhd,brnkhd->brnhqk', qb, kk) * (hd ** -0.5) + bias[None, None, None]
    delta = _band_delta()
    in_band = (delta >= 0) & (delta <= window // dilation)
    not_before_start = (jnp.arange(n_blk)[:, None, None] > 0) | (jnp.arange(2 * BLOCK) >= BLOCK)[None, None, :]
    mask = in_band[None] & not_before_start
    logits = jnp.where(mask[None, None, :, None], logits, -jnp.inf)
    m = jnp.max(logits, axis=-1, keepdims=True)
    p = jnp.exp(logits - m)
    den = jnp.sum(p, axis=-1)
    o = jnp.einsum('brnhqk,brnkhd->brnqhd', p, vv) / jnp.swapaxes(den, -1, -2)[..., None]
    lse = jnp.swapaxes(m[..., 0] + jnp.log(den), -1, -2)
    o = o.reshape(bsz, dilation, n_sub, heads, hd).transpose(0, 2, 1, 3, 4).reshape(bsz, seq_p, heads, hd)[:, :seq]
    lse = lse.reshape(bsz, dilation, n_sub, heads).transpose(0, 2, 1, 3).reshape(bsz, seq_p, heads)[:, :seq]
    return o, lse

def attention_mixer(h, w_qkv, w_out, rel_bias):
    bsz, seq, _ = h.shape
    qkv = (h @ w_qkv).reshape(bsz, seq, N_PATTERNS, 3, AT_HEADS, HEAD_DIM)
    outs, lses = [], []
    for g, (window, dilation) in enumerate(PATTERNS):
        bias = rel_bias_block(rel_bias[:, g * AT_HEADS:(g + 1) * AT_HEADS], dilation)
        o, lse = dilated_window_attention(qkv[:, :, g, 0], qkv[:, :, g, 1], qkv[:, :, g, 2], bias, window, dilation)
        outs.append(o)
        lses.append(lse)
    wts = jax.nn.softmax(jnp.stack(lses, axis=0), axis=0)
    o = jnp.sum(wts[..., None] * jnp.stack(outs, axis=0), axis=0)
    return o.reshape(bsz, seq, AT_HEADS * HEAD_DIM).astype(h.dtype) @ w_out

def _count(kind):
    return len(range(kind, DEPTH, N_MIXERS_2))

def second_inputs(seed: int = 0) -> dict:
    key = jax.random.key(seed)
    ks = iter(jax.random.split(key, 48))

    def nrm(shape, scale):
        return scale * jax.random.normal(next(ks), shape, jnp.float32)

    na, nb, nc, nd = _count(0), _count(1), _count(2), _count(3)
    D, F, G, P, HG, E = D_MODEL, D_FF, S5_GROUPS, S5_STATE, S5_GROUP, GM_E
    return {
        "x": nrm((BATCH, SEQ, D), 1.0),
        "norm_pre": 1.0 + nrm((DEPTH, 3, D), 0.05),
        "norm_post": 1.0 + nrm((DEPTH, 3, D), 0.05),
        "ffn_w1": nrm((DEPTH, 2, D, F), D ** -0.5),
        "ffn_w3": nrm((DEPTH, 2, D, F), D ** -0.5),
        "ffn_w2": nrm((DEPTH, 2, F, D), F ** -0.5),
        "rel_bias": nrm((NUM_BUCKETS, N_PATTERNS * AT_HEADS), 0.5),
        "s5_w_in": nrm((na, D, D), D ** -0.5),
        "s5_a_re": -0.5 + nrm((na, G, P), 0.01),
        "s5_a_im": jnp.pi * jnp.arange(P, dtype=jnp.float32) + nrm((na, G, P), 0.01),
        "s5_log_dt": jax.random.uniform(next(ks), (na, G), jnp.float32, math.log(DT_MIN), math.log(DT_MAX)),
        "s5_b_re": nrm((na, G, P, HG), (2 * HG) ** -0.5),
        "s5_b_im": nrm((na, G, P, HG), (2 * HG) ** -0.5),
        "s5_c_re": nrm((na, G, HG, P), (2 * P) ** -0.5),
        "s5_c_im": nrm((na, G, HG, P), (2 * P) ** -0.5),
        "s5_d": nrm((na, D), 1.0),
        "s5_w_glu": nrm((na, D, D), D ** -0.5),
        "s5_b_glu": nrm((na, D), 0.01),
        "s5_w_out": nrm((na, D, D), D ** -0.5),
        "cv_w_in": nrm((nb, D, 2 * D), D ** -0.5),
        "cv_b_in": nrm((nb, 2 * D), 0.01),
        "cv_dw": nrm((nb, CONV_W, D), CONV_W ** -0.5),
        "cv_dw_b": nrm((nb, D), 0.01),
        "cv_ln_g": 1.0 + nrm((nb, D), 0.05),
        "cv_ln_b": nrm((nb, D), 0.01),
        "cv_w_out": nrm((nb, D, D), D ** -0.5),
        "cv_b_out": nrm((nb, D), 0.01),
        "gm_w_in": nrm((nc, D, 2 * E), D ** -0.5),
        "gm_b_in": nrm((nc, 2 * E), 0.01),
        "gm_ln_g": 1.0 + nrm((nc, E), 0.05),
        "gm_ln_b": nrm((nc, E), 0.01),
        "gm_w_s": nrm((nc, GM_HEADS, GM_CHUNK, GM_CHUNK), GM_CHUNK ** -0.5),
        "gm_b_s": 1.0 + nrm((nc, GM_HEADS, GM_CHUNK), 0.01),
        "gm_w_out": nrm((nc, E, D), E ** -0.5),
        "gm_b_out": nrm((nc, D), 0.01),
        "at_w_qkv": nrm((nd, D, N_PATTERNS * 3 * AT_HEADS * HEAD_DIM), D ** -0.5),
        "at_w_out": nrm((nd, AT_HEADS * HEAD_DIM, D), (AT_HEADS * HEAD_DIM) ** -0.5),
    }

def second_block(x, norm_pre, norm_post, ffn_w1, ffn_w3, ffn_w2, rel_bias,
              s5_w_in, s5_a_re, s5_a_im, s5_log_dt, s5_b_re, s5_b_im, s5_c_re, s5_c_im,
              s5_d, s5_w_glu, s5_b_glu, s5_w_out,
              cv_w_in, cv_b_in, cv_dw, cv_dw_b, cv_ln_g, cv_ln_b, cv_w_out, cv_b_out,
              gm_w_in, gm_b_in, gm_ln_g, gm_ln_b, gm_w_s, gm_b_s, gm_w_out, gm_b_out,
              at_w_qkv, at_w_out):
    for i in range(DEPTH):
        kind, j = i % N_MIXERS_2, i // N_MIXERS_2
        h = swiglu(rmsnorm(x, norm_pre[i, 0]), ffn_w1[i, 0], ffn_w3[i, 0], ffn_w2[i, 0])
        x = x + 0.5 * rmsnorm(h, norm_post[i, 0])
        h = rmsnorm(x, norm_pre[i, 1])
        if kind == 0:
            h = s5_mixer(h, s5_w_in[j], s5_a_re[j], s5_a_im[j], s5_log_dt[j], s5_b_re[j], s5_b_im[j],
                         s5_c_re[j], s5_c_im[j], s5_d[j], s5_w_glu[j], s5_b_glu[j], s5_w_out[j])
        elif kind == 1:
            h = conv_mixer(h, cv_w_in[j], cv_b_in[j], cv_dw[j], cv_dw_b[j], cv_ln_g[j], cv_ln_b[j],
                           cv_w_out[j], cv_b_out[j])
        elif kind == 2:
            h = gmlp_mixer(h, gm_w_in[j], gm_b_in[j], gm_ln_g[j], gm_ln_b[j], gm_w_s[j], gm_b_s[j],
                           gm_w_out[j], gm_b_out[j])
        else:
            h = attention_mixer(h, at_w_qkv[j], at_w_out[j], rel_bias)
        x = x + rmsnorm(h, norm_post[i, 1])
        h = swiglu(rmsnorm(x, norm_pre[i, 2]), ffn_w1[i, 1], ffn_w3[i, 1], ffn_w2[i, 1])
        x = x + 0.5 * rmsnorm(h, norm_post[i, 2])
    return x


def setup_inputs(seed=0):
    out = dict(first_inputs(seed))
    for name, value in second_inputs(seed + 1).items():
        if name != "x":
            out[name + "_2"] = value
    return out


def reference(
    x, mem, mlstm_w_in, mlstm_b_gates, mlstm_norm_g, rglru_w_in, rglru_conv_w, rglru_conv_b,
    rglru_w_a, rglru_b_a, rglru_w_x, rglru_b_x, rglru_lam, xattn_w_kv, w_out, ln1_g, ln1_b,
    peer_w_q, peer_subkeys, peer_u, peer_v, ln2_g, ln2_b, norm_pre_2, norm_post_2, ffn_w1_2,
    ffn_w3_2, ffn_w2_2, rel_bias_2, s5_w_in_2, s5_a_re_2, s5_a_im_2, s5_log_dt_2, s5_b_re_2,
    s5_b_im_2, s5_c_re_2, s5_c_im_2, s5_d_2, s5_w_glu_2, s5_b_glu_2, s5_w_out_2, cv_w_in_2,
    cv_b_in_2, cv_dw_2, cv_dw_b_2, cv_ln_g_2, cv_ln_b_2, cv_w_out_2, cv_b_out_2, gm_w_in_2,
    gm_b_in_2, gm_ln_g_2, gm_ln_b_2, gm_w_s_2, gm_b_s_2, gm_w_out_2, gm_b_out_2, at_w_qkv_2,
    at_w_out_2,
):
    x = first_block(
        x, mem, mlstm_w_in, mlstm_b_gates, mlstm_norm_g, rglru_w_in, rglru_conv_w, rglru_conv_b,
        rglru_w_a, rglru_b_a, rglru_w_x, rglru_b_x, rglru_lam, xattn_w_kv, w_out, ln1_g, ln1_b,
        peer_w_q, peer_subkeys, peer_u, peer_v, ln2_g, ln2_b,
    )
    return second_block(
        x, norm_pre_2, norm_post_2, ffn_w1_2, ffn_w3_2, ffn_w2_2, rel_bias_2, s5_w_in_2,
        s5_a_re_2, s5_a_im_2, s5_log_dt_2, s5_b_re_2, s5_b_im_2, s5_c_re_2, s5_c_im_2, s5_d_2,
        s5_w_glu_2, s5_b_glu_2, s5_w_out_2, cv_w_in_2, cv_b_in_2, cv_dw_2, cv_dw_b_2, cv_ln_g_2,
        cv_ln_b_2, cv_w_out_2, cv_b_out_2, gm_w_in_2, gm_b_in_2, gm_ln_g_2, gm_ln_b_2, gm_w_s_2,
        gm_b_s_2, gm_w_out_2, gm_b_out_2, at_w_qkv_2, at_w_out_2,
    )


_drawn_inputs = setup_inputs


def setup_inputs(seed=0):
    import zlib

    import numpy as np

    out = dict(_drawn_inputs(seed))
    spreads = {}
    factors = {'mlstm_norm_g': 8.0,
     'rglru_conv_b': 5.814,
     'rglru_b_a': 43.955,
     'rglru_b_x': 24.697,
     'peer_w_q': 5.595,
     'peer_subkeys': 5.583,
     'peer_u': 6.181,
     'peer_v': 5.592,
     's5_a_re_2': 200.0,
     's5_b_glu_2': 8.0,
     'cv_b_in_2': 8.0,
     'cv_dw_b_2': 5.117,
     'cv_ln_b_2': 8.0,
     'cv_b_out_2': 6.207,
     's5_a_im_2': 26.712,
     's5_log_dt_2': 28.576,
     's5_b_re_2': 37.168,
     's5_b_im_2': 36.848,
     's5_c_re_2': 37.264,
     's5_c_im_2': 37.32}
    for name, (base, spread) in spreads.items():
        noise = np.random.default_rng([zlib.crc32(name.encode()), seed]).standard_normal(out[name].shape)
        drawn = base * np.exp(spread * noise) if base else spread * noise
        out[name] = __import__('jax').numpy.asarray(drawn.astype(out[name].dtype))
    for name, factor in factors.items():
        out[name] = (out[name] * factor).astype(out[name].dtype)
    return out
```

```python
from contextlib import ExitStack

import numpy as np

import concourse.bass as bass
from concourse import mybir

ACT = mybir.ActivationFunctionType
ALU = mybir.AluOpType
AX = mybir.AxisListType.X
F32 = mybir.dt.float32
U32 = mybir.dt.uint32

P = 128
S = 256
TT = S // P
D = 1024
KD = D // P
DEPTH = 2
ALPHA = (2 * DEPTH) ** 0.25
LN_EPS = 1e-5
RMS_EPS = 1e-6
ML_HEADS, ML_DH = 4, 192
ML_W = ML_HEADS * ML_DH
ML_K = ML_W // P
RG_B, RG_D = 8, 96
RG_CONV = 4
RG_C = 8.0
XA_HEADS, XA_DH = 4, 64
XA_W = XA_HEADS * XA_DH
PR_HEADS, PR_K = 8, 16
PR_KEYS = 128
FF = 2816
FF_T = FF // P
S5_J = 32
CV_TAPS = 31
NEG = -3.0e38
ROUND = 12582912.0

RING, SLOT = 6, 2112
BANKS = 4
U_SLOTS = V_SLOTS = 8
ARENA = 26000


class Steps:

    def __init__(self, who, found):
        self.who, self.found, self.n = who, found, 0

    def step(self, label=None):
        self.n += 1
        if label is not None:
            self.found[label] = (self.who, self.n)
        return 1


def weight_plan(A):
    plan = []

    def columns(name, w, c0, n, p=P):
        plan.append((name, w.rearrange("(k p) n -> p k n", p=p)[:, :, c0:c0 + n], p, w.shape[0] // p, n))

    def rows(name, w, r0, k, p=P):
        plan.append((name, w[r0:r0 + k * p, :].rearrange("(k p) n -> p k n", p=p), p, k, w.shape[1]))

    def mix_out(i, p_main, k_main):
        w = A["w_out"][i]
        for c in range(k_main // 2):
            rows(f"wout{i}.{c}", w, 2 * c * p_main, 2, p_main)
        rows(f"wout{i}.x", w, k_main * p_main, 2)

    def peer(i):
        for c in range(8):
            columns(f"wq{i}.{c}", A["peer_w_q"][i], 256 * c, 256)

    def ffn(l, s):
        for c in range(FF_T // 2):
            columns(f"w1.{l}{s}.{c}", A["ffn_w1_2"][l, s // 2], 256 * c, 256)
            columns(f"w3.{l}{s}.{c}", A["ffn_w3_2"][l, s // 2], 256 * c, 256)
        for c in range(FF_T // 2):
            rows(f"w2.{l}{s}.{c}", A["ffn_w2_2"][l, s // 2], 256 * c, 2)

    for i in range(DEPTH):
        for c in range(2):
            columns(f"wkv{i}.{c}", A["xattn_w_kv"][i], 256 * c, 256)
    w = A["mlstm_w_in"][0]
    columns("m.gx", w, 4 * ML_W, 2 * ML_HEADS + XA_W)
    for c in range(12):
        columns(f"m.{c}", w, 256 * c, 256)
    mix_out(0, P, ML_K)
    peer(0)
    w = A["rglru_w_in"][0]
    for c in range(4):
        columns(f"r.x{c}", w, RG_B * RG_D + 192 * c, 192)
    plan.append(("r.a", A["rglru_w_a"][0].rearrange("g i j -> i g j"), RG_D, RG_B, RG_D))
    plan.append(("r.i", A["rglru_w_x"][0].rearrange("g i j -> i g j"), RG_D, RG_B, RG_D))
    columns("r.q", w, 2 * RG_B * RG_D, 256)
    for c in range(4):
        columns(f"r.g{c}", w, 192 * c, 192)
    mix_out(1, RG_D, RG_B)
    peer(1)
    for l in range(DEPTH):
        ffn(l, 0)
        if l == 0:
            for c in range(4):
                columns(f"s.in{c}", A["s5_w_in_2"][0], 256 * c, 256)
            for c in range(4):
                columns(f"s.glu{c}", A["s5_w_glu_2"][0], 256 * c, 256)
            for c in range(4):
                rows(f"s.out{c}", A["s5_w_out_2"][0], 256 * c, 2)
        else:
            for c in range(4):
                columns(f"c.a{c}", A["cv_w_in_2"][0], 256 * c, 256)
                columns(f"c.g{c}", A["cv_w_in_2"][0], D + 256 * c, 256)
            for c in range(4):
                rows(f"c.out{c}", A["cv_w_out_2"][0], 256 * c, 2)
        ffn(l, 2)
    return plan


def row_plan(A):
    g = [("mnorm", A["mlstm_norm_g"][0])]
    for i in range(DEPTH):
        g += [(f"ln1g{i}", A["ln1_g"][i]), (f"ln1b{i}", A["ln1_b"][i]), (f"ln2g{i}", A["ln2_g"][i]), (f"ln2b{i}", A["ln2_b"][i])]
    for l in range(DEPTH):
        g += [(f"post{l}0", A["norm_post_2"][l, 0])]
        if l == 1:
            g += [("cvbout", A["cv_b_out_2"][0])]
        g += [(f"post{l}1", A["norm_post_2"][l, 1]), (f"post{l}2", A["norm_post_2"][l, 2])]
    return g


ROWS = 4

COL_PRE, COL_D, COL_GLU, COL_BIN, COL_DWB, COL_LNG, COL_LNB = 0, 48, 56, 64, 80, 88, 96
COL_ROWS = 104
RG_CB, RG_BA, RG_BX, RG_LAM = 32, 40, 48, 56


def build(nc, A, out, known):
    found = {}
    chunks = weight_plan(A)
    chunk_at = {c[0]: i for i, c in enumerate(chunks)}
    rows_at = {r[0]: i for i, r in enumerate(row_plan(A))}
    ctx = ExitStack()
    with ctx:
        def sb(name, shape, dt=F32):
            return ctx.enter_context(nc.sbuf_tensor(name, shape, dt))

        names = (["pe_steps", "act_steps", "dve_steps", "pool_steps", "params", "tokens", "memory", "stored"]
                 + [f"weights{i}" for i in range(RING)] + [f"rows{i}" for i in range(ROWS)]
                 + [f"u_rows{i}" for i in range(U_SLOTS)] + [f"v_rows{i}" for i in range(V_SLOTS)]
                 + ["s5_b", "s5_c"])
        sems = {n: ctx.enter_context(nc.semaphore(n)) for n in names}
        pe_steps, act_steps, dve_steps, pool_steps, params, tokens, memory, stored, s5_b, s5_c = (
            sems[n] for n in ("pe_steps", "act_steps", "dve_steps", "pool_steps", "params", "tokens", "memory", "stored", "s5_b", "s5_c"))

        def by(label):
            who, n = known[label] if known is not None else ("pe_steps", 1)
            return sems[who], n

        def count_of(label):
            return by(label)[1]

        def landed(name, label):
            n = found.get(("count", name), 0) + 16
            found[("count", name)] = n
            found[label] = (name, n)
            return 16

        ring = sb("ring", [P, RING, SLOT])
        x_tok = sb("x_tok", [P, TT, D])
        x_fm = sb("x_fm", [P, KD, S])
        mix_fm = sb("mix_fm", [P, RG_B + 2, S])
        rowb = sb("rowb", [P, ROWS, D])
        k_mem = sb("k_mem", [P, DEPTH, 2, S])
        v_mem = sb("v_mem", [P, DEPTH, TT, XA_W])
        ident = sb("ident", [P, P])
        col = sb("col", [P, COL_ROWS])
        col_dw = sb("col_dw", [P, 2, 124])
        col_rg = sb("col_rg", [RG_D, 64])
        col_s5 = sb("col_s5", [P, 96])
        skT = sb("skT", [P, 2 * DEPTH, PR_KEYS])
        mask32 = sb("mask32", [P, 32])
        iota16 = sb("iota16", [P, PR_K])
        stat = sb("stat", [P, 64])
        arena = sb("arena", [P, ARENA])
        ps = ctx.enter_context(nc.psum_tensor("ps", [P, BANKS, 512], F32))
        acc = ctx.enter_context(nc.psum_tensor("acc", [P, 2 * TT, 512], F32))

        def area(at, *shape):
            n = int(np.prod(shape))
            assert at + n <= ARENA, (at, shape)
            v = arena[:, at:at + n]
            if len(shape) == 2:
                v = v.rearrange("p (a b) -> p a b", b=shape[1])
            elif len(shape) == 3:
                v = v.rearrange("p (a b c) -> p a b c", b=shape[1], c=shape[2])
            elif len(shape) == 4:
                v = v.rearrange("p (a b c d) -> p a b c d", b=shape[1], c=shape[2], d=shape[3])
            return v

        def x_tile(t, k):
            return x_tok[:, t, 128 * k:128 * k + 128]

        block = ctx.enter_context(nc.Block())
        TE = Steps("pe_steps", found)
        AC = Steps("act_steps", found)
        VE = Steps("dve_steps", found)
        PO = Steps("pool_steps", found)
        act, dve, pool, pe = nc.scalar, nc.vector, nc.gpsimd, nc.tensor
        engine_of = {"pe_steps": pe, "act_steps": act, "dve_steps": dve, "pool_steps": pool}

        tiles, tile_bank = [], {}

        def open_tile(name):
            i = len(tiles)
            if i >= BANKS:
                pe.wait_ge(*by("read " + tiles[i - BANKS]))
            tiles.append(name)
            tile_bank[name] = i % BANKS
            return ps[:, i % BANKS, :]

        def tile_of(e, name):
            engine_of[e.who].wait_ge(pe_steps, count_of("tile " + name))
            return ps[:, tile_bank[name], :]

        def chunk(name, e=None):
            i = chunk_at[name]
            _, _, p, k, n = chunks[i]
            if e is not None:
                engine_of[e.who].wait_ge(sems[f"weights{i % RING}"], 16 * (i // RING + 1))
            return ring[0:p, i % RING, 0:k * n].rearrange("p (k n) -> p k n", k=k)

        def mm(o, l, r, first, last):
            return pe.matmul(o, l, r, start=first, stop=last)

        def row(name, e):
            i = rows_at[name]
            engine_of[e.who].wait_ge(sems[f"rows{i % ROWS}"], 16 * (i // ROWS + 1))
            return rowb[:, i % ROWS, :]

        def pe_transposes(name, src, n_tiles=KD):
            for c in range(n_tiles // 2):
                o = open_tile(f"{name}.{c}")
                for k in range(2):
                    for t in range(TT):
                        i = pe.transpose(o[:, 256 * k + 128 * t:256 * k + 128 * t + 128],
                                         src(t, 2 * c + k), ident[:, :])
                i.then_inc(pe_steps, TE.step(f"tile {name}.{c}"))
            TE.found[f"{name} transposed"] = (TE.who, TE.n)

        def pe_columns(name, w, rhs, m=P, k_tiles=KD):
            o = open_tile(name)
            for half in range(2):
                for k in range(k_tiles):
                    i = mm(o[0:m, 256 * half:256 * half + 256], w[:, k, half * m:half * m + m], rhs[:, k, :],
                           k == 0, k == k_tiles - 1)
            i.then_inc(pe_steps, TE.step(f"tile {name}"))

        def pe_token_rows(name, w, lhs, n=256):
            o = open_tile(name)
            for t in range(TT):
                for k in range(KD):
                    i = mm(o[:, n * t:n * t + n], lhs[:, k, 128 * t:128 * t + 128], w[:, k, 0:n], k == 0, k == KD - 1)
            i.then_inc(pe_steps, TE.step(f"tile {name}"))

        def release(name):
            found[f"used {name}"] = (TE.who, TE.n)

        def pe_into_acc(name, names, lhs):
            n_all = sum(chunks[chunk_at[c]][3] for c in names)
            at = 0
            for c in names:
                w = chunk(c, TE)
                for k in range(w.shape[1]):
                    for t in range(TT):
                        for half in range(2):
                            left = lhs(at)
                            i = mm(acc[:, 2 * t + half, :], left[:, 128 * t:128 * t + 128],
                                   w[:, k, 512 * half:512 * half + 512], at == 0, at == n_all - 1)
                    at += 1
                i.then_inc(pe_steps, TE.step())
                release(c)
            found[f"acc {name}"] = (TE.who, TE.n)

        def pe_attention(i, q, p_of, pT_of, m0):
            pe.wait_ge(act_steps, count_of(f"xq{i} ready"))
            pe.wait_ge(act_steps, count_of(f"kv{i} ready"))
            for h in range(XA_HEADS):
                o = open_tile(f"xs{i}.{h}")
                r = slice(64 * (h % 2), 64 * (h % 2) + 64)
                for t in range(TT):
                    ins = mm(o[:, 256 * t:256 * t + 256], q[r, h // 2, 128 * t:128 * t + 128], k_mem[r, i, h // 2, :], True, True)
                ins.then_inc(pe_steps, TE.step(f"tile xs{i}.{h}"))
            for h in range(XA_HEADS):
                pe.wait_ge(dve_steps, count_of(f"xp{i}.{h}"))
                o = open_tile(f"xpT{i}.{h}")
                for m in range(2):
                    for t in range(TT):
                        ins = pe.transpose(o[:, 256 * m + 128 * t:256 * m + 128 * t + 128],
                                           p_of(h)[:, t, 128 * m:128 * m + 128], ident[:, :])
                ins.then_inc(pe_steps, TE.step(f"tile xpT{i}.{h}"))
            for pair in range(2):
                for h in (2 * pair, 2 * pair + 1):
                    pe.wait_ge(act_steps, count_of(f"xpT{i}.{h} ready"))
                o = open_tile(f"xo{i}.{pair}")
                for h in (2 * pair, 2 * pair + 1):
                    for m in range(2):
                        ins = mm(o[64 * (h % 2):64 * (h % 2) + 64, 0:256], v_mem[:, i, m, 64 * h:64 * h + 64],
                                 pT_of(h)[:, m, :], m == 0, m == 1)
                ins.then_inc(pe_steps, TE.step(f"tile xo{i}.{pair}"))

        def attention_softmax(i, p_of, pT_of, m0):
            for h in range(XA_HEADS):
                o = tile_of(VE, f"xs{i}.{h}").rearrange("p (t m) -> p t m", t=TT)
                mx = stat[:, 2 * h:2 * h + 2]
                dve.tensor_reduce(mx, o, AX, ALU.max).then_inc(dve_steps, VE.step())
                dve.wait_ge(dve_steps, VE.n)
                dve.tensor_scalar(mx, mx, -XA_DH ** -0.5, None, ALU.mult).then_inc(dve_steps, VE.step(f"xmax{i}.{h}"))
                dve.wait_ge(dve_steps, VE.n)
            for h in range(XA_HEADS):
                dve.wait_ge(act_steps, count_of(f"xexp{i}.{h}"))
                rs = stat[:, 8 + 2 * h:10 + 2 * h]
                dve.reciprocal(rs, rs).then_inc(dve_steps, VE.step())
                dve.wait_ge(dve_steps, VE.n)
                for t in range(TT):
                    dve.tensor_scalar(p_of(h)[:, t, :], p_of(h)[:, t, :], rs[:, t:t + 1], None, ALU.mult).then_inc(dve_steps, VE.step(f"xp{i}.{h}"))

        def act_attention(i, p_of, pT_of, m0):
            for h in range(XA_HEADS):
                act.wait_ge(dve_steps, count_of(f"xmax{i}.{h}"))
                o = tile_of(AC, f"xs{i}.{h}")
                for t in range(TT):
                    act.activation(p_of(h)[:, t, :], o[:, 256 * t:256 * t + 256], ACT.Exp,
                                           bias=stat[:, 2 * h + t:2 * h + t + 1], scale=XA_DH ** -0.5,
                                           accum_out=stat[:, 8 + 2 * h + t:9 + 2 * h + t]).then_inc(act_steps, AC.step(f"xexp{i}.{h}"))
                found[f"read xs{i}.{h}"] = (AC.who, AC.n)
            for h in range(XA_HEADS):
                o = tile_of(AC, f"xpT{i}.{h}")
                act.copy(pT_of(h).rearrange("p a b -> p (a b)"), o).then_inc(act_steps, AC.step(f"xpT{i}.{h} ready"))
                found[f"read xpT{i}.{h}"] = (AC.who, AC.n)
            for pair in range(2):
                o = tile_of(AC, f"xo{i}.{pair}")
                act.copy(mix_fm[:, m0 + pair, :], o[:, 0:256]).then_inc(act_steps, AC.step(f"read xo{i}.{pair}"))
            found[f"xa{i} ready"] = (AC.who, AC.n)

        def dve_layer_norm(i, which, g, b):
            dve.wait_ge(pe_steps, count_of(f"acc {which}{i}"))
            for t in range(TT):
                dve.scalar_tensor_tensor(x_tok[:, t, :], x_tok[:, t, :], ALPHA,
                                                 acc[:, 2 * t:2 * t + 2, :].rearrange("p a b -> p (a b)"), ALU.mult, ALU.add).then_inc(dve_steps, VE.step())
            dve.wait_ge(dve_steps, VE.n)
            found[f"acc {which}{i} read"] = (VE.who, VE.n)
            bn, ag, rstd = stat[:, 0:24].rearrange("p (t a b) -> p t a b", t=2, a=2), stat[:, 24:28].rearrange("p (t b) -> p t b", t=2), stat[:, 28:30]
            for t in range(TT):
                for h in range(2):
                    dve.bn_stats(bn[:, t, h, :], x_tok[:, t, 512 * h:512 * h + 512]).then_inc(dve_steps, VE.step())
            dve.wait_ge(dve_steps, VE.n)
            for t in range(TT):
                dve.bn_aggr(ag[:, t, :], bn[:, t, :, :].rearrange("p a b -> p (a b)")).then_inc(dve_steps, VE.step())
            dve.wait_ge(dve_steps, VE.n)
            dve.tensor_scalar(rstd, ag[:, :, 1], LN_EPS, None, ALU.add).then_inc(dve_steps, VE.step(f"var {which}{i}"))
            dve.wait_ge(dve_steps, VE.n)
            dve.wait_ge(act_steps, count_of(f"std {which}{i}"))
            dve.reciprocal(rstd, rstd).then_inc(dve_steps, VE.step())
            dve.wait_ge(dve_steps, VE.n)
            for t in range(TT):
                dve.tensor_scalar(x_tok[:, t, :], x_tok[:, t, :], ag[:, t, 0:1], rstd[:, t:t + 1], ALU.subtract, ALU.mult).then_inc(dve_steps, VE.step())
            dve.wait_ge(dve_steps, VE.n)
            gr, br = row(g, VE), row(b, VE)
            for t in range(TT):
                dve.tensor_tensor(x_tok[:, t, :], x_tok[:, t, :], gr, ALU.mult).then_inc(dve_steps, VE.step())
            dve.wait_ge(dve_steps, VE.n)
            found[f"row {g}"] = (VE.who, VE.n)
            for t in range(TT):
                dve.tensor_tensor(x_tok[:, t, :], x_tok[:, t, :], br, ALU.add).then_inc(dve_steps, VE.step(f"x {which}{i}.{t}"))
            dve.wait_ge(dve_steps, VE.n)
            found[f"row {b}"] = (VE.who, VE.n)
            found[f"x {which}{i}"] = (VE.who, VE.n)
            if which == "peer" and i == DEPTH - 1:
                found["x ffn00"] = (VE.who, VE.n)

        def act_sqrt(name, v):
            act.wait_ge(dve_steps, count_of(f"var {name}"))
            act.sqrt(v, v).then_inc(act_steps, AC.step(f"std {name}"))

        def x_transposed(name, e, out_of, scale=None, func=None):
            for c in range(KD // 2):
                who = (AC, VE)[c % 2]
                if who is not e:
                    continue
                o = tile_of(e, f"{name}.{c}")
                if scale is None:
                    dst = out_of[:, 2 * c:2 * c + 2, :].rearrange("p a b -> p (a b)")
                    ins = act.copy(dst, o) if e is AC else dve.tensor_copy(dst, o)
                    ins.then_inc(sems[e.who], e.step(f"read {name}.{c}"))
                else:
                    for k in range(2):
                        dst, sc = out_of[:, 2 * c + k, :], scale[:, 2 * c + k:2 * c + k + 1]
                        if e is AC:
                            ins = act.activation(dst, o[:, 256 * k:256 * k + 256], ACT.Copy, scale=sc)
                        else:
                            ins = dve.tensor_scalar(dst, o[:, 256 * k:256 * k + 256], sc, None, ALU.mult)
                        ins.then_inc(sems[e.who], e.step(f"read {name}.{c}"))

        def wait_transposed(e, name):
            for c in range(KD // 2):
                engine_of[e.who].wait_ge(*by(f"read {name}.{c}"))

        st_a, st_b, st_r, st_s = area(0, 128), area(128, 2, 128), area(384, 96), area(480, 128)
        st_k = area(608, 2 * DEPTH, P)
        st_dt = area(1120, 2)
        mem_tok, mem_fm = area(2048, TT, D), area(4096, KD, S)

        def sp_inputs():
            nc.sync.dma_start(x_tok[:, :, :], A["x"][0].rearrange("(t p) d -> p t d", p=P)).then_inc(tokens, landed("tokens", "x loaded"))
            nc.sync.dma_start(mem_tok, A["mem"][0].rearrange("(t p) d -> p t d", p=P)).then_inc(memory, landed("memory", "mem loaded"))

        def sp_weights():
            for i, (name, src, p, k, n) in enumerate(chunks):
                if i >= RING:
                    nc.sync.wait_ge(pe_steps, count_of("used " + chunks[i - RING][0]))
                nc.sync.dma_start(ring[0:p, i % RING, 0:k * n].rearrange("p (k n) -> p k n", k=k), src).then_inc(sems[f"weights{i % RING}"], landed(f"weights{i % RING}", f"chunk {name}"))

        def act_param_loads():
            def two(ap):
                return ap.rearrange("a (k p) -> (a k) p", p=P)

            def vec(ap, p=P):
                return ap.rearrange("(k p) -> k p", p=p)

            loads = [
                (st_a[COL_PRE:COL_PRE + 48, :], A["norm_pre_2"].rearrange("l i (k p) -> (l i k) p", p=P)),
                (st_a[COL_D:COL_D + 8, :], vec(A["s5_d_2"][0])),
                (st_a[COL_GLU:COL_GLU + 8, :], vec(A["s5_b_glu_2"][0])),
                (st_a[COL_BIN:COL_BIN + 16, :], vec(A["cv_b_in_2"][0])),
                (st_a[COL_DWB:COL_DWB + 8, :], vec(A["cv_dw_b_2"][0])),
                (st_a[COL_LNG:COL_LNG + 8, :], vec(A["cv_ln_g_2"][0])),
                (st_a[COL_LNB:COL_LNB + 8, :], vec(A["cv_ln_b_2"][0])),
                (st_b[0:124, 0, :], two(A["cv_dw_2"][0])[0:124, :]),
                (st_b[0:124, 1, :], two(A["cv_dw_2"][0])[124:248, :]),
                (st_r[0:32, :], A["rglru_conv_w"][0].rearrange("a (k p) -> (a k) p", p=RG_D)),
                (st_r[RG_CB:RG_CB + 8, :], vec(A["rglru_conv_b"][0], RG_D)),
                (st_r[RG_BA:RG_BA + 8, :], vec(A["rglru_b_a"][0], RG_D)),
                (st_r[RG_BX:RG_BX + 8, :], vec(A["rglru_b_x"][0], RG_D)),
                (st_r[RG_LAM:RG_LAM + 8, :], vec(A["rglru_lam"][0], RG_D)),
                (st_s[0:32, :], A["s5_a_re_2"][0].rearrange("(j two) p -> j (two p)", two=2)),
                (st_s[32:64, :], A["s5_a_im_2"][0].rearrange("(j two) p -> j (two p)", two=2)),
                (st_dt[64:96, :], A["s5_log_dt_2"][0].rearrange("(j two) -> j two", two=2)),
                (st_k, A["peer_subkeys"].rearrange("l h k c -> k (l h) c")),
                (gate_b[0:ML_HEADS, 0:1], A["mlstm_b_gates"][0, 0:ML_HEADS].rearrange("(h a) -> h a", a=1)),
                (gate_b[0:ML_HEADS, 1:2], A["mlstm_b_gates"][0, ML_HEADS:].rearrange("(h a) -> h a", a=1)),
            ]
            for dst, src in loads:
                act.dma_start(dst, src).then_inc(params, landed("params", "params loaded"))

        gate_b = stat[:, 62:64]

        def pool_setup():
            pool.memset(ident[:, :], 0.0).then_inc(pool_steps, PO.step())
            pool.memset(mask32[:, :], 0.0).then_inc(pool_steps, PO.step())
            pool.iota(iota_i, [[1, S]], base=0, channel_multiplier=0).then_inc(pool_steps, PO.step("iota"))
            pool.wait_ge(pool_steps, PO.n)
            pool.affine_select(out=ident[:, :], in_=ident[:, :], compare_op=ALU.not_equal, fill=1.0, base=0,
                                      pattern=[[-1, P]], channel_multiplier=1).then_inc(pool_steps, PO.step("ident"))
            pool.wait_ge(pool_steps, PO.n)
            pool.memset(mask32[0:64, 0:16], 1.0).then_inc(pool_steps, PO.step())
            pool.memset(mask32[64:128, 16:32], 1.0).then_inc(pool_steps, PO.step("mask32"))
            pool.wait_ge(pool_steps, PO.n)

        iota_i = area(1200, S).bitcast(mybir.dt.int32)

        def dve_setup():
            dve.wait_ge(params, count_of("params loaded"))
            dve.tensor_copy(st_s[64:96, :].rearrange("j (two p) -> j two p", two=2),
                                   st_dt[64:96, :].unsqueeze(2).to_broadcast([32, 2, 64])).then_inc(dve_steps, VE.step("log_dt spread"))
            dve.wait_ge(dve_steps, VE.n)
            dve.wait_ge(pool_steps, count_of("iota"))
            dve.tensor_copy(iota16[:, :], iota_i[:, 0:PR_K]).then_inc(dve_steps, VE.step())
            dve.tensor_copy(t_row[:, :], iota_i).then_inc(dve_steps, VE.step("t_row"))
            o = tile_of(VE, "par")
            dve.tensor_copy(col[:, :], o[:, 0:COL_ROWS]).then_inc(dve_steps, VE.step())
            dve.tensor_copy(col_dw[:, :, :], o[:, 104:352].rearrange("p (a b) -> p a b", a=2)).then_inc(dve_steps, VE.step())
            dve.tensor_copy(col_s5[:, :], o[:, 352:448]).then_inc(dve_steps, VE.step())
            dve.tensor_copy(col_rg[:, :], o[0:RG_D, 448:512]).then_inc(dve_steps, VE.step("read par"))
            o = tile_of(VE, "sk")
            dve.tensor_copy(skT[:, :, :].rearrange("p a b -> p (a b)"), o).then_inc(dve_steps, VE.step("read sk"))
            dve.wait_ge(dve_steps, VE.n)

        t_row = sb("t_row", [P, S])

        def pe_setup():
            pe.wait_ge(pool_steps, count_of("ident"))
            pe.wait_ge(tokens, count_of("x loaded"))
            pe_transposes("x0", lambda t, k: x_tok[:, t, 128 * k:128 * k + 128])
            pe.wait_ge(memory, count_of("mem loaded"))
            pe_transposes("mem", lambda t, k: mem_tok[:, t, 128 * k:128 * k + 128])
            pe.wait_ge(dve_steps, count_of("log_dt spread"))
            pe.wait_ge(params, count_of("params loaded"))
            o = open_tile("par")
            pe.transpose(o[:, 0:COL_ROWS], st_a[0:COL_ROWS, :], ident[0:COL_ROWS, 0:COL_ROWS])
            for h in range(2):
                pe.transpose(o[:, 104 + 124 * h:228 + 124 * h], st_b[0:124, h, :], ident[0:124, 0:124])
            pe.transpose(o[:, 352:448], st_s[0:96, :], ident[0:96, 0:96])
            pe.transpose(o[0:RG_D, 448:512], st_r[0:64, :], ident[0:64, 0:64]).then_inc(pe_steps, TE.step("tile par"))
            o = open_tile("sk")
            for n in range(4):
                i = pe.transpose(o[:, 128 * n:128 * n + 128], st_k[:, n, :], ident[:, :])
            i.then_inc(pe_steps, TE.step("tile sk"))

        def pe_memory():
            wait_transposed(TE, "mem")
            for i in range(DEPTH):
                w = chunk(f"wkv{i}.0", TE)
                pe_columns(f"kv{i}.k", w, mem_fm)
                release(f"wkv{i}.0")
                w = chunk(f"wkv{i}.1", TE)
                pe_token_rows(f"kv{i}.v", w, mem_fm)
                release(f"wkv{i}.1")

        def act_memory():
            for i in range(DEPTH):
                o = tile_of(AC, f"kv{i}.k")
                act.copy(k_mem[:, i, :, :].rearrange("p a b -> p (a b)"), o).then_inc(act_steps, AC.step(f"read kv{i}.k"))
                o = tile_of(AC, f"kv{i}.v")
                act.copy(v_mem[:, i, :, :].rearrange("p a b -> p (a b)"), o).then_inc(act_steps, AC.step(f"read kv{i}.v"))
                found[f"kv{i} ready"] = (AC.who, AC.n)

        q_fm, kk_fm = area(0, ML_K, S), area(1536, ML_K, S)
        v_tok = area(3072, TT, ML_HEADS, ML_DH + 1)
        o_sig = area(4620, TT, ML_W)
        g_if, g_b, g_a, g_g, g_e, g_1 = (area(6156, 2, S), area(6668, S), area(6924, S), area(7180, S), area(7436, S),
                                         area(7692, S))
        a_col = area(7948, 2, TT, ML_HEADS)
        decay = area(7968, ML_HEADS, 384)
        sT = area(9504, ML_HEADS, 384)
        h_tok = area(11040, TT, ML_W)
        sel = area(12576, ML_HEADS, P)
        xq0, p0, pT0 = area(13088, 2, S), area(13600, XA_HEADS, TT, S), area(15648, XA_HEADS, 2, S)
        den = area(17696, ML_HEADS, TT)
        mbn, mag = area(17704, TT * ML_HEADS, 6), area(17760, TT * ML_HEADS, 2)
        mrs = area(17780, TT * ML_HEADS)
        HEAD_PARTS = [[(0, 0, 128), (1, 0, 64)], [(1, 64, 128), (2, 0, 128)], [(3, 0, 128), (4, 0, 64)], [(4, 64, 128), (5, 0, 128)]]

        def pe_mlstm():
            wait_transposed(TE, "x0")
            w = chunk("m.gx", TE)
            o = open_tile("m.gates")
            for half in range(2):
                for k in range(KD):
                    i = mm(o[0:4, 256 * half:256 * half + 256], w[:, k, 4 * half:4 * half + 4], x_fm[:, k, :], k == 0, k == KD - 1)
            i.then_inc(pe_steps, TE.step("tile m.gates"))
            pe_columns("m.xq", w[:, :, 8:264], x_fm)
            release("m.gx")
            for c in range(6):
                w = chunk(f"m.{c}", TE)
                pe_columns(f"m.{c}", w, x_fm)
                release(f"m.{c}")
            for c in range(6, 12):
                w = chunk(f"m.{c}", TE)
                pe_token_rows(f"m.{c}", w, x_fm)
                release(f"m.{c}")
            pe.wait_ge(act_steps, count_of("gates done"))
            o = open_tile("m.col")
            for n, src in enumerate((g_a, g_e)):
                for t in range(TT):
                    i = pe.transpose(o[:, 8 * n + 4 * t:8 * n + 4 * t + 4], src[0:4, 128 * t:128 * t + 128], ident[0:4, 0:4])
            i.then_inc(pe_steps, TE.step("tile m.col"))
            pe.wait_ge(act_steps, count_of("read m.5"))
            pe.wait_ge(dve_steps, count_of("read m.4"))
            for h in range(ML_HEADS):
                o = open_tile(f"m.G{h}")
                mm(o[:, 0:S], sel[0:4, h, :], g_g[0:4, :], True, True).then_inc(pe_steps, TE.step(f"tile m.G{h}"))
                o = open_tile(f"m.S{h}")
                parts = HEAD_PARTS[h]
                for n, (tile, a, b) in enumerate(parts):
                    mm(o[:, 0:S], kk_fm[a:b, tile, 0:P], q_fm[a:b, tile, :], n == 0, n == len(parts) - 1)
                for n, (tile, a, b) in enumerate(parts):
                    i = mm(o[:, S:S + P], kk_fm[a:b, tile, P:S], q_fm[a:b, tile, P:S], n == 0, n == len(parts) - 1)
                i.then_inc(pe_steps, TE.step(f"tile m.S{h}"))
            pe_attention(0, xq0, lambda h: p0[:, h, :, :], lambda h: pT0[:, h, :, :], ML_K)
            pe.wait_ge(dve_steps, count_of("read m.8"))
            for h in range(ML_HEADS):
                pe.wait_ge(dve_steps, count_of(f"sT{h}"))
                o = open_tile(f"m.N{h}")
                mm(o[:, 0:193], sT[:, h, 0:P], v_tok[:, 0, h, :], True, True)
                mm(o[:, 256:449], sT[:, h, P:S], v_tok[:, 0, h, :], True, False)
                mm(o[:, 256:449], sT[:, h, S:S + P], v_tok[:, 1, h, :], False, True).then_inc(pe_steps, TE.step(f"tile m.N{h}"))
            pe.wait_ge(dve_steps, count_of("y mlstm"))
            pe_transposes("my", lambda t, k: h_tok[:, t, 128 * k:128 * k + 128], ML_K)
            wait_transposed_n(TE, "my", ML_K)
            pe.wait_ge(act_steps, count_of("xa0 ready"))
            pe_into_acc("mix0", [f"wout0.{c}" for c in range(ML_K // 2)] + ["wout0.x"], lambda k: mix_fm[:, k, :])

        def wait_transposed_n(e, name, n):
            for c in range(n // 2):
                engine_of[e.who].wait_ge(act_steps, count_of(f"read {name}.{c}"))

        def act_mlstm():
            o = tile_of(AC, "m.xq")
            act.copy(xq0.rearrange("p a b -> p (a b)"), o).then_inc(act_steps, AC.step("read m.xq"))
            found["xq0 ready"] = (AC.who, AC.n)
            act.wait_ge(dve_steps, count_of("abs f"))
            act.activation(g_e[0:4, :], g_e[0:4, :], ACT.Exp, scale=-1.0).then_inc(act_steps, AC.step())
            act.wait_ge(act_steps, AC.n)
            act.activation(g_e[0:4, :], g_e[0:4, :], ACT.Ln, bias=1.0).then_inc(act_steps, AC.step("log1p"))
            act.wait_ge(act_steps, AC.n)
            for c in (1, 3, 5):
                o = tile_of(AC, f"m.{c}")
                dst = (q_fm if c < 3 else kk_fm)[:, 2 * (c % 3):2 * (c % 3) + 2, :]
                act.copy(dst.rearrange("p a b -> p (a b)"), o).then_inc(act_steps, AC.step(f"read m.{c}"))
            act.wait_ge(dve_steps, count_of("guard sum"))
            act.activation(g_e[0:4, :], g_e[0:4, :], ACT.Exp, scale=-1.0).then_inc(act_steps, AC.step("gates done"))
            act.wait_ge(act_steps, AC.n)
            for c in range(9, 12):
                o = tile_of(AC, f"m.{c}")
                act.activation(o_sig[:, :, 256 * (c - 9):256 * (c - 9) + 256], o.rearrange("p (t n) -> p t n", t=TT),
                                       ACT.Sigmoid).then_inc(act_steps, AC.step(f"read m.{c}"))
            for h in range(ML_HEADS):
                act.wait_ge(dve_steps, count_of(f"decay arg{h}"))
                act.activation(decay[:, h, :], decay[:, h, :], ACT.Exp).then_inc(act_steps, AC.step(f"decay exp{h}"))
            act_attention(0, lambda h: p0[:, h, :, :], lambda h: pT0[:, h, :, :], ML_K)
            act_sqrt("mhead", mrs)
            for c in range(ML_K // 2):
                o = tile_of(AC, f"my.{c}")
                act.copy(mix_fm[:, 2 * c:2 * c + 2, :].rearrange("p a b -> p (a b)"), o).then_inc(act_steps, AC.step(f"read my.{c}"))

        def pool_mlstm():
            for h in range(ML_HEADS):
                pool.wait_ge(act_steps, count_of(f"decay exp{h}"))
                for a in (0, S):
                    pool.affine_select(out=decay[:, h, a:a + P], in_=decay[:, h, a:a + P], compare_op=ALU.is_ge,
                                               fill=0.0, base=0, pattern=[[1, P]], channel_multiplier=-1).then_inc(pool_steps, PO.step(f"decay {h}"))

        def dve_mlstm():
            o = tile_of(VE, "m.gates")
            dve.tensor_scalar(g_if[0:4, 0, :], o[0:4, 0:S], gate_b[0:4, 0:1], None, ALU.add).then_inc(dve_steps, VE.step())
            dve.tensor_scalar(g_if[0:4, 1, :], o[0:4, S:2 * S], gate_b[0:4, 1:2], None, ALU.add).then_inc(dve_steps, VE.step("read m.gates"))
            dve.wait_ge(dve_steps, VE.n)
            dve.memset(g_1[0:4, :], 1.0).then_inc(dve_steps, VE.step())
            dve.memset(v_tok[:, :, :, ML_DH:ML_DH + 1], 1.0).then_inc(dve_steps, VE.step())
            dve.tensor_copy(sel[0:4, :, :], ident[0:4, 0:4].unsqueeze(2).to_broadcast([4, ML_HEADS, P])).then_inc(dve_steps, VE.step("sel"))
            dve.scalar_tensor_tensor(g_e[0:4, :], g_if[0:4, 1, :], -1.0, g_if[0:4, 1, :], ALU.mult, ALU.max).then_inc(dve_steps, VE.step("abs f"))
            dve.wait_ge(dve_steps, VE.n)
            for c in (0, 2, 4):
                o = tile_of(VE, f"m.{c}")
                dst = (q_fm if c < 3 else kk_fm)[:, 2 * (c % 3):2 * (c % 3) + 2, :]
                dve.tensor_copy(dst.rearrange("p a b -> p (a b)"), o).then_inc(dve_steps, VE.step(f"read m.{c}"))
            dve.wait_ge(act_steps, count_of("log1p"))
            dve.scalar_tensor_tensor(g_a[0:4, :], g_if[0:4, 1, :], 0.0, g_e[0:4, :], ALU.min, ALU.subtract).then_inc(dve_steps, VE.step())
            dve.wait_ge(dve_steps, VE.n)
            dve.tensor_tensor_scan(g_b[0:4, :], g_1[0:4, :], g_a[0:4, :], 0.0, ALU.mult, ALU.add).then_inc(dve_steps, VE.step())
            dve.wait_ge(dve_steps, VE.n)
            dve.tensor_tensor(g_a[0:4, :], g_if[0:4, 0, :], g_b[0:4, :], ALU.subtract).then_inc(dve_steps, VE.step())
            dve.wait_ge(dve_steps, VE.n)
            dve.tensor_tensor_scan(g_g[0:4, :], g_1[0:4, :], g_a[0:4, :], 0.0, ALU.mult, ALU.max).then_inc(dve_steps, VE.step())
            dve.wait_ge(dve_steps, VE.n)
            dve.tensor_tensor(g_e[0:4, :], g_b[0:4, :], g_g[0:4, :], ALU.add).then_inc(dve_steps, VE.step("guard sum"))
            dve.wait_ge(dve_steps, VE.n)
            dve.tensor_scalar(g_g[0:4, :], g_g[0:4, :], -1.0, None, ALU.mult).then_inc(dve_steps, VE.step("neg G"))
            dve.wait_ge(dve_steps, VE.n)
            for c in range(3):
                o = tile_of(VE, f"m.{6 + c}").rearrange("p (t n) -> p t n", t=TT)
                at = 256 * c
                while at < 256 * c + 256:
                    h, a = divmod(at, ML_DH)
                    n = min(ML_DH - a, 256 * c + 256 - at)
                    dve.tensor_copy(v_tok[:, :, h, a:a + n], o[:, :, at - 256 * c:at - 256 * c + n]).then_inc(dve_steps, VE.step(f"read m.{6 + c}"))
                    at += n
            o = tile_of(VE, "m.col")
            dve.tensor_copy(a_flat, o[:, 0:16]).then_inc(dve_steps, VE.step("read m.col"))
            dve.wait_ge(dve_steps, VE.n)
            for h in range(ML_HEADS):
                o = tile_of(VE, f"m.G{h}")
                dve.tensor_scalar(decay[:, h, 0:S], o[:, 0:S], a_flat[:, h:h + 1], 0.0, ALU.add, ALU.min).then_inc(dve_steps, VE.step())
                dve.tensor_scalar(decay[:, h, S:S + P], o[:, P:S], a_flat[:, 4 + h:5 + h], 0.0, ALU.add, ALU.min).then_inc(dve_steps, VE.step(f"read m.G{h}"))
                found[f"decay arg{h}"] = (VE.who, VE.n)
                if h:
                    dve_weights(h - 1)
            dve_weights(ML_HEADS - 1)
            attention_softmax(0, lambda h: p0[:, h, :, :], None, 0)
            for h in range(ML_HEADS):
                o = tile_of(VE, f"m.N{h}").rearrange("p (t n) -> p t n", t=TT)
                d = den[:, h, :]
                dve.tensor_copy(d.unsqueeze(2), o[:, :, ML_DH:ML_DH + 1]).then_inc(dve_steps, VE.step())
                dve.wait_ge(dve_steps, VE.n)
                dve.scalar_tensor_tensor(d, d, -1.0, d, ALU.mult, ALU.max).then_inc(dve_steps, VE.step())
                dve.wait_ge(dve_steps, VE.n)
                dve.tensor_tensor(d, d, a_flat[:, 8 + h:16:4], ALU.max).then_inc(dve_steps, VE.step())
                dve.wait_ge(dve_steps, VE.n)
                dve.reciprocal(d, d).then_inc(dve_steps, VE.step())
                dve.wait_ge(dve_steps, VE.n)
                for t in range(TT):
                    dve.tensor_scalar(h_tok[:, t, ML_DH * h:ML_DH * h + ML_DH], o[:, t, 0:ML_DH], d[:, t:t + 1], None, ALU.mult).then_inc(dve_steps, VE.step(f"read m.N{h}"))
            dve.wait_ge(dve_steps, VE.n)
            for t in range(TT):
                for h in range(ML_HEADS):
                    dve.bn_stats(mbn[:, 4 * t + h, :], h_tok[:, t, ML_DH * h:ML_DH * h + ML_DH]).then_inc(dve_steps, VE.step())
            dve.wait_ge(dve_steps, VE.n)
            for n in range(TT * ML_HEADS):
                dve.bn_aggr(mag[:, n, :], mbn[:, n, :]).then_inc(dve_steps, VE.step())
            dve.wait_ge(dve_steps, VE.n)
            dve.tensor_scalar(mrs, mag[:, :, 1], LN_EPS, None, ALU.add).then_inc(dve_steps, VE.step("var mhead"))
            dve.wait_ge(dve_steps, VE.n)
            dve.wait_ge(act_steps, count_of("std mhead"))
            dve.reciprocal(mrs, mrs).then_inc(dve_steps, VE.step())
            dve.wait_ge(dve_steps, VE.n)
            for t in range(TT):
                for h in range(ML_HEADS):
                    v, n = h_tok[:, t, ML_DH * h:ML_DH * h + ML_DH], 4 * t + h
                    dve.tensor_scalar(v, v, mag[:, n, 0:1], mrs[:, n:n + 1], ALU.subtract, ALU.mult).then_inc(dve_steps, VE.step())
            dve.wait_ge(dve_steps, VE.n)
            g = row("mnorm", VE)[:, 0:ML_W]
            for t in range(TT):
                dve.tensor_tensor(h_tok[:, t, :], h_tok[:, t, :], g, ALU.mult).then_inc(dve_steps, VE.step("row mnorm"))
            dve.wait_ge(dve_steps, VE.n)
            dve.wait_ge(act_steps, count_of("read m.11"))
            for t in range(TT):
                dve.tensor_tensor(h_tok[:, t, :], h_tok[:, t, :], o_sig[:, t, :], ALU.mult).then_inc(dve_steps, VE.step("y mlstm"))
            dve_layer_norm(0, "mix", "ln1g0", "ln1b0")

        a_flat = area(7948, 16)

        def dve_weights(h):
            dve.wait_ge(pool_steps, count_of(f"decay {h}"))
            o = tile_of(VE, f"m.S{h}")
            dve.scalar_tensor_tensor(sT[:, h, :], o[:, 0:384], ML_DH ** -0.5, decay[:, h, :], ALU.mult, ALU.mult).then_inc(dve_steps, VE.step(f"read m.S{h}"))
            found[f"sT{h}"] = (VE.who, VE.n)

        u_ring, v_ring = area(0, U_SLOTS, D), area(8192, V_SLOTS, D)
        qT = area(0, 2 * PR_HEADS, S)
        sc = area(16384, TT, 2 * PR_HEADS * PR_KEYS)
        diag = area(20480, PR_K, P)

        def small(at, slots, *shape):
            n = int(np.prod(shape))
            return [area(at + n * s, *shape) for s in range(slots)]

        sv, si_u, si_f = small(22528, 2, 2, PR_K), small(22592, 2, 2, PR_K), small(22656, 2, 2, PR_K)
        cand, eq = small(22720, 1, PR_K, PR_K)[0], area(22976, 2 * PR_K, PR_K)
        fv, fi = small(23488, 2, PR_K), small(23520, 2, PR_K)
        ab_u, ab_f, ids = area(23552, 2, PR_K), area(23584, 2, PR_K), area(23616, 2, PR_K)
        ix = small(23648, 4, PR_K)
        ex, dots, gel, coef = small(23712, 2, PR_K), small(23744, 2, PR_K), small(23776, 2, PR_K), small(23808, 2, PR_K)
        nmx, sm = small(23840, 2, 1), small(23842, 2, 1)
        NJ = TT * PR_HEADS

        def pe_peer(i):
            wait_transposed(TE, f"xp{i}t")
            for c in range(8):
                w = chunk(f"wq{i}.{c}", TE)
                pe_columns(f"pq{i}.{c}", w, x_fm)
                release(f"wq{i}.{c}")
            for c in range(8):
                pe.wait_ge(*by(f"read pq{i}.{c}"))
            for t in range(TT):
                for c in range(4):
                    o = open_tile(f"ps{i}.{t}{c}")
                    for n in range(4):
                        hp = 4 * c + n
                        ins = mm(o[:, 128 * n:128 * n + 128], qT[:, hp, 128 * t:128 * t + 128], skT[:, 2 * i + hp % 2, :], True, True)
                    ins.then_inc(pe_steps, TE.step(f"tile ps{i}.{t}{c}"))
            for j in range(NJ):
                t = j // PR_HEADS
                for k in range(PR_K):
                    g = PR_K * (NJ * i + j) + k
                    pe.wait_ge(act_steps, count_of(f"diag {i}.{j}.{k}"))
                    pe.wait_ge(sems[f"v_rows{g % V_SLOTS}"], 16 * (g // V_SLOTS + 1))
                    for half in range(2):
                        ins = mm(acc[:, 2 * t + half, :], diag[:, k, :], v_ring[:, g % V_SLOTS, 512 * half:512 * half + 512],
                                 j % PR_HEADS == 0 and k == 0, j % PR_HEADS == PR_HEADS - 1 and k == PR_K - 1)
                    ins.then_inc(pe_steps, TE.step(f"v used {g}"))
            found[f"acc peer{i}"] = (TE.who, TE.n)

        def act_peer(i):
            for c in range(0, 8, 2):
                o = tile_of(AC, f"pq{i}.{c}")
                act.copy(qT[:, 2 * c:2 * c + 2, :].rearrange("p a b -> p (a b)"), o).then_inc(act_steps, AC.step(f"read pq{i}.{c}"))
            for t in range(TT):
                for c in range(4):
                    o = tile_of(AC, f"ps{i}.{t}{c}")
                    act.copy(sc[:, t, 512 * c:512 * c + 512], o).then_inc(act_steps, AC.step(f"read ps{i}.{t}{c}"))
            for j in range(NJ + 1):
                if j < NJ:
                    b = j % 2
                    act.wait_ge(dve_steps, count_of(f"nmax {i}.{j}"))
                    act.activation(ex[b], fv[b], ACT.Exp, bias=nmx[b], accum_out=sm[b]).then_inc(act_steps, AC.step(f"ex {i}.{j}"))
                if j:
                    b = (j - 1) % 2
                    act.wait_ge(dve_steps, count_of(f"dots {i}.{j - 1}"))
                    act.activation(gel[b], dots[b], ACT.Gelu).then_inc(act_steps, AC.step(f"gelu {i}.{j - 1}"))
                    act.wait_ge(dve_steps, count_of(f"coef {i}.{j - 1}"))
                    for k in range(PR_K):
                        g = PR_K * (NJ * i + j - 1) + k
                        if j > 1:
                            act.wait_ge(pe_steps, count_of(f"v used {g - PR_K}"))
                        act.activation(diag[:, k, :], ident[:, :], ACT.Copy, scale=coef[b][:, k:k + 1]).then_inc(act_steps, AC.step(f"diag {i}.{j - 1}.{k}"))

        def dve_topk(out_v, out_i, s):
            a, b = slice(0, 8), slice(8, 16)
            dve.max(out_v[:, a], s).then_inc(dve_steps, VE.step())
            dve.wait_ge(dve_steps, VE.n)
            dve.max_index(out_i[:, a], out_v[:, a], s).then_inc(dve_steps, VE.step())
            dve.wait_ge(dve_steps, VE.n)
            dve.match_replace(s, out_v[:, a], s, NEG).then_inc(dve_steps, VE.step())
            dve.wait_ge(dve_steps, VE.n)
            dve.max(out_v[:, b], s).then_inc(dve_steps, VE.step())
            dve.wait_ge(dve_steps, VE.n)
            dve.max_index(out_i[:, b], out_v[:, b], s).then_inc(dve_steps, VE.step())
            dve.wait_ge(dve_steps, VE.n)

        def dve_select(i, j):
            t, h, b = j // PR_HEADS, j % PR_HEADS, j % 2
            for p in range(2):
                dve_topk(sv[b][:, p, :], si_u[b][:, p, :].bitcast(U32), sc[:, t, 256 * h + 128 * p:256 * h + 128 * p + 128])
            dve.tensor_scalar(si_f[b][:, 0, :], si_u[b][:, 0, :].bitcast(U32), float(PR_KEYS * i), None, ALU.add).then_inc(dve_steps, VE.step())
            dve.tensor_copy(si_f[b][:, 1, :], si_u[b][:, 1, :].bitcast(U32)).then_inc(dve_steps, VE.step())
            dve.tensor_tensor(cand, sv[b][:, 0, :].unsqueeze(2).to_broadcast([P, PR_K, PR_K]),
                                     sv[b][:, 1, :].unsqueeze(1).to_broadcast([P, PR_K, PR_K]), ALU.add).then_inc(dve_steps, VE.step())
            dve.wait_ge(dve_steps, VE.n)
            if j >= 2:
                dve.wait_ge(act_steps, count_of(f"ex {i}.{j - 2}"))
            dve_topk(fv[b], fi[b].bitcast(U32), cand.rearrange("p a b -> p (a b)"))
            dve.tensor_scalar(nmx[b], fv[b][:, 0:1], -1.0, None, ALU.mult).then_inc(dve_steps, VE.step(f"nmax {i}.{j}"))
            dve.tensor_scalar(ab_u[:, 0, :].bitcast(U32), fi[b].bitcast(U32), 4, None, ALU.logical_shift_right).then_inc(dve_steps, VE.step())
            dve.tensor_scalar(ab_u[:, 1, :].bitcast(U32), fi[b].bitcast(U32), 15, None, ALU.bitwise_and).then_inc(dve_steps, VE.step())
            dve.wait_ge(dve_steps, VE.n)
            dve.tensor_copy(ab_f, ab_u.bitcast(U32)).then_inc(dve_steps, VE.step())
            dve.wait_ge(dve_steps, VE.n)
            dve.tensor_tensor(eq, ab_f.rearrange("p a b -> p (a b)").unsqueeze(2).to_broadcast([P, 2 * PR_K, PR_K]),
                                     iota16[:, :].unsqueeze(1).to_broadcast([P, 2 * PR_K, PR_K]), ALU.is_equal).then_inc(dve_steps, VE.step())
            dve.wait_ge(dve_steps, VE.n)
            eq4 = eq.rearrange("p (a b) c -> p a b c", a=2)
            dve.tensor_tensor(eq4, eq4, si_f[b].unsqueeze(2).to_broadcast([P, 2, PR_K, PR_K]), ALU.mult).then_inc(dve_steps, VE.step())
            dve.wait_ge(dve_steps, VE.n)
            dve.tensor_reduce(ids.rearrange("p a b -> p (a b)"), eq, AX, ALU.add).then_inc(dve_steps, VE.step())
            dve.wait_ge(dve_steps, VE.n)
            if j >= 4:
                dve.wait_ge(pe_steps, count_of(f"v used {PR_K * (NJ * i + j - 4) + PR_K - 1}"))
            dve.scalar_tensor_tensor(ix[j % 4].bitcast(U32), ids[:, 0, :], float(PR_KEYS), ids[:, 1, :], ALU.mult, ALU.add).then_inc(dve_steps, VE.step(f"ix {i}.{j}"))
            dve.wait_ge(dve_steps, VE.n)

        def dve_dots(i, j, k0, k1):
            t, b = j // PR_HEADS, j % 2
            if k0 == 0 and j >= 2:
                dve.wait_ge(act_steps, count_of(f"gelu {i}.{j - 2}"))
            for k in range(k0, k1):
                g = PR_K * (NJ * i + j) + k
                dve.wait_ge(sems[f"u_rows{g % U_SLOTS}"], 16 * (g // U_SLOTS + 1))
                r = u_ring[:, g % U_SLOTS, :]
                dve.tensor_tensor_reduce(r, r, x_tok[:, t, :], 1.0, 0.0, ALU.mult, ALU.add, dots[b][:, k:k + 1]).then_inc(dve_steps, VE.step(f"u used {g}"))
            if k1 == PR_K:
                found[f"dots {i}.{j}"] = (VE.who, VE.n)

        def dve_coef(i, j):
            b = j % 2
            dve.wait_ge(act_steps, count_of(f"ex {i}.{j}"))
            dve.reciprocal(sm[b], sm[b]).then_inc(dve_steps, VE.step())
            dve.wait_ge(dve_steps, VE.n)
            dve.wait_ge(act_steps, count_of(f"gelu {i}.{j}"))
            if j >= 2:
                dve.wait_ge(act_steps, count_of(f"diag {i}.{j - 2}.{PR_K - 1}"))
            dve.scalar_tensor_tensor(coef[b], ex[b], sm[b], gel[b], ALU.mult, ALU.mult).then_inc(dve_steps, VE.step(f"coef {i}.{j}"))
            dve.wait_ge(dve_steps, VE.n)

        def dve_peer(i):
            for c in range(1, 8, 2):
                o = tile_of(VE, f"pq{i}.{c}")
                dve.tensor_copy(qT[:, 2 * c:2 * c + 2, :].rearrange("p a b -> p (a b)"), o).then_inc(dve_steps, VE.step(f"read pq{i}.{c}"))
            for c in range(4):
                dve.wait_ge(act_steps, count_of(f"read ps{i}.0{c}"))
            dve_select(i, 0)
            for j in range(NJ):
                dve_dots(i, j, 0, 4)
                if j:
                    dve_coef(i, j - 1)
                dve_dots(i, j, 4, 8)
                if j + 1 < NJ:
                    if (j + 1) % PR_HEADS == 0:
                        for c in range(4):
                            dve.wait_ge(act_steps, count_of(f"read ps{i}.1{c}"))
                    dve_select(i, j + 1)
                dve_dots(i, j, 8, PR_K)
            dve_coef(i, NJ - 1)
            dve_layer_norm(i, "peer", f"ln2g{i}", f"ln2b{i}")

        u_table, v_table = (A[n].rearrange("l e d -> (l e) d") for n in ("peer_u", "peer_v"))

        def pool_peer(i):
            def gather(j, k, ring_, sem_, slots, used, table):
                g = PR_K * (NJ * i + j) + k
                if g >= slots:
                    pool.wait_ge(*by(f"{used} used {g - slots}"))
                pool.indirect_dma_start(ring_[:, g % slots, :], None, table,
                                                  bass.IndirectOffsetOnAxis(ix[j % 4][:, k:k + 1].bitcast(U32), 0),
                                                  element_offset=0).then_inc(sems[f"{sem_}{g % slots}"], landed(f"{sem_}{g % slots}", f"{sem_} {g}"))

            for c in range(4):
                pool.wait_ge(act_steps, count_of(f"read ps{i}.1{c}"))
            for j in range(NJ + 1):
                if j < NJ:
                    pool.wait_ge(dve_steps, count_of(f"ix {i}.{j}"))
                for k in range(PR_K):
                    if j < NJ:
                        gather(j, k, u_ring, "u_rows", U_SLOTS, "u", u_table)
                    if j:
                        gather(j - 1, k, v_ring, "v_rows", V_SLOTS, "v", v_table)

        x_pad = area(0, RG_B, S + RG_CONV - 1)
        xc, r_g, i_g, a_t, th, l1, gg = (area(2072 + 2048 * n, RG_B, S) for n in range(7))
        xq1, p1, pT1 = area(16408, 2, S), area(16920, XA_HEADS, TT, S), area(18968, XA_HEADS, 2, S)
        sp_c = area(21016, 4, RG_B)
        xc_tmp = area(21056, S)

        def pe_rglru():
            wait_transposed(TE, "xrt")
            for c in range(4):
                w = chunk(f"r.x{c}", TE)
                pe_columns(f"r.x{c}", w, x_fm, RG_D)
                release(f"r.x{c}")
            wa, wi = chunk("r.a", TE), chunk("r.i", TE)
            for b in range(RG_B):
                pe.wait_ge(dve_steps, count_of(f"xc {b}"))
                o = open_tile(f"r.g{b}.ri")
                mm(o[0:RG_D, 0:S], wa[:, b, :], xc[0:RG_D, b, :], True, True)
                mm(o[0:RG_D, S:2 * S], wi[:, b, :], xc[0:RG_D, b, :], True, True).then_inc(pe_steps, TE.step(f"tile r.g{b}.ri"))
            release("r.a")
            release("r.i")
            w = chunk("r.q", TE)
            pe_columns("r.xq", w, x_fm)
            release("r.q")
            for c in range(4):
                w = chunk(f"r.g{c}", TE)
                pe_columns(f"r.gate{c}", w, x_fm, RG_D)
                release(f"r.g{c}")
            pe_attention(1, xq1, lambda h: p1[:, h, :, :], lambda h: pT1[:, h, :, :], RG_B)
            pe.wait_ge(act_steps, count_of("xa1 ready"))
            pe.wait_ge(dve_steps, count_of("y rglru"))
            pe.wait_ge(dve_steps, count_of("acc peer0 read"))
            pe_into_acc("mix1", [f"wout1.{c}" for c in range(RG_B // 2)] + ["wout1.x"],
                        lambda k: mix_fm[0:RG_D, k, :] if k < RG_B else mix_fm[:, k, :])

        def act_rglru():
            R = slice(0, RG_D)
            act.wait_ge(dve_steps, count_of("abs lam"))
            act.activation(sp_c[R, 1, :], sp_c[R, 1, :], ACT.Exp, scale=-1.0).then_inc(act_steps, AC.step())
            act.wait_ge(act_steps, AC.n)
            act.activation(sp_c[R, 1, :], sp_c[R, 1, :], ACT.Ln, bias=1.0).then_inc(act_steps, AC.step("log1p lam"))
            for b in range(RG_B):
                o = tile_of(AC, f"r.g{b}.ri")
                act.activation(r_g[R, b, :], o[R, 0:S], ACT.Sigmoid, bias=col_rg[:, RG_BA + b:RG_BA + b + 1]).then_inc(act_steps, AC.step())
                act.activation(i_g[R, b, :], o[R, S:2 * S], ACT.Sigmoid, bias=col_rg[:, RG_BX + b:RG_BX + b + 1]).then_inc(act_steps, AC.step(f"read r.g{b}.ri"))
            act.wait_ge(act_steps, AC.n)
            act.wait_ge(dve_steps, count_of("softplus lam"))
            for b in range(RG_B):
                act.activation(a_t[R, b, :], r_g[R, b, :], ACT.Exp, scale=sp_c[R, 2, b:b + 1]).then_inc(act_steps, AC.step())
                act.activation(th[R, b, :], r_g[R, b, :], ACT.Tanh, scale=sp_c[R, 3, b:b + 1]).then_inc(act_steps, AC.step())
            act.wait_ge(act_steps, AC.n)
            act.activation(l1[R, :, :], th[R, :, :], ACT.Ln, bias=1.0).then_inc(act_steps, AC.step())
            act.wait_ge(act_steps, AC.n)
            act.activation(l1[R, :, :], l1[R, :, :], ACT.Exp, scale=-0.5).then_inc(act_steps, AC.step())
            act.wait_ge(act_steps, AC.n)
            act.activation(th[R, :, :], th[R, :, :], ACT.Sqrt, scale=2.0).then_inc(act_steps, AC.step("sqrt parts"))
            o = tile_of(AC, "r.xq")
            act.copy(xq1.rearrange("p a b -> p (a b)"), o).then_inc(act_steps, AC.step("read r.xq"))
            found["xq1 ready"] = (AC.who, AC.n)
            for c in range(4):
                o = tile_of(AC, f"r.gate{c}")
                act.activation(gg[R, 2 * c:2 * c + 2, :].rearrange("p a b -> p (a b)"), o[R, :], ACT.Gelu).then_inc(act_steps, AC.step(f"read r.gate{c}"))
            act_attention(1, lambda h: p1[:, h, :, :], lambda h: pT1[:, h, :, :], RG_B)

        def dve_rglru():
            R = slice(0, RG_D)
            lam = col_rg[:, RG_LAM:RG_LAM + RG_B]
            dve.tensor_scalar(sp_c[R, 0, :], lam, -1.0, None, ALU.mult).then_inc(dve_steps, VE.step())
            dve.wait_ge(dve_steps, VE.n)
            dve.tensor_tensor(sp_c[R, 1, :], sp_c[R, 0, :], lam, ALU.max).then_inc(dve_steps, VE.step("abs lam"))
            dve.wait_ge(dve_steps, VE.n)
            dve.memset(x_pad[R, :, 0:RG_CONV - 1], 0.0).then_inc(dve_steps, VE.step())
            for c in range(4):
                o = tile_of(VE, f"r.x{c}")
                dve.tensor_copy(x_pad[R, 2 * c:2 * c + 2, RG_CONV - 1:], o[R, :].rearrange("p (a b) -> p a b", a=2)).then_inc(dve_steps, VE.step(f"read r.x{c}"))
                dve.wait_ge(dve_steps, VE.n)
                for b in (2 * c, 2 * c + 1):
                    def tap(k):
                        return col_rg[:, RG_B * k + b:RG_B * k + b + 1]
                    dve.tensor_scalar(xc[R, b, :], x_pad[R, b, 0:S], tap(0), col_rg[:, RG_CB + b:RG_CB + b + 1], ALU.mult, ALU.add).then_inc(dve_steps, VE.step())
                    dve.wait_ge(dve_steps, VE.n)
                    for k in range(1, RG_CONV):
                        dve.scalar_tensor_tensor(xc[R, b, :], x_pad[R, b, k:k + S], tap(k), xc[R, b, :], ALU.mult, ALU.add).then_inc(dve_steps, VE.step(f"xc {b}"))
                        dve.wait_ge(dve_steps, VE.n)
            dve.wait_ge(act_steps, count_of("log1p lam"))
            dve.scalar_tensor_tensor(sp_c[R, 1, :], sp_c[R, 0, :], 0.0, sp_c[R, 1, :], ALU.max, ALU.add).then_inc(dve_steps, VE.step())
            dve.wait_ge(dve_steps, VE.n)
            dve.tensor_scalar(sp_c[R, 2, :], sp_c[R, 1, :], -RG_C, None, ALU.mult).then_inc(dve_steps, VE.step())
            dve.tensor_scalar(sp_c[R, 3, :], sp_c[R, 1, :], RG_C, None, ALU.mult).then_inc(dve_steps, VE.step("softplus lam"))
            dve.wait_ge(dve_steps, VE.n)
            dve.wait_ge(act_steps, count_of(f"read r.g{RG_B - 1}.ri"))
            dve.tensor_tensor(i_g[R, :, :], i_g[R, :, :], xc[R, :, :], ALU.mult).then_inc(dve_steps, VE.step())
            dve.wait_ge(dve_steps, VE.n)
            dve.wait_ge(act_steps, count_of("sqrt parts"))
            dve.tensor_tensor(i_g[R, :, :], i_g[R, :, :], l1[R, :, :], ALU.mult).then_inc(dve_steps, VE.step())
            dve.wait_ge(dve_steps, VE.n)
            dve.tensor_tensor(i_g[R, :, :], i_g[R, :, :], th[R, :, :], ALU.mult).then_inc(dve_steps, VE.step())
            dve.wait_ge(dve_steps, VE.n)
            for b in range(RG_B):
                dve.tensor_tensor_scan(r_g[R, b, :], a_t[R, b, :], i_g[R, b, :], 0.0, ALU.mult, ALU.add).then_inc(dve_steps, VE.step())
            dve.wait_ge(dve_steps, VE.n)
            attention_softmax(1, lambda h: p1[:, h, :, :], None, 0)
            for c in range(4):
                dve.wait_ge(act_steps, count_of(f"read r.gate{c}"))
            dve.tensor_tensor(mix_fm[R, 0:RG_B, :], r_g[R, :, :], gg[R, :, :], ALU.mult).then_inc(dve_steps, VE.step("y rglru"))
            dve_layer_norm(1, "mix", "ln1g1", "ln1b1")

        hn = area(0, TT, D)
        junk = area(2048, TT, D)
        ssq, psq = stat[:, 32:34], stat[:, 34:36]

        def act_pre(n):
            act.wait_ge(dve_steps, count_of(f"x {n}"))
            for t in range(TT):
                act.activation(hn[:, t, :], x_tok[:, t, :], ACT.Square, accum_out=ssq[:, t:t + 1]).then_inc(act_steps, AC.step(f"ssq {n}"))
            act.wait_ge(dve_steps, count_of(f"var {n}"))
            act.sqrt(ssq, ssq).then_inc(act_steps, AC.step(f"std {n}"))
            x_transposed(n + "t", AC, x_fm, pre_scale(n))

        def pre_scale(n):
            l, s = int(n[3]), int(n[4])
            at = COL_PRE + 8 * (3 * l + s)
            return col[:, at:at + 8]

        def dve_pre(n):
            dve.wait_ge(act_steps, count_of(f"ssq {n}"))
            dve.tensor_scalar(ssq, ssq, 1.0 / D, RMS_EPS, ALU.mult, ALU.add).then_inc(dve_steps, VE.step(f"var {n}"))
            dve.wait_ge(dve_steps, VE.n)
            dve.wait_ge(act_steps, count_of(f"std {n}"))
            dve.reciprocal(ssq, ssq).then_inc(dve_steps, VE.step())
            dve.wait_ge(dve_steps, VE.n)
            for t in range(TT):
                dve.tensor_scalar(hn[:, t, :], x_tok[:, t, :], ssq[:, t:t + 1], None, ALU.mult).then_inc(dve_steps, VE.step(f"hn {n}"))
            x_transposed(n + "t", VE, x_fm, pre_scale(n))

        def pe_pre(n):
            pe.wait_ge(dve_steps, count_of(f"hn {n}"))
            pe_transposes(n + "t", lambda t, k: hn[:, t, 128 * k:128 * k + 128])
            wait_transposed(TE, n + "t")

        def act_post(n, src):
            for t in range(TT):
                act.activation(junk2[:, t, :], src(t), ACT.Square, accum_out=psq[:, t:t + 1]).then_inc(act_steps, AC.step(f"psq {n}"))
            act.wait_ge(dve_steps, count_of(f"pvar {n}"))
            act.sqrt(psq, psq).then_inc(act_steps, AC.step(f"pstd {n}"))

        junk2 = area(23952, TT, D)

        def acc_rows(t):
            return acc[:, 2 * t:2 * t + 2, :].rearrange("p a b -> p (a b)")

        def dve_post(n, src, gain, tmp, last):
            dve.wait_ge(act_steps, count_of(f"psq {n}"))
            dve.tensor_scalar(psq, psq, 1.0 / D, RMS_EPS, ALU.mult, ALU.add).then_inc(dve_steps, VE.step(f"pvar {n}"))
            dve.wait_ge(dve_steps, VE.n)
            dve.wait_ge(act_steps, count_of(f"pstd {n}"))
            dve.reciprocal(psq, psq).then_inc(dve_steps, VE.step())
            dve.wait_ge(dve_steps, VE.n)
            g = row("post" + n[3:], VE)
            for t in range(TT):
                dve.scalar_tensor_tensor(tmp[:, t, :], src(t), psq[:, t:t + 1], g, ALU.mult, ALU.mult).then_inc(dve_steps, VE.step(f"row post{n[3:]}"))
            dve.wait_ge(dve_steps, VE.n)
            found[f"acc {n} read"] = (VE.who, VE.n)
            for t in range(TT):
                dve.scalar_tensor_tensor(x_tok[:, t, :], tmp[:, t, :], gain, x_tok[:, t, :], ALU.mult, ALU.add).then_inc(dve_steps, VE.step(f"x {last}"))
            dve.wait_ge(dve_steps, VE.n)

        a_fm = area(4096, FF_T, S)
        sg = area(9728, 2, S)
        tmp_f = area(10240, TT, D)

        def pe_ffn(l, s, before):
            n = f"ffn{l}{s}"
            pe_pre(n)
            for c in range(FF_T // 2):
                w1, w3 = chunk(f"w1.{l}{s}.{c}", TE), chunk(f"w3.{l}{s}.{c}", TE)
                for f in range(2):
                    o = open_tile(f"{n}.{2 * c + f}")
                    for half, w in ((0, w1), (1, w3)):
                        for k in range(KD):
                            i = mm(o[:, S * half:S * half + S], w[:, k, P * f:P * f + P], x_fm[:, k, :], k == 0, k == KD - 1)
                    i.then_inc(pe_steps, TE.step(f"tile {n}.{2 * c + f}"))
                release(f"w1.{l}{s}.{c}")
                release(f"w3.{l}{s}.{c}")
            pe.wait_ge(dve_steps, count_of(f"acc {before} read"))
            pe.wait_ge(dve_steps, count_of(f"read {n}.{FF_T - 1}"))
            pe_into_acc(n, [f"w2.{l}{s}.{c}" for c in range(FF_T // 2)], lambda k: a_fm[:, k, :])

        def act_ffn(l, s):
            n = f"ffn{l}{s}"
            act_pre(n)
            for f in range(FF_T):
                o = tile_of(AC, f"{n}.{f}")
                if f >= 2:
                    act.wait_ge(dve_steps, count_of(f"read {n}.{f - 2}"))
                act.activation(sg[:, f % 2, :], o[:, 0:S], ACT.Silu).then_inc(act_steps, AC.step(f"silu {n}.{f}"))
            act.wait_ge(pe_steps, count_of(f"acc {n}"))
            act_post(n, acc_rows)

        def dve_ffn(l, s, last):
            n = f"ffn{l}{s}"
            dve_pre(n)
            for f in range(FF_T):
                dve.wait_ge(act_steps, count_of(f"silu {n}.{f}"))
                o = tile_of(VE, f"{n}.{f}")
                dve.tensor_tensor(a_fm[:, f, :], sg[:, f % 2, :], o[:, S:2 * S], ALU.mult).then_inc(dve_steps, VE.step(f"read {n}.{f}"))
            dve_post(n, acc_rows, 0.5, tmp_f, last)

        u_fm, y_fm = area(2048, KD, S), area(4096, KD, S)
        b_T = area(6144, 2, KD, P)
        c_z = area(8192, 3, S5_J, 32)
        cs = area(11264, 2, 4, 2, S)
        turn = area(15360, 2, 4, S)
        w_t1, w_t2 = area(17408, 2, 2, S), area(18432, 2, 2, S)
        w_in, w_sc = area(19456, 2, 2, S), area(20480, 2, 2, S)
        w_q1, w_q2 = area(21504, 2, 2, S), area(22528, 2, 2, S)
        s5v = area(23552, 12, S5_J)
        b_raw = area(11264, 2, S5_J, 16)
        c_raw = area(12288, 2, KD, P)
        bb = area(14336, 2, S5_J, 16)
        b_tmp = area(15360, 2, S5_J, 16)
        bbz = area(17408, 2, S5_J, 32)
        TWO_PI = 6.2831850

        def act_s5_loads():
            for n, name in enumerate(("s5_b_re_2", "s5_b_im_2")):
                for two in range(2):
                    act.dma_start(b_raw[64 * two:64 * two + 64, n, :, :],
                                            A[name][0].rearrange("(j two) p h -> two p j h", two=2)[two]).then_inc(s5_b, landed("s5_b", "s5 b loaded"))
            for n, name in enumerate(("s5_c_re_2", "s5_c_im_2")):
                for two in range(2):
                    act.dma_start(c_raw[:, n, :, 64 * two:64 * two + 64],
                                            A[name][0].rearrange("(m g) h p -> (g h) m p", g=8)).then_inc(s5_c, landed("s5_c", "s5 c loaded"))

        def pe_s5():
            n = "mid01"
            pe_pre(n)
            for c in range(4):
                w = chunk(f"s.in{c}", TE)
                pe_columns(f"s.u{c}", w, x_fm)
                release(f"s.in{c}")
            pe.wait_ge(s5_c, count_of("s5 c loaded"))
            for part in range(2):
                for m in range(0, KD, 4):
                    o = open_tile(f"s.c{part}{m}")
                    for q in range(4):
                        i = pe.transpose(o[:, 128 * q:128 * q + 128], c_raw[:, part, m + q, :], ident[:, :])
                    i.then_inc(pe_steps, TE.step(f"tile s.c{part}{m}"))
            pe.wait_ge(dve_steps, count_of("bbz"))
            for part in range(2):
                for m in range(0, KD, 4):
                    o = open_tile(f"s.b{part}{m}")
                    for q in range(4):
                        i = pe.transpose(o[:, 128 * q:128 * q + 128],
                                         bbz[:, part, 4 * (m + q):4 * (m + q) + 4, :].rearrange("p a b -> p (a b)"), ident[:, :])
                    i.then_inc(pe_steps, TE.step(f"tile s.b{part}{m}"))
            for part in range(2):
                for m in range(0, KD, 4):
                    pe.wait_ge(act_steps, count_of(f"read s.b{part}{m}"))
                    pe.wait_ge(dve_steps, count_of(f"read s.c{part}{m}"))
            for c in range(4):
                pe.wait_ge(act_steps, count_of(f"read s.u{c}"))

            def drive(j):
                o = open_tile(f"s.bu{j}")
                r = slice(32 * (j % 4), 32 * (j % 4) + 32)
                for part in range(2):
                    i = mm(o[:, S * part:S * part + S], b_T[r, part, j // 4, :], u_fm[r, j // 4, :], True, True)
                i.then_inc(pe_steps, TE.step(f"tile s.bu{j}"))

            pe.wait_ge(dve_steps, count_of("acc ffn00 read"))
            drive(0)
            drive(1)
            for j in range(S5_J):
                if j % 4 == 0:
                    if j >= 8:
                        pe.wait_ge(act_steps, count_of(f"read s.y{j // 4 - 2}"))
                o = acc[:, (j // 4) % 2, 0:S]
                r = slice(32 * (j % 4), 32 * (j % 4) + 32)
                pe.wait_ge(dve_steps, count_of(f"s.q1 {j}"))
                pe.wait_ge(pool_steps, count_of(f"s.q2 {j}"))
                for q, (sign, src) in enumerate(((0, w_q1[:, j % 2, 0, :]), (1, w_q1[:, j % 2, 1, :]),
                                                 (2, w_q2[:, j % 2, 0, :]), (2, w_q2[:, j % 2, 1, :]))):
                    i = mm(o[r, :], c_z[:, sign, j, :], src, q == 0, q == 3)
                i.then_inc(pe_steps, TE.step(f"s.y used {j}"))
                if j + 2 < S5_J:
                    drive(j + 2)
            for c in range(4):
                w = chunk(f"s.glu{c}", TE)
                if c == 0:
                    pe.wait_ge(act_steps, count_of("s5 y"))
                pe_columns(f"s.g{c}", w, y_fm)
                release(f"s.glu{c}")
            for c in range(4):
                pe.wait_ge(dve_steps, count_of(f"s.z{c}"))
            pe.wait_ge(act_steps, count_of("read s.y7"))
            pe_into_acc(n, [f"s.out{c}" for c in range(4)], lambda k: u_fm[:, k, :])

        def act_s5():
            n = "mid01"
            act.wait_ge(dve_steps, count_of("x mid01"))
            act_s5_loads()
            act_pre(n)
            for c in range(4):
                o = tile_of(AC, f"s.u{c}")
                act.copy(u_fm[:, 2 * c:2 * c + 2, :].rearrange("p a b -> p (a b)"), o).then_inc(act_steps, AC.step(f"read s.u{c}"))
            act.wait_ge(dve_steps, count_of("log dt"))
            act.activation(s5v[:, 0, :], col_s5[:, 64:96], ACT.Exp).then_inc(act_steps, AC.step("dt"))
            act.wait_ge(act_steps, AC.n)
            act.wait_ge(dve_steps, count_of("dt re"))
            act.activation(s5v[:, 1, :], s5v[:, 1, :], ACT.Exp).then_inc(act_steps, AC.step("mag"))
            act.wait_ge(dve_steps, count_of("angle"))
            act.activation(s5v[:, 4, :], s5v[:, 3, :], ACT.Sin, scale=TWO_PI).then_inc(act_steps, AC.step())
            act.activation(s5v[:, 5, :], s5v[:, 3, :], ACT.Sin, scale=TWO_PI / 2).then_inc(act_steps, AC.step("sines"))
            for part in range(2):
                for m in range(0, KD, 4):
                    o = tile_of(AC, f"s.b{part}{m}")
                    act.copy(b_T[:, part, m:m + 4, :].rearrange("p a b -> p (a b)"), o).then_inc(act_steps, AC.step(f"read s.b{part}{m}"))
            for q in range(8):
                act.wait_ge(pool_steps, count_of(f"turn {q}"))
                b = q % 2
                act.activation(cs[:, b, :, 1, :], turn[:, b, :, :], ACT.Sin, scale=TWO_PI / 2).then_inc(act_steps, AC.step())
                act.wait_ge(act_steps, AC.n)
                act.activation(cs[:, b, :, 1, :], cs[:, b, :, 1, :], ACT.Square).then_inc(act_steps, AC.step())
                act.wait_ge(act_steps, AC.n)
                act.activation(cs[:, b, :, 0, :], cs[:, b, :, 1, :], ACT.Copy, scale=-2.0, bias=1.0).then_inc(act_steps, AC.step())
                act.wait_ge(act_steps, AC.n)
                act.activation(cs[:, b, :, 1, :], turn[:, b, :, :], ACT.Sin, scale=TWO_PI).then_inc(act_steps, AC.step(f"cs {q}"))
                if q >= 1:
                    act_s5_y(q - 1)
            act_s5_y(7)
            for m in range(KD):
                act.wait_ge(dve_steps, count_of(f"y sum {m}"))
                act.activation(y_fm[:, m, :], y_fm[:, m, :], ACT.Gelu_apprx_tanh).then_inc(act_steps, AC.step("s5 y"))
            for c in range(4):
                o = tile_of(AC, f"s.g{c}")
                for k in range(2):
                    m = 2 * c + k
                    act.activation(u_fm[:, m, :], o[:, S * k:S * k + S], ACT.Sigmoid, bias=col[:, COL_GLU + m:COL_GLU + m + 1]).then_inc(act_steps, AC.step(f"read s.g{c}"))
            act.wait_ge(pe_steps, count_of("acc mid01"))
            act_post(n, acc_rows)

        def act_s5_y(m):
            act.wait_ge(pe_steps, count_of(f"s.y used {4 * m + 3}"))
            act.copy(y_fm[:, m, :], acc[:, m % 2, 0:S]).then_inc(act_steps, AC.step(f"read s.y{m}"))

        def pool_s5_turn(q):
            b = q % 2
            if q >= 2:
                pool.wait_ge(act_steps, count_of(f"cs {q - 2}"))
            pool.tensor_tensor(turn[:, b, :, :], s5v[:, 3, 4 * q:4 * q + 4].unsqueeze(2).to_broadcast([P, 4, S]),
                                      t_row[:, :].unsqueeze(1).to_broadcast([P, 4, S]), ALU.mult).then_inc(pool_steps, PO.step())
            pool.wait_ge(pool_steps, PO.n)
            pool.tensor_scalar(turn_r[:, :, :], turn[:, b, :, :], ROUND, None, ALU.add).then_inc(pool_steps, PO.step())
            pool.wait_ge(pool_steps, PO.n)
            pool.tensor_scalar(turn_r[:, :, :], turn_r[:, :, :], ROUND, None, ALU.subtract).then_inc(pool_steps, PO.step())
            pool.wait_ge(pool_steps, PO.n)
            pool.tensor_tensor(turn[:, b, :, :], turn[:, b, :, :], turn_r[:, :, :], ALU.subtract).then_inc(pool_steps, PO.step(f"turn {q}"))
            pool.wait_ge(pool_steps, PO.n)

        turn_r = area(24000, 4, S)

        def swapped(v):
            return bass.AP(v.tensor, v.offset + S, [list(v.ap[0]), [-S, 2], [1, S]])

        def pool_s5():
            pool.wait_ge(dve_steps, count_of("bbz"))
            pool_s5_turn(0)
            pool_s5_turn(1)
            for j in range(S5_J):
                b = j % 2
                pool.wait_ge(dve_steps, count_of(f"scan {j}"))
                if j >= 2:
                    pool.wait_ge(pe_steps, count_of(f"s.y used {j - 2}"))
                v = cs[:, (j // 4) % 2, j % 4, :, :]
                pool.tensor_tensor(w_q2[:, b, :, :], w_sc[:, b, :, :], swapped(v), ALU.mult).then_inc(pool_steps, PO.step(f"s.q2 {j}"))
                if j % 4 == 3 and j // 4 + 2 < 8:
                    pool_s5_turn(j // 4 + 2)

        def dve_s5():
            n = "mid01"
            dve_pre(n)
            re, im = col_s5[:, 0:32], col_s5[:, 32:64]
            V = lambda k: s5v[:, k, :]
            dve.tensor_copy(V(2), col_s5[:, 64:96]).then_inc(dve_steps, VE.step("log dt"))
            dve.wait_ge(act_steps, count_of("dt"))
            dve.tensor_tensor(V(1), V(0), re, ALU.mult).then_inc(dve_steps, VE.step("dt re"))
            dve.tensor_tensor(V(3), V(0), im, ALU.mult).then_inc(dve_steps, VE.step())
            dve.wait_ge(dve_steps, VE.n)
            dve.tensor_scalar(V(3), V(3), 1.0 / (2.0 * np.pi), None, ALU.mult).then_inc(dve_steps, VE.step())
            dve.wait_ge(dve_steps, VE.n)
            dve.tensor_scalar(V(2), V(3), ROUND, None, ALU.add).then_inc(dve_steps, VE.step())
            dve.wait_ge(dve_steps, VE.n)
            dve.tensor_scalar(V(2), V(2), ROUND, None, ALU.subtract).then_inc(dve_steps, VE.step())
            dve.wait_ge(dve_steps, VE.n)
            dve.tensor_tensor(V(3), V(3), V(2), ALU.subtract).then_inc(dve_steps, VE.step("angle"))
            dve.wait_ge(dve_steps, VE.n)
            dve.wait_ge(act_steps, count_of("sines"))
            dve.wait_ge(act_steps, count_of("mag"))
            dve.tensor_tensor(V(5), V(5), V(5), ALU.mult).then_inc(dve_steps, VE.step())
            dve.wait_ge(dve_steps, VE.n)
            dve.tensor_scalar(V(5), V(5), -2.0, 1.0, ALU.mult, ALU.add).then_inc(dve_steps, VE.step())
            dve.wait_ge(dve_steps, VE.n)
            dve.tensor_tensor(V(5), V(5), V(1), ALU.mult).then_inc(dve_steps, VE.step())
            dve.wait_ge(dve_steps, VE.n)
            dve.tensor_scalar(V(5), V(5), 1.0, None, ALU.subtract).then_inc(dve_steps, VE.step())
            dve.wait_ge(dve_steps, VE.n)
            dve.tensor_tensor(V(4), V(4), V(1), ALU.mult).then_inc(dve_steps, VE.step())
            dve.wait_ge(dve_steps, VE.n)
            dve.tensor_tensor(V(6), re, re, ALU.mult).then_inc(dve_steps, VE.step())
            dve.wait_ge(dve_steps, VE.n)
            dve.tensor_tensor(V(7), im, im, ALU.mult).then_inc(dve_steps, VE.step())
            dve.wait_ge(dve_steps, VE.n)
            dve.tensor_tensor(V(6), V(6), V(7), ALU.add).then_inc(dve_steps, VE.step())
            dve.wait_ge(dve_steps, VE.n)
            dve.reciprocal(V(6), V(6)).then_inc(dve_steps, VE.step())
            dve.wait_ge(dve_steps, VE.n)
            dve.tensor_tensor(V(7), V(5), re, ALU.mult).then_inc(dve_steps, VE.step())
            dve.wait_ge(dve_steps, VE.n)
            dve.tensor_tensor(V(8), V(4), im, ALU.mult).then_inc(dve_steps, VE.step())
            dve.wait_ge(dve_steps, VE.n)
            dve.tensor_tensor(V(7), V(7), V(8), ALU.add).then_inc(dve_steps, VE.step())
            dve.wait_ge(dve_steps, VE.n)
            dve.tensor_tensor(V(7), V(7), V(6), ALU.mult).then_inc(dve_steps, VE.step())
            dve.wait_ge(dve_steps, VE.n)
            dve.tensor_tensor(V(8), V(4), re, ALU.mult).then_inc(dve_steps, VE.step())
            dve.wait_ge(dve_steps, VE.n)
            dve.tensor_tensor(V(9), V(5), im, ALU.mult).then_inc(dve_steps, VE.step())
            dve.wait_ge(dve_steps, VE.n)
            dve.tensor_tensor(V(8), V(8), V(9), ALU.subtract).then_inc(dve_steps, VE.step())
            dve.wait_ge(dve_steps, VE.n)
            dve.tensor_tensor(V(8), V(8), V(6), ALU.mult).then_inc(dve_steps, VE.step())
            dve.wait_ge(dve_steps, VE.n)
            fr, fi_ = (V(k).unsqueeze(2).to_broadcast([P, S5_J, 16]) for k in (7, 8))
            dve.wait_ge(s5_b, count_of("s5 b loaded"))
            dve.tensor_tensor(bb[:, 0, :, :], b_raw[:, 0, :, :], fr, ALU.mult).then_inc(dve_steps, VE.step())
            dve.tensor_tensor(b_tmp[:, 0, :, :], b_raw[:, 1, :, :], fi_, ALU.mult).then_inc(dve_steps, VE.step())
            dve.tensor_tensor(bb[:, 1, :, :], b_raw[:, 1, :, :], fr, ALU.mult).then_inc(dve_steps, VE.step())
            dve.tensor_tensor(b_tmp[:, 1, :, :], b_raw[:, 0, :, :], fi_, ALU.mult).then_inc(dve_steps, VE.step())
            dve.wait_ge(dve_steps, VE.n)
            dve.tensor_tensor(bb[:, 0, :, :], bb[:, 0, :, :], b_tmp[:, 0, :, :], ALU.subtract).then_inc(dve_steps, VE.step())
            dve.tensor_tensor(bb[:, 1, :, :], bb[:, 1, :, :], b_tmp[:, 1, :, :], ALU.add).then_inc(dve_steps, VE.step())
            dve.wait_ge(dve_steps, VE.n)
            mk = mask32[:, :].rearrange("p (a b) -> p a b", a=2).unsqueeze(1).to_broadcast([P, S5_J, 2, 16])
            for part in range(2):
                dve.tensor_tensor(bbz[:, part, :, :].rearrange("p j (a b) -> p j a b", a=2),
                                          bb[:, part, :, :].unsqueeze(2).to_broadcast([P, S5_J, 2, 16]), mk, ALU.mult).then_inc(dve_steps, VE.step("bbz"))
            mk = mask32[:, :].unsqueeze(1).to_broadcast([P, 16, 32])
            for part in range(2):
                for m in range(0, KD, 4):
                    o = tile_of(VE, f"s.c{part}{m}").rearrange("p (a b) -> p a b", a=16)
                    js = slice(4 * m, 4 * m + 16)
                    if part == 0:
                        dve.tensor_tensor(c_z[:, 0, js, :], o, mk, ALU.mult).then_inc(dve_steps, VE.step())
                        dve.wait_ge(dve_steps, VE.n)
                        dve.tensor_scalar(c_z[:, 1, js, :], c_z[:, 0, js, :], -1.0, None, ALU.mult).then_inc(dve_steps, VE.step())
                    else:
                        dve.scalar_tensor_tensor(c_z[:, 2, js, :], o, -1.0, mk, ALU.mult, ALU.mult).then_inc(dve_steps, VE.step())
                    found[f"read s.c{part}{m}"] = (VE.who, VE.n)
            dve.wait_ge(dve_steps, VE.n)
            for part in range(2):
                for m in range(0, KD, 4):
                    dve.wait_ge(act_steps, count_of(f"read s.b{part}{m}"))
            for j in range(S5_J + 1):
                if j < S5_J:
                    b = j % 2
                    if j % 4 == 0:
                        dve.wait_ge(act_steps, count_of(f"cs {j // 4}"))
                    v = cs[:, (j // 4) % 2, j % 4, :, :]
                    o = tile_of(VE, f"s.bu{j}").rearrange("p (a b) -> p a b", a=2)
                    dve.tensor_tensor(w_t1[:, b, :, :], o, v, ALU.mult).then_inc(dve_steps, VE.step())
                    dve.tensor_tensor(w_t2[:, b, :, :], o, swapped(v), ALU.mult).then_inc(dve_steps, VE.step(f"read s.bu{j}"))
                    dve.wait_ge(dve_steps, VE.n)
                    dve.tensor_tensor(w_in[:, b, 0, :], w_t1[:, b, 0, :], w_t1[:, b, 1, :], ALU.add).then_inc(dve_steps, VE.step())
                    dve.tensor_tensor(w_in[:, b, 1, :], w_t2[:, b, 1, :], w_t2[:, b, 0, :], ALU.subtract).then_inc(dve_steps, VE.step())
                    dve.wait_ge(dve_steps, VE.n)
                    if j >= 2:
                        dve.wait_ge(pool_steps, count_of(f"s.q2 {j - 2}"))
                    m_ = s5v[:, 1, j:j + 1].to_broadcast([P, S])
                    for part in range(2):
                        dve.tensor_tensor_scan(w_sc[:, b, part, :], m_, w_in[:, b, part, :], 0.0, ALU.mult, ALU.add).then_inc(dve_steps, VE.step(f"scan {j}"))
                    dve.wait_ge(dve_steps, VE.n)
                    if j >= 2:
                        dve.wait_ge(pe_steps, count_of(f"s.y used {j - 2}"))
                    dve.tensor_tensor(w_q1[:, b, :, :], w_sc[:, b, :, :], v, ALU.mult).then_inc(dve_steps, VE.step(f"s.q1 {j}"))
            for m in range(KD):
                dve.wait_ge(act_steps, count_of(f"read s.y{m}"))
                dve.scalar_tensor_tensor(y_fm[:, m, :], u_fm[:, m, :], col[:, COL_D + m:COL_D + m + 1], y_fm[:, m, :],
                                                 ALU.mult, ALU.add).then_inc(dve_steps, VE.step(f"y sum {m}"))
            for c in range(4):
                dve.wait_ge(act_steps, count_of(f"read s.g{c}"))
                dve.tensor_tensor(u_fm[:, 2 * c:2 * c + 2, :], u_fm[:, 2 * c:2 * c + 2, :], y_fm[:, 2 * c:2 * c + 2, :], ALU.mult).then_inc(dve_steps, VE.step(f"s.z{c}"))
            dve_post(n, acc_rows, 1.0, tmp_s5, "ffn02")

        tmp_s5 = area(11264, TT, D)

        CP = CV_TAPS - 1
        z_pad = area(2048, KD, S + CP)
        c_acc = area(4352, KD, S)
        c_sg = area(6400, 2, S)
        c_sq = area(6912, KD, S)
        c_mean, c_rstd = area(8960, S), area(9216, S)
        ones_d = area(9472, P)
        tmp_c = area(9600, TT, D)

        def pe_conv():
            n = "mid11"
            pe_pre(n)
            for c in range(4):
                wa, wg = chunk(f"c.a{c}", TE), chunk(f"c.g{c}", TE)
                for f in range(2):
                    o = open_tile(f"c.{2 * c + f}")
                    for half, w in ((0, wa), (1, wg)):
                        for k in range(KD):
                            i = mm(o[:, S * half:S * half + S], w[:, k, P * f:P * f + P], x_fm[:, k, :], k == 0, k == KD - 1)
                    i.then_inc(pe_steps, TE.step(f"tile c.{2 * c + f}"))
                release(f"c.a{c}")
                release(f"c.g{c}")
            for name, src in (("mean", c_acc), ("var", c_sq)):
                pe.wait_ge(*by(f"{name} terms"))
                o = open_tile(f"c.{name}")
                for k in range(KD):
                    i = mm(o[:, 0:S], ones_d, src[:, k, :], k == 0, k == KD - 1)
                i.then_inc(pe_steps, TE.step(f"tile c.{name}"))
            pe.wait_ge(act_steps, count_of("c silu"))
            pe.wait_ge(dve_steps, count_of("acc ffn10 read"))
            pe_into_acc(n, [f"c.out{c}" for c in range(4)], lambda k: c_acc[:, k, :])

        def act_conv():
            n = "mid11"
            act_pre(n)
            for f in range(KD):
                o = tile_of(AC, f"c.{f}")
                if f >= 2:
                    act.wait_ge(dve_steps, count_of(f"read c.{f - 2}"))
                act.activation(c_sg[:, f % 2, :], o[:, S:2 * S], ACT.Sigmoid, bias=col[:, COL_BIN + 8 + f:COL_BIN + 9 + f]).then_inc(act_steps, AC.step(f"sg {f}"))
            act.wait_ge(dve_steps, count_of("centred"))
            act.activation(c_sq, c_acc, ACT.Square).then_inc(act_steps, AC.step("var terms"))
            act.wait_ge(dve_steps, count_of("var c"))
            act.sqrt(c_rstd, c_rstd).then_inc(act_steps, AC.step("std c"))
            act.wait_ge(dve_steps, count_of("normed c"))
            for k in range(KD):
                act.activation(c_acc[:, k, :], c_acc[:, k, :], ACT.Silu, bias=col[:, COL_LNB + k:COL_LNB + k + 1],
                                       scale=col[:, COL_LNG + k:COL_LNG + k + 1]).then_inc(act_steps, AC.step("c silu"))
            act.wait_ge(dve_steps, count_of("c out"))
            act_post(n, lambda t: tmp_c[:, t, :])

        def dve_conv():
            n = "mid11"
            dve_pre(n)
            dve.memset(z_pad[:, :, 0:CP], 0.0).then_inc(dve_steps, VE.step())
            dve.memset(ones_d, 1.0 / D).then_inc(dve_steps, VE.step())
            for f in range(KD):
                dve.wait_ge(act_steps, count_of(f"sg {f}"))
                o = tile_of(VE, f"c.{f}")
                dve.scalar_tensor_tensor(z_pad[:, f, CP:], o[:, 0:S], col[:, COL_BIN + f:COL_BIN + f + 1], c_sg[:, f % 2, :],
                                                ALU.add, ALU.mult).then_inc(dve_steps, VE.step(f"read c.{f}"))
                dve.wait_ge(dve_steps, VE.n)
                for k in range(CV_TAPS):
                    at = 8 * k + f
                    w = col_dw[:, at // 124, at % 124:at % 124 + 1]
                    if k == 0:
                        dve.tensor_scalar(c_acc[:, f, :], z_pad[:, f, 0:S], w, col[:, COL_DWB + f:COL_DWB + f + 1], ALU.mult, ALU.add).then_inc(dve_steps, VE.step())
                        dve.wait_ge(dve_steps, VE.n)
                    else:
                        dve.scalar_tensor_tensor(c_acc[:, f, :], z_pad[:, f, k:k + S], w, c_acc[:, f, :], ALU.mult, ALU.add).then_inc(dve_steps, VE.step("mean terms"))
                        dve.wait_ge(dve_steps, VE.n)
            o = tile_of(VE, "c.mean")
            dve.tensor_copy(c_mean, o[:, 0:S]).then_inc(dve_steps, VE.step("read c.mean"))
            dve.wait_ge(dve_steps, VE.n)
            dve.tensor_tensor(c_acc, c_acc, c_mean.unsqueeze(1).to_broadcast([P, KD, S]), ALU.subtract).then_inc(dve_steps, VE.step("centred"))
            dve.wait_ge(dve_steps, VE.n)
            o = tile_of(VE, "c.var")
            dve.tensor_scalar(c_rstd, o[:, 0:S], RMS_EPS, None, ALU.add).then_inc(dve_steps, VE.step("read c.var"))
            dve.wait_ge(dve_steps, VE.n)
            found["var c"] = (VE.who, VE.n)
            dve.wait_ge(act_steps, count_of("std c"))
            dve.reciprocal(c_rstd, c_rstd).then_inc(dve_steps, VE.step())
            dve.wait_ge(dve_steps, VE.n)
            dve.tensor_tensor(c_acc, c_acc, c_rstd.unsqueeze(1).to_broadcast([P, KD, S]), ALU.mult).then_inc(dve_steps, VE.step("normed c"))
            dve.wait_ge(dve_steps, VE.n)
            dve.wait_ge(pe_steps, count_of("acc mid11"))
            g = row("cvbout", VE)
            for t in range(TT):
                dve.tensor_tensor(tmp_c[:, t, :], acc_rows(t), g, ALU.add).then_inc(dve_steps, VE.step("c out"))
            dve.wait_ge(dve_steps, VE.n)
            found["row cvbout"] = (VE.who, VE.n)
            dve_post(n, lambda t: tmp_c[:, t, :], 1.0, tmp_c, "ffn12")

        def pool_rows(a, b):
            plan = row_plan(A)
            for i in range(a, b):
                name, src = plan[i]
                if i >= ROWS:
                    pool.wait_ge(dve_steps, count_of("row " + plan[i - ROWS][0]))
                w = src.shape[0]
                pool.dma_start(rowb[:, i % ROWS, 0:w], src.partition_broadcast(P)).then_inc(sems[f"rows{i % ROWS}"], landed(f"rows{i % ROWS}", f"row loaded {name}"))

        @block.tensor
        def _(_):
            pe_setup()
            pe_memory()
            pe_mlstm()
            for i in range(DEPTH):
                pe.wait_ge(dve_steps, count_of(f"x mix{i}"))
                pe_transposes(f"xp{i}t", x_tile)
                pe_peer(i)
                if i == 0:
                    pe.wait_ge(dve_steps, count_of("x peer0"))
                    pe_transposes("xrt", x_tile)
                    pe_rglru()
            pe_ffn(0, 0, "peer1")
            pe_s5()
            pe_ffn(0, 2, "mid01")
            pe_ffn(1, 0, "ffn02")
            pe_conv()
            pe_ffn(1, 2, "mid11")

        @block.scalar
        def _(_):
            act_param_loads()
            x_transposed("x0", AC, x_fm)
            x_transposed("mem", AC, mem_fm)
            act_memory()
            for i in range(DEPTH):
                if i == 0:
                    act_mlstm()
                else:
                    x_transposed("xrt", AC, x_fm)
                    act_rglru()
                act_sqrt(f"mix{i}", stat[:, 28:30])
                x_transposed(f"xp{i}t", AC, x_fm)
                act_peer(i)
                act_sqrt(f"peer{i}", stat[:, 28:30])
            act_ffn(0, 0)
            act_s5()
            act_ffn(0, 2)
            act_ffn(1, 0)
            act_conv()
            act_ffn(1, 2)

        @block.vector
        def _(_):
            x_transposed("x0", VE, x_fm)
            x_transposed("mem", VE, mem_fm)
            dve_setup()
            for i in range(DEPTH):
                if i == 0:
                    dve_mlstm()
                else:
                    x_transposed("xrt", VE, x_fm)
                    dve_rglru()
                x_transposed(f"xp{i}t", VE, x_fm)
                dve_peer(i)
            dve_ffn(0, 0, "mid01")
            dve_s5()
            dve_ffn(0, 2, "ffn10")
            dve_ffn(1, 0, "mid11")
            dve_conv()
            dve_ffn(1, 2, "end")

        @block.gpsimd
        def _(_):
            pool_setup()
            pool_rows(0, 4)
            pool_mlstm()
            pool_rows(4, 5)
            pool_peer(0)
            pool_rows(5, 9)
            pool_peer(1)
            pool_rows(9, 12)
            pool_s5()
            pool_rows(12, 16)

        @block.sync
        def _(sync):
            sp_inputs()
            sp_weights()
            sync.wait_ge(dve_steps, count_of("x end"))
            for t in range(TT):
                sync.dma_start(out[0, P * t:P * t + P, :], x_tok[:, t, :]).then_inc(stored, landed("stored", "stored"))
            sync.wait_ge(stored, 16 * TT)
    return found


_INS = ["x", "mem", "mlstm_w_in", "mlstm_b_gates", "mlstm_norm_g", "rglru_w_in", "rglru_conv_w", "rglru_conv_b", "rglru_w_a",
        "rglru_b_a", "rglru_w_x", "rglru_b_x", "rglru_lam", "xattn_w_kv", "w_out", "ln1_g", "ln1_b", "peer_w_q", "peer_subkeys",
        "peer_u", "peer_v", "ln2_g", "ln2_b", "norm_pre_2", "norm_post_2", "ffn_w1_2", "ffn_w3_2", "ffn_w2_2", "s5_w_in_2",
        "s5_a_re_2", "s5_a_im_2", "s5_log_dt_2", "s5_b_re_2", "s5_b_im_2", "s5_c_re_2", "s5_c_im_2", "s5_d_2", "s5_w_glu_2",
        "s5_b_glu_2", "s5_w_out_2", "cv_w_in_2", "cv_b_in_2", "cv_dw_2", "cv_dw_b_2", "cv_ln_g_2", "cv_ln_b_2", "cv_w_out_2",
        "cv_b_out_2"]


def kernel(**inputs):
    import concourse.bacc as bacc
    from concourse.bass_utils import run_bass_kernel_spmd

    def program(known):
        nc = bacc.Bacc("TRN2", target_bir_lowering=False, num_devices=1)
        A = {n: nc.dram_tensor(f"in_{n}", inputs[n].shape, F32, kind="ExternalInput").ap() for n in _INS}
        out = nc.dram_tensor("out", (1, S, D), F32, kind="ExternalOutput").ap()
        return nc, build(nc, A, out, known)

    _, counts = program(None)
    nc, again = program(counts)
    assert counts == again
    arrays = {f"in_{n}": np.ascontiguousarray(inputs[n]) for n in _INS}
    return run_bass_kernel_spmd(nc, [arrays], core_ids=[0]).results[0]["out"]
```

```python
from contextlib import ExitStack

import numpy as np

import concourse.bass as bass
from concourse import mybir

ACT = mybir.ActivationFunctionType
ALU = mybir.AluOpType
AX = mybir.AxisListType.X
F32 = mybir.dt.float32
F32R = mybir.dt.float32r
U32 = mybir.dt.uint32

P = 128
S = 256
TT = S // P
D = 1024
KD = D // P
DEPTH = 2
ALPHA = (2 * DEPTH) ** 0.25
LN_EPS = 1e-5
RMS_EPS = 1e-6
ML_HEADS, ML_DH = 4, 192
ML_W = ML_HEADS * ML_DH
ML_K = ML_W // P
RG_B, RG_D = 8, 96
RG_CONV = 4
RG_C = 8.0
XA_HEADS, XA_DH = 4, 64
XA_W = XA_HEADS * XA_DH
PR_HEADS, PR_K = 8, 16
PR_KEYS = 128
FF = 2816
FF_T = FF // P
S5_J = 32
CV_TAPS = 31
NEG = -3.0e38
ROUND = 12582912.0

RING, SLOT = 6, 2112
BANKS = 4
HI_SLOTS = 4
U_SLOTS = V_SLOTS = 8
ARENA = 26000


class Steps:

    def __init__(self, who, found):
        self.who, self.found, self.n = who, found, 0

    def step(self, label=None):
        self.n += 1
        if label is not None:
            self.found[label] = (self.who, self.n)
        return 1


def weight_plan(A):
    plan = []

    def columns(name, w, c0, n, p=P):
        plan.append((name, w.rearrange("(k p) n -> p k n", p=p)[:, :, c0:c0 + n], p, w.shape[0] // p, n))

    def rows(name, w, r0, k, p=P):
        plan.append((name, w[r0:r0 + k * p, :].rearrange("(k p) n -> p k n", p=p), p, k, w.shape[1]))

    def mix_out(i, p_main, k_main):
        w = A["w_out"][i]
        for c in range(k_main // 2):
            rows(f"wout{i}.{c}", w, 2 * c * p_main, 2, p_main)
        rows(f"wout{i}.x", w, k_main * p_main, 2)

    def peer(i):
        for c in range(8):
            columns(f"wq{i}.{c}", A["peer_w_q"][i], 256 * c, 256)

    def ffn(l, s):
        for c in range(FF_T // 2):
            columns(f"w1.{l}{s}.{c}", A["ffn_w1_2"][l, s // 2], 256 * c, 256)
            columns(f"w3.{l}{s}.{c}", A["ffn_w3_2"][l, s // 2], 256 * c, 256)
        for c in range(FF_T // 2):
            rows(f"w2.{l}{s}.{c}", A["ffn_w2_2"][l, s // 2], 256 * c, 2)

    for i in range(DEPTH):
        for c in range(2):
            columns(f"wkv{i}.{c}", A["xattn_w_kv"][i], 256 * c, 256)
    w = A["mlstm_w_in"][0]
    columns("m.gx", w, 4 * ML_W, 2 * ML_HEADS + XA_W)
    for c in range(12):
        columns(f"m.{c}", w, 256 * c, 256)
    mix_out(0, P, ML_K)
    peer(0)
    w = A["rglru_w_in"][0]
    for c in range(4):
        columns(f"r.x{c}", w, RG_B * RG_D + 192 * c, 192)
    plan.append(("r.a", A["rglru_w_a"][0].rearrange("g i j -> i g j"), RG_D, RG_B, RG_D))
    plan.append(("r.i", A["rglru_w_x"][0].rearrange("g i j -> i g j"), RG_D, RG_B, RG_D))
    columns("r.q", w, 2 * RG_B * RG_D, 256)
    for c in range(4):
        columns(f"r.g{c}", w, 192 * c, 192)
    mix_out(1, RG_D, RG_B)
    peer(1)
    for l in range(DEPTH):
        ffn(l, 0)
        if l == 0:
            for c in range(4):
                columns(f"s.in{c}", A["s5_w_in_2"][0], 256 * c, 256)
            for c in range(4):
                columns(f"s.glu{c}", A["s5_w_glu_2"][0], 256 * c, 256)
            for c in range(4):
                rows(f"s.out{c}", A["s5_w_out_2"][0], 256 * c, 2)
        else:
            for c in range(4):
                columns(f"c.a{c}", A["cv_w_in_2"][0], 256 * c, 256)
                columns(f"c.g{c}", A["cv_w_in_2"][0], D + 256 * c, 256)
            for c in range(4):
                rows(f"c.out{c}", A["cv_w_out_2"][0], 256 * c, 2)
        ffn(l, 2)
    return plan


def row_plan(A):
    g = [("mnorm", A["mlstm_norm_g"][0])]
    for i in range(DEPTH):
        g += [(f"ln1g{i}", A["ln1_g"][i]), (f"ln1b{i}", A["ln1_b"][i]), (f"ln2g{i}", A["ln2_g"][i]), (f"ln2b{i}", A["ln2_b"][i])]
    for l in range(DEPTH):
        g += [(f"post{l}0", A["norm_post_2"][l, 0])]
        if l == 1:
            g += [("cvbout", A["cv_b_out_2"][0])]
        g += [(f"post{l}1", A["norm_post_2"][l, 1]), (f"post{l}2", A["norm_post_2"][l, 2])]
    return g


ROWS = 4

COL_PRE, COL_D, COL_GLU, COL_BIN, COL_DWB, COL_LNG, COL_LNB = 0, 48, 56, 64, 80, 88, 96
COL_ROWS = 104
RG_CB, RG_BA, RG_BX, RG_LAM = 32, 40, 48, 56


def build(nc, A, out, known):
    found = {}
    chunks = weight_plan(A)
    chunk_at = {c[0]: i for i, c in enumerate(chunks)}
    rows_at = {r[0]: i for i, r in enumerate(row_plan(A))}
    ctx = ExitStack()
    with ctx:
        base = {}

        def sb(name, shape, dt=F32):
            base[name] = -(-nc.sbuf_base // 32) * 32
            return ctx.enter_context(nc.sbuf_tensor(name, shape, dt))

        def over(name, which, at, *shape):
            return nc.alloc_sbuf_tensor_at(name, [P, *shape], F32R, offset=base[which] + 4 * at)

        names = (["pe_steps", "act_steps", "dve_steps", "pool_steps", "params", "tokens", "memory", "stored"]
                 + [f"weights{i}" for i in range(RING)] + [f"rows{i}" for i in range(ROWS)]
                 + [f"u_rows{i}" for i in range(U_SLOTS)] + [f"v_rows{i}" for i in range(V_SLOTS)]
                 + ["s5_b", "s5_c"])
        sems = {n: ctx.enter_context(nc.semaphore(n)) for n in names}
        pe_steps, act_steps, dve_steps, pool_steps, params, tokens, memory, stored, s5_b, s5_c = (
            sems[n] for n in ("pe_steps", "act_steps", "dve_steps", "pool_steps", "params", "tokens", "memory", "stored", "s5_b", "s5_c"))

        def by(label):
            who, n = known[label] if known is not None else ("pe_steps", 1)
            return sems[who], n

        def count_of(label):
            return by(label)[1]

        def landed(name, label):
            n = found.get(("count", name), 0) + 16
            found[("count", name)] = n
            found[label] = (name, n)
            return 16

        ring = sb("ring", [P, RING, SLOT])
        x_tok = sb("x_tok", [P, TT, D])
        x_fm = sb("x_fm", [P, KD, S])
        mix_fm = sb("mix_fm", [P, RG_B + 2, S])
        rowb = sb("rowb", [P, ROWS, D])
        k_mem = sb("k_mem", [P, DEPTH, 2, S])
        v_mem = sb("v_mem", [P, DEPTH, TT, XA_W])
        ident = sb("ident", [P, P])
        col = sb("col", [P, COL_ROWS])
        col_dw = sb("col_dw", [P, 2, 124])
        col_rg = sb("col_rg", [RG_D, 64])
        col_s5 = sb("col_s5", [P, 96])
        skT = sb("skT", [P, 2 * DEPTH, PR_KEYS])
        mask32 = sb("mask32", [P, 32])
        iota16 = sb("iota16", [P, PR_K])
        stat = sb("stat", [P, 64])
        arena = sb("arena", [P, ARENA])
        ps = ctx.enter_context(nc.psum_tensor("ps", [P, BANKS, 512], F32))
        acc = ctx.enter_context(nc.psum_tensor("acc", [P, 2 * TT, 512], F32))

        def area(at, *shape):
            n = int(np.prod(shape))
            assert at + n <= ARENA, (at, shape)
            v = arena[:, at:at + n]
            if len(shape) == 2:
                v = v.rearrange("p (a b) -> p a b", b=shape[1])
            elif len(shape) == 3:
                v = v.rearrange("p (a b c) -> p a b c", b=shape[1], c=shape[2])
            elif len(shape) == 4:
                v = v.rearrange("p (a b c d) -> p a b c d", b=shape[1], c=shape[2], d=shape[3])
            return v

        def x_tile(t, k):
            return x_tok[:, t, 128 * k:128 * k + 128]

        block = ctx.enter_context(nc.Block())
        TE = Steps("pe_steps", found)
        AC = Steps("act_steps", found)
        VE = Steps("dve_steps", found)
        PO = Steps("pool_steps", found)
        act, dve, pool, pe = nc.scalar, nc.vector, nc.gpsimd, nc.tensor
        engine_of = {"pe_steps": pe, "act_steps": act, "dve_steps": dve, "pool_steps": pool}

        tiles, tile_bank = [], {}

        def open_tile(name):
            i = len(tiles)
            if i >= BANKS:
                pe.wait_ge(*by("read " + tiles[i - BANKS]))
            tiles.append(name)
            tile_bank[name] = i % BANKS
            return ps[:, i % BANKS, :]

        def tile_of(e, name):
            engine_of[e.who].wait_ge(pe_steps, count_of("tile " + name))
            return ps[:, tile_bank[name], :]

        def chunk(name, e=None):
            i = chunk_at[name]
            _, _, p, k, n = chunks[i]
            if e is not None:
                engine_of[e.who].wait_ge(sems[f"weights{i % RING}"], 16 * (i // RING + 1))
            return ring[0:p, i % RING, 0:k * n].rearrange("p (k n) -> p k n", k=k)

        def mm(o, l, r, first, last):
            return pe.matmul(o, l, r, start=first, stop=last)

        hi_ring = over("hi_ring", "arena", ARENA - HI_SLOTS * SLOT, HI_SLOTS, SLOT)
        lo_ring = over("lo_ring", "ring", 0, RING, SLOT)
        split_chunks = [c[0] for c in chunks if c[0][:3] in ("w1.", "w2.", "w3.")]
        split_at = {name: i for i, name in enumerate(split_chunks)}

        def flat(name, store, slot):
            _, _, p, k, n = chunks[chunk_at[name]]
            return store[0:p, slot, 0:k * n]

        def parts(name):
            return flat(name, hi_ring, split_at[name] % HI_SLOTS), flat(name, lo_ring, chunk_at[name] % RING)

        def act_split(name):
            i, s = chunk_at[name], split_at[name]
            if s >= HI_SLOTS:
                act.wait_ge(pe_steps, count_of("used " + split_chunks[s - HI_SLOTS]))
            act.wait_ge(sems[f"weights{i % RING}"], 16 * (i // RING + 1))
            act.copy(parts(name)[0], flat(name, ring, i % RING)).then_inc(act_steps, AC.step("hi " + name))

        def dve_split(name):
            i = chunk_at[name]
            hi, lo = parts(name)
            dve.wait_ge(act_steps, count_of("hi " + name))
            dve.wait_ge(sems[f"weights{i % RING}"], 16 * (i // RING + 1))
            dve.tensor_tensor(lo, flat(name, ring, i % RING), hi.bitcast(F32), ALU.subtract).then_inc(dve_steps, VE.step("lo " + name))

        def split_chunk(name):
            pe.wait_ge(dve_steps, count_of("lo " + name))
            k = chunks[chunk_at[name]][3]
            return [v.rearrange("p (k n) -> p k n", k=k) for v in parts(name)]

        def mm3(o, left, right, first, last):
            mm(o, left[0], right[0], first, False)
            mm(o, left[0], right[1], False, False)
            return mm(o, left[1], right[0], False, last)

        def row(name, e):
            i = rows_at[name]
            engine_of[e.who].wait_ge(sems[f"rows{i % ROWS}"], 16 * (i // ROWS + 1))
            return rowb[:, i % ROWS, :]

        def pe_transposes(name, src, n_tiles=KD):
            for c in range(n_tiles // 2):
                o = open_tile(f"{name}.{c}")
                for k in range(2):
                    for t in range(TT):
                        i = pe.transpose(o[:, 256 * k + 128 * t:256 * k + 128 * t + 128],
                                         src(t, 2 * c + k), ident[:, :])
                i.then_inc(pe_steps, TE.step(f"tile {name}.{c}"))
            TE.found[f"{name} transposed"] = (TE.who, TE.n)

        def pe_columns(name, w, rhs, m=P, k_tiles=KD):
            o = open_tile(name)
            for half in range(2):
                for k in range(k_tiles):
                    i = mm(o[0:m, 256 * half:256 * half + 256], w[:, k, half * m:half * m + m], rhs[:, k, :],
                           k == 0, k == k_tiles - 1)
            i.then_inc(pe_steps, TE.step(f"tile {name}"))

        def pe_token_rows(name, w, lhs, n=256):
            o = open_tile(name)
            for t in range(TT):
                for k in range(KD):
                    i = mm(o[:, n * t:n * t + n], lhs[:, k, 128 * t:128 * t + 128], w[:, k, 0:n], k == 0, k == KD - 1)
            i.then_inc(pe_steps, TE.step(f"tile {name}"))

        def release(name):
            found[f"used {name}"] = (TE.who, TE.n)

        def pe_into_acc(name, names, lhs):
            n_all = sum(chunks[chunk_at[c]][3] for c in names)
            at = 0
            for c in names:
                w = chunk(c, TE)
                for k in range(w.shape[1]):
                    for t in range(TT):
                        for half in range(2):
                            left = lhs(at)
                            i = mm(acc[:, 2 * t + half, :], left[:, 128 * t:128 * t + 128],
                                   w[:, k, 512 * half:512 * half + 512], at == 0, at == n_all - 1)
                    at += 1
                i.then_inc(pe_steps, TE.step())
                release(c)
            found[f"acc {name}"] = (TE.who, TE.n)

        def pe_attention(i, q, p_of, pT_of, m0):
            pe.wait_ge(act_steps, count_of(f"xq{i} ready"))
            pe.wait_ge(act_steps, count_of(f"kv{i} ready"))
            for h in range(XA_HEADS):
                o = open_tile(f"xs{i}.{h}")
                r = slice(64 * (h % 2), 64 * (h % 2) + 64)
                for t in range(TT):
                    ins = mm(o[:, 256 * t:256 * t + 256], q[r, h // 2, 128 * t:128 * t + 128], k_mem[r, i, h // 2, :], True, True)
                ins.then_inc(pe_steps, TE.step(f"tile xs{i}.{h}"))
            for h in range(XA_HEADS):
                pe.wait_ge(dve_steps, count_of(f"xp{i}.{h}"))
                o = open_tile(f"xpT{i}.{h}")
                for m in range(2):
                    for t in range(TT):
                        ins = pe.transpose(o[:, 256 * m + 128 * t:256 * m + 128 * t + 128],
                                           p_of(h)[:, t, 128 * m:128 * m + 128], ident[:, :])
                ins.then_inc(pe_steps, TE.step(f"tile xpT{i}.{h}"))
            for pair in range(2):
                for h in (2 * pair, 2 * pair + 1):
                    pe.wait_ge(act_steps, count_of(f"xpT{i}.{h} ready"))
                o = open_tile(f"xo{i}.{pair}")
                for h in (2 * pair, 2 * pair + 1):
                    for m in range(2):
                        ins = mm(o[64 * (h % 2):64 * (h % 2) + 64, 0:256], v_mem[:, i, m, 64 * h:64 * h + 64],
                                 pT_of(h)[:, m, :], m == 0, m == 1)
                ins.then_inc(pe_steps, TE.step(f"tile xo{i}.{pair}"))

        def attention_softmax(i, p_of, pT_of, m0):
            for h in range(XA_HEADS):
                o = tile_of(VE, f"xs{i}.{h}").rearrange("p (t m) -> p t m", t=TT)
                mx = stat[:, 2 * h:2 * h + 2]
                dve.tensor_reduce(mx, o, AX, ALU.max).then_inc(dve_steps, VE.step())
                dve.wait_ge(dve_steps, VE.n)
                dve.tensor_scalar(mx, mx, -XA_DH ** -0.5, None, ALU.mult).then_inc(dve_steps, VE.step(f"xmax{i}.{h}"))
                dve.wait_ge(dve_steps, VE.n)
            for h in range(XA_HEADS):
                dve.wait_ge(act_steps, count_of(f"xexp{i}.{h}"))
                rs = stat[:, 8 + 2 * h:10 + 2 * h]
                dve.reciprocal(rs, rs).then_inc(dve_steps, VE.step())
                dve.wait_ge(dve_steps, VE.n)
                for t in range(TT):
                    dve.tensor_scalar(p_of(h)[:, t, :], p_of(h)[:, t, :], rs[:, t:t + 1], None, ALU.mult).then_inc(dve_steps, VE.step(f"xp{i}.{h}"))

        def act_attention(i, p_of, pT_of, m0):
            for h in range(XA_HEADS):
                act.wait_ge(dve_steps, count_of(f"xmax{i}.{h}"))
                o = tile_of(AC, f"xs{i}.{h}")
                for t in range(TT):
                    act.activation(p_of(h)[:, t, :], o[:, 256 * t:256 * t + 256], ACT.Exp,
                                           bias=stat[:, 2 * h + t:2 * h + t + 1], scale=XA_DH ** -0.5,
                                           accum_out=stat[:, 8 + 2 * h + t:9 + 2 * h + t]).then_inc(act_steps, AC.step(f"xexp{i}.{h}"))
                found[f"read xs{i}.{h}"] = (AC.who, AC.n)
            for h in range(XA_HEADS):
                o = tile_of(AC, f"xpT{i}.{h}")
                act.copy(pT_of(h).rearrange("p a b -> p (a b)"), o).then_inc(act_steps, AC.step(f"xpT{i}.{h} ready"))
                found[f"read xpT{i}.{h}"] = (AC.who, AC.n)
            for pair in range(2):
                o = tile_of(AC, f"xo{i}.{pair}")
                act.copy(mix_fm[:, m0 + pair, :], o[:, 0:256]).then_inc(act_steps, AC.step(f"read xo{i}.{pair}"))
            found[f"xa{i} ready"] = (AC.who, AC.n)

        x_hi, x_lo = over("x_hi", "x_fm", 0, KD, S), over("x_lo", "mix_fm", 0, KD, S)

        def dve_layer_norm(i, which, g, b):
            dve.wait_ge(pe_steps, count_of(f"acc {which}{i}"))
            for t in range(TT):
                dve.scalar_tensor_tensor(x_tok[:, t, :], x_tok[:, t, :], ALPHA,
                                                 acc[:, 2 * t:2 * t + 2, :].rearrange("p a b -> p (a b)"), ALU.mult, ALU.add).then_inc(dve_steps, VE.step())
            dve.wait_ge(dve_steps, VE.n)
            found[f"acc {which}{i} read"] = (VE.who, VE.n)
            bn, ag, rstd = stat[:, 0:24].rearrange("p (t a b) -> p t a b", t=2, a=2), stat[:, 24:28].rearrange("p (t b) -> p t b", t=2), stat[:, 28:30]
            for t in range(TT):
                for h in range(2):
                    dve.bn_stats(bn[:, t, h, :], x_tok[:, t, 512 * h:512 * h + 512]).then_inc(dve_steps, VE.step())
            dve.wait_ge(dve_steps, VE.n)
            for t in range(TT):
                dve.bn_aggr(ag[:, t, :], bn[:, t, :, :].rearrange("p a b -> p (a b)")).then_inc(dve_steps, VE.step())
            dve.wait_ge(dve_steps, VE.n)
            dve.tensor_scalar(rstd, ag[:, :, 1], LN_EPS, None, ALU.add).then_inc(dve_steps, VE.step(f"var {which}{i}"))
            gr, br = row(g, VE), row(b, VE)
            for t in range(TT):
                dve.scalar_tensor_tensor(x_tok[:, t, :], x_tok[:, t, :], ag[:, t, 0:1], gr, ALU.subtract, ALU.mult).then_inc(
                    dve_steps, VE.step(f"row {g}"))
            dve.wait_ge(dve_steps, VE.n)
            dve.wait_ge(act_steps, count_of(f"std {which}{i}"))
            dve.reciprocal(rstd, rstd).then_inc(dve_steps, VE.step())
            dve.wait_ge(dve_steps, VE.n)
            for t in range(TT):
                dve.scalar_tensor_tensor(x_tok[:, t, :], x_tok[:, t, :], rstd[:, t:t + 1], br, ALU.mult, ALU.add).then_inc(
                    dve_steps, VE.step(f"x {which}{i}.{t}"))
            dve.wait_ge(dve_steps, VE.n)
            found[f"row {b}"] = (VE.who, VE.n)
            found[f"x {which}{i}"] = (VE.who, VE.n)
            if which == "peer" and i == DEPTH - 1:
                for t in range(TT):
                    found[f"x ffn00.{t}"] = found[f"x {which}{i}.{t}"]

        def act_sqrt(name, v):
            act.sqrt(spare, spare).then_inc(act_steps, AC.step())
            act.wait_ge(dve_steps, count_of(f"var {name}"))
            act.sqrt(v, v).then_inc(act_steps, AC.step(f"std {name}"))

        def x_transposed(name, e, out_of, scale=None, func=None):
            for c in range(KD // 2):
                who = (AC, VE)[c % 2]
                if who is not e:
                    continue
                o = tile_of(e, f"{name}.{c}")
                if scale is None:
                    dst = out_of[:, 2 * c:2 * c + 2, :].rearrange("p a b -> p (a b)")
                    ins = act.copy(dst, o) if e is AC else dve.tensor_copy(dst, o)
                    ins.then_inc(sems[e.who], e.step(f"read {name}.{c}"))
                else:
                    for k in range(2):
                        dst, sc = out_of[:, 2 * c + k, :], scale[:, 2 * c + k:2 * c + k + 1]
                        if e is AC:
                            ins = act.activation(dst, o[:, 256 * k:256 * k + 256], ACT.Copy, scale=sc)
                        else:
                            ins = dve.tensor_scalar(dst, o[:, 256 * k:256 * k + 256], sc, None, ALU.mult)
                        ins.then_inc(sems[e.who], e.step(f"read {name}.{c}"))

        def wait_transposed(e, name):
            for c in range(KD // 2):
                engine_of[e.who].wait_ge(*by(f"read {name}.{c}"))

        st_a, st_b, st_r, st_s = area(0, 128), area(128, 2, 128), area(384, 96), area(480, 128)
        st_k = area(608, 2 * DEPTH, P)
        st_dt = area(1120, 2)
        mem_tok, mem_fm = area(2048, TT, D), area(4096, KD, S)

        def sp_inputs():
            nc.sync.dma_start(mem_tok, A["mem"][0].rearrange("(t p) d -> p t d", p=P)).then_inc(memory, landed("memory", "mem loaded"))

        def sp_weights():
            for i, (name, src, p, k, n) in enumerate(chunks):
                if i == 2:
                    nc.sync.dma_start(x_tok[:, :, :], A["x"][0].rearrange("(t p) d -> p t d", p=P)).then_inc(tokens, landed("tokens", "x loaded"))
                    nc.sync.wait_ge(memory, count_of("mem loaded"))
                if i >= RING:
                    nc.sync.wait_ge(pe_steps, count_of("used " + chunks[i - RING][0]))
                nc.sync.dma_start(ring[0:p, i % RING, 0:k * n].rearrange("p (k n) -> p k n", k=k), src).then_inc(sems[f"weights{i % RING}"], landed(f"weights{i % RING}", f"chunk {name}"))

        def act_param_loads():
            def two(ap):
                return ap.rearrange("a (k p) -> (a k) p", p=P)

            def vec(ap, p=P):
                return ap.rearrange("(k p) -> k p", p=p)

            loads = [
                (st_a[COL_PRE:COL_PRE + 48, :], A["norm_pre_2"].rearrange("l i (k p) -> (l i k) p", p=P)),
                (st_a[COL_D:COL_D + 8, :], vec(A["s5_d_2"][0])),
                (st_a[COL_GLU:COL_GLU + 8, :], vec(A["s5_b_glu_2"][0])),
                (st_a[COL_BIN:COL_BIN + 16, :], vec(A["cv_b_in_2"][0])),
                (st_a[COL_DWB:COL_DWB + 8, :], vec(A["cv_dw_b_2"][0])),
                (st_a[COL_LNG:COL_LNG + 8, :], vec(A["cv_ln_g_2"][0])),
                (st_a[COL_LNB:COL_LNB + 8, :], vec(A["cv_ln_b_2"][0])),
                (st_b[0:124, 0, :], two(A["cv_dw_2"][0])[0:124, :]),
                (st_b[0:124, 1, :], two(A["cv_dw_2"][0])[124:248, :]),
                (st_r[0:32, :], A["rglru_conv_w"][0].rearrange("a (k p) -> (a k) p", p=RG_D)),
                (st_r[RG_CB:RG_CB + 8, :], vec(A["rglru_conv_b"][0], RG_D)),
                (st_r[RG_BA:RG_BA + 8, :], vec(A["rglru_b_a"][0], RG_D)),
                (st_r[RG_BX:RG_BX + 8, :], vec(A["rglru_b_x"][0], RG_D)),
                (st_r[RG_LAM:RG_LAM + 8, :], vec(A["rglru_lam"][0], RG_D)),
                (st_s[0:32, :], A["s5_a_re_2"][0].rearrange("(j two) p -> j (two p)", two=2)),
                (st_s[32:64, :], A["s5_a_im_2"][0].rearrange("(j two) p -> j (two p)", two=2)),
                (st_dt[64:96, :], A["s5_log_dt_2"][0].rearrange("(j two) -> j two", two=2)),
                (st_k, A["peer_subkeys"].rearrange("l h k c -> k (l h) c")),
                (gate_b[0:ML_HEADS, 0:1], A["mlstm_b_gates"][0, 0:ML_HEADS].rearrange("(h a) -> h a", a=1)),
                (gate_b[0:ML_HEADS, 1:2], A["mlstm_b_gates"][0, ML_HEADS:].rearrange("(h a) -> h a", a=1)),
            ]
            for dst, src in loads:
                act.dma_start(dst, src).then_inc(params, landed("params", "params loaded"))

        gate_b = stat[:, 62:64]

        def pool_setup():
            pool.memset(ident[:, :], 0.0).then_inc(pool_steps, PO.step())
            pool.memset(mask32[:, :], 0.0).then_inc(pool_steps, PO.step())
            pool.iota(iota_i, [[1, S]], base=0, channel_multiplier=0).then_inc(pool_steps, PO.step("iota"))
            pool.wait_ge(pool_steps, PO.n)
            pool.affine_select(out=ident[:, :], in_=ident[:, :], compare_op=ALU.not_equal, fill=1.0, base=0,
                                      pattern=[[-1, P]], channel_multiplier=1).then_inc(pool_steps, PO.step("ident"))
            pool.wait_ge(pool_steps, PO.n)
            pool.memset(mask32[0:64, 0:16], 1.0).then_inc(pool_steps, PO.step())
            pool.memset(mask32[64:128, 16:32], 1.0).then_inc(pool_steps, PO.step("mask32"))
            pool.wait_ge(pool_steps, PO.n)

        iota_i = area(1200, S).bitcast(mybir.dt.int32)

        def dve_setup():
            dve.memset(spare, 1.0).then_inc(dve_steps, VE.step())
            dve.wait_ge(params, count_of("params loaded"))
            dve.tensor_copy(st_s[64:96, :].rearrange("j (two p) -> j two p", two=2),
                                   st_dt[64:96, :].unsqueeze(2).to_broadcast([32, 2, 64])).then_inc(dve_steps, VE.step("log_dt spread"))
            dve.wait_ge(dve_steps, VE.n)
            dve.wait_ge(pool_steps, count_of("iota"))
            dve.tensor_copy(iota16[:, :], iota_i[:, 0:PR_K]).then_inc(dve_steps, VE.step())
            dve.tensor_copy(t_row[:, :], iota_i).then_inc(dve_steps, VE.step("t_row"))
            o = tile_of(VE, "par")
            dve.tensor_copy(col[:, :], o[:, 0:COL_ROWS]).then_inc(dve_steps, VE.step())
            dve.tensor_copy(col_dw[:, :, :], o[:, 104:352].rearrange("p (a b) -> p a b", a=2)).then_inc(dve_steps, VE.step())
            dve.tensor_copy(col_s5[:, :], o[:, 352:448]).then_inc(dve_steps, VE.step())
            dve.tensor_copy(col_rg[:, :], o[0:RG_D, 448:512]).then_inc(dve_steps, VE.step("read par"))
            o = tile_of(VE, "sk")
            dve.tensor_copy(skT[:, :, :].rearrange("p a b -> p (a b)"), o).then_inc(dve_steps, VE.step("read sk"))
            dve.wait_ge(dve_steps, VE.n)

        t_row = sb("t_row", [P, S])

        def pe_setup():
            pe.wait_ge(pool_steps, count_of("ident"))
            pe.wait_ge(memory, count_of("mem loaded"))
            pe_transposes("mem", lambda t, k: mem_tok[:, t, 128 * k:128 * k + 128])

        def pe_params():
            pe.wait_ge(dve_steps, count_of("log_dt spread"))
            pe.wait_ge(params, count_of("params loaded"))
            o = open_tile("par")
            pe.transpose(o[:, 0:COL_ROWS], st_a[0:COL_ROWS, :], ident[0:COL_ROWS, 0:COL_ROWS])
            for h in range(2):
                pe.transpose(o[:, 104 + 124 * h:228 + 124 * h], st_b[0:124, h, :], ident[0:124, 0:124])
            pe.transpose(o[:, 352:448], st_s[0:96, :], ident[0:96, 0:96])
            pe.transpose(o[0:RG_D, 448:512], st_r[0:64, :], ident[0:64, 0:64]).then_inc(pe_steps, TE.step("tile par"))
            o = open_tile("sk")
            for n in range(4):
                i = pe.transpose(o[:, 128 * n:128 * n + 128], st_k[:, n, :], ident[:, :])
            i.then_inc(pe_steps, TE.step("tile sk"))

        def pe_memory():
            wait_transposed(TE, "mem")
            for i in range(DEPTH):
                w = chunk(f"wkv{i}.0", TE)
                pe_columns(f"kv{i}.k", w, mem_fm)
                release(f"wkv{i}.0")
                w = chunk(f"wkv{i}.1", TE)
                pe_token_rows(f"kv{i}.v", w, mem_fm)
                release(f"wkv{i}.1")

        def act_memory():
            for i in range(DEPTH):
                o = tile_of(AC, f"kv{i}.k")
                act.copy(k_mem[:, i, :, :].rearrange("p a b -> p (a b)"), o).then_inc(act_steps, AC.step(f"read kv{i}.k"))
                o = tile_of(AC, f"kv{i}.v")
                act.copy(v_mem[:, i, :, :].rearrange("p a b -> p (a b)"), o).then_inc(act_steps, AC.step(f"read kv{i}.v"))
                found[f"kv{i} ready"] = (AC.who, AC.n)

        q_fm, kk_fm = area(0, ML_K, S), area(1536, ML_K, S)
        v_tok = area(3072, TT, ML_HEADS, ML_DH + 1)
        o_sig = area(4620, TT, ML_W)
        g_if, g_b, g_a, g_g, g_e, g_1 = (area(6156, 2, S), area(6668, S), area(6924, S), area(7180, S), area(7436, S),
                                         area(7692, S))
        decay = area(7968, ML_HEADS, 384)
        sT = area(9504, ML_HEADS, 384)
        h_tok = area(11040, TT, ML_W)
        sel = area(12576, ML_HEADS, P)
        xq0, p0, pT0 = area(13088, 2, S), area(13600, XA_HEADS, TT, S), area(15648, XA_HEADS, 2, S)
        den = area(17696, ML_HEADS, TT)
        mbn, mag = area(17704, TT * ML_HEADS, 6), area(17760, TT * ML_HEADS, 2)
        mrs = area(17780, TT * ML_HEADS)
        HEAD_PARTS = [[(0, 0, 128), (1, 0, 64)], [(1, 64, 128), (2, 0, 128)], [(3, 0, 128), (4, 0, 64)], [(4, 64, 128), (5, 0, 128)]]

        def pe_mlstm():
            wait_transposed(TE, "x0")
            w = chunk("m.gx", TE)
            o = open_tile("m.gates")
            for half in range(2):
                for k in range(KD):
                    i = mm(o[0:4, 256 * half:256 * half + 256], w[:, k, 4 * half:4 * half + 4], x_fm[:, k, :], k == 0, k == KD - 1)
            i.then_inc(pe_steps, TE.step("tile m.gates"))
            pe_columns("m.xq", w[:, :, 8:264], x_fm)
            release("m.gx")
            for c in range(6):
                w = chunk(f"m.{c}", TE)
                pe_columns(f"m.{c}", w, x_fm)
                release(f"m.{c}")
            for c in range(6, 12):
                w = chunk(f"m.{c}", TE)
                pe_token_rows(f"m.{c}", w, x_fm)
                release(f"m.{c}")
            pe.wait_ge(act_steps, count_of("gates done"))
            o = open_tile("m.col")
            for n, src in enumerate((g_a, g_e)):
                for t in range(TT):
                    i = pe.transpose(o[:, 8 * n + 4 * t:8 * n + 4 * t + 4], src[0:4, 128 * t:128 * t + 128], ident[0:4, 0:4])
            i.then_inc(pe_steps, TE.step("tile m.col"))
            pe.wait_ge(act_steps, count_of("read m.5"))
            pe.wait_ge(dve_steps, count_of("read m.4"))
            for h in range(ML_HEADS):
                o = open_tile(f"m.G{h}")
                mm(o[:, 0:S], sel[0:4, h, :], g_g[0:4, :], True, True).then_inc(pe_steps, TE.step(f"tile m.G{h}"))
                o = open_tile(f"m.S{h}")
                parts = HEAD_PARTS[h]
                for n, (tile, a, b) in enumerate(parts):
                    mm(o[:, 0:S], kk_fm[a:b, tile, 0:P], q_fm[a:b, tile, :], n == 0, n == len(parts) - 1)
                for n, (tile, a, b) in enumerate(parts):
                    i = mm(o[:, S:S + P], kk_fm[a:b, tile, P:S], q_fm[a:b, tile, P:S], n == 0, n == len(parts) - 1)
                i.then_inc(pe_steps, TE.step(f"tile m.S{h}"))
            pe_attention(0, xq0, lambda h: p0[:, h, :, :], lambda h: pT0[:, h, :, :], ML_K)
            pe.wait_ge(dve_steps, count_of("read m.8"))
            for h in range(ML_HEADS):
                pe.wait_ge(dve_steps, count_of(f"sT{h}"))
                o = open_tile(f"m.N{h}")
                mm(o[:, 0:193], sT[:, h, 0:P], v_tok[:, 0, h, :], True, True)
                mm(o[:, 256:449], sT[:, h, P:S], v_tok[:, 0, h, :], True, False)
                mm(o[:, 256:449], sT[:, h, S:S + P], v_tok[:, 1, h, :], False, True).then_inc(pe_steps, TE.step(f"tile m.N{h}"))
            pe.wait_ge(dve_steps, count_of("y mlstm"))
            pe_transposes("my", lambda t, k: h_tok[:, t, 128 * k:128 * k + 128], ML_K)
            wait_transposed_n(TE, "my", ML_K)
            pe.wait_ge(act_steps, count_of("xa0 ready"))
            pe_into_acc("mix0", [f"wout0.{c}" for c in range(ML_K // 2)] + ["wout0.x"], lambda k: mix_fm[:, k, :])

        def wait_transposed_n(e, name, n):
            for c in range(n // 2):
                engine_of[e.who].wait_ge(act_steps, count_of(f"read {name}.{c}"))

        def act_mlstm():
            o = tile_of(AC, "m.xq")
            act.copy(xq0.rearrange("p a b -> p (a b)"), o).then_inc(act_steps, AC.step("read m.xq"))
            found["xq0 ready"] = (AC.who, AC.n)
            act.wait_ge(dve_steps, count_of("abs f"))
            act.activation(g_e[0:4, :], g_e[0:4, :], ACT.Exp, scale=-1.0).then_inc(act_steps, AC.step())
            act.wait_ge(act_steps, AC.n)
            act.activation(g_e[0:4, :], g_e[0:4, :], ACT.Ln, bias=1.0).then_inc(act_steps, AC.step("log1p"))
            act.wait_ge(act_steps, AC.n)
            for c in (1, 3, 5):
                o = tile_of(AC, f"m.{c}")
                dst = (q_fm if c < 3 else kk_fm)[:, 2 * (c % 3):2 * (c % 3) + 2, :]
                act.copy(dst.rearrange("p a b -> p (a b)"), o).then_inc(act_steps, AC.step(f"read m.{c}"))
            act.wait_ge(dve_steps, count_of("guard sum"))
            act.activation(g_e[0:4, :], g_e[0:4, :], ACT.Exp, scale=-1.0).then_inc(act_steps, AC.step("gates done"))
            act.wait_ge(act_steps, AC.n)
            for c in range(9, 12):
                o = tile_of(AC, f"m.{c}")
                act.activation(o_sig[:, :, 256 * (c - 9):256 * (c - 9) + 256], o.rearrange("p (t n) -> p t n", t=TT),
                                       ACT.Sigmoid).then_inc(act_steps, AC.step(f"read m.{c}"))
            for h in range(ML_HEADS):
                act.wait_ge(dve_steps, count_of(f"decay arg{h}"))
                act.activation(decay[:, h, :], decay[:, h, :], ACT.Exp).then_inc(act_steps, AC.step(f"decay exp{h}"))
            act_attention(0, lambda h: p0[:, h, :, :], lambda h: pT0[:, h, :, :], ML_K)
            act_sqrt("mhead", mrs)
            for c in range(ML_K // 2):
                o = tile_of(AC, f"my.{c}")
                act.copy(mix_fm[:, 2 * c:2 * c + 2, :].rearrange("p a b -> p (a b)"), o).then_inc(act_steps, AC.step(f"read my.{c}"))

        def pool_mlstm():
            for h in range(ML_HEADS):
                pool.wait_ge(act_steps, count_of(f"decay exp{h}"))
                for a in (0, S):
                    pool.affine_select(out=decay[:, h, a:a + P], in_=decay[:, h, a:a + P], compare_op=ALU.is_ge,
                                               fill=0.0, base=0, pattern=[[1, P]], channel_multiplier=-1).then_inc(pool_steps, PO.step(f"decay {h}"))

        def dve_mlstm():
            o = tile_of(VE, "m.gates")
            dve.tensor_scalar(g_if[0:4, 0, :], o[0:4, 0:S], gate_b[0:4, 0:1], None, ALU.add).then_inc(dve_steps, VE.step())
            dve.tensor_scalar(g_if[0:4, 1, :], o[0:4, S:2 * S], gate_b[0:4, 1:2], None, ALU.add).then_inc(dve_steps, VE.step("read m.gates"))
            dve.wait_ge(dve_steps, VE.n)
            dve.memset(g_1[0:4, :], 1.0).then_inc(dve_steps, VE.step())
            dve.memset(v_tok[:, :, :, ML_DH:ML_DH + 1], 1.0).then_inc(dve_steps, VE.step())
            dve.tensor_copy(sel[0:4, :, :], ident[0:4, 0:4].unsqueeze(2).to_broadcast([4, ML_HEADS, P])).then_inc(dve_steps, VE.step("sel"))
            dve.scalar_tensor_tensor(g_e[0:4, :], g_if[0:4, 1, :], -1.0, g_if[0:4, 1, :], ALU.mult, ALU.max).then_inc(dve_steps, VE.step("abs f"))
            dve.wait_ge(dve_steps, VE.n)
            for c in (0, 2, 4):
                o = tile_of(VE, f"m.{c}")
                dst = (q_fm if c < 3 else kk_fm)[:, 2 * (c % 3):2 * (c % 3) + 2, :]
                dve.tensor_copy(dst.rearrange("p a b -> p (a b)"), o).then_inc(dve_steps, VE.step(f"read m.{c}"))
            dve.wait_ge(act_steps, count_of("log1p"))
            dve.scalar_tensor_tensor(g_a[0:4, :], g_if[0:4, 1, :], 0.0, g_e[0:4, :], ALU.min, ALU.subtract).then_inc(dve_steps, VE.step())
            dve.wait_ge(dve_steps, VE.n)
            dve.tensor_tensor_scan(g_b[0:4, :], g_1[0:4, :], g_a[0:4, :], 0.0, ALU.mult, ALU.add).then_inc(dve_steps, VE.step())
            dve.wait_ge(dve_steps, VE.n)
            dve.tensor_tensor(g_a[0:4, :], g_if[0:4, 0, :], g_b[0:4, :], ALU.subtract).then_inc(dve_steps, VE.step())
            dve.wait_ge(dve_steps, VE.n)
            dve.tensor_tensor_scan(g_g[0:4, :], g_1[0:4, :], g_a[0:4, :], 0.0, ALU.mult, ALU.max).then_inc(dve_steps, VE.step())
            dve.wait_ge(dve_steps, VE.n)
            dve.tensor_tensor(g_e[0:4, :], g_b[0:4, :], g_g[0:4, :], ALU.add).then_inc(dve_steps, VE.step("guard sum"))
            dve.wait_ge(dve_steps, VE.n)
            dve.tensor_scalar(g_g[0:4, :], g_g[0:4, :], -1.0, None, ALU.mult).then_inc(dve_steps, VE.step("neg G"))
            dve.wait_ge(dve_steps, VE.n)
            for c in range(3):
                o = tile_of(VE, f"m.{6 + c}").rearrange("p (t n) -> p t n", t=TT)
                at = 256 * c
                while at < 256 * c + 256:
                    h, a = divmod(at, ML_DH)
                    n = min(ML_DH - a, 256 * c + 256 - at)
                    dve.tensor_copy(v_tok[:, :, h, a:a + n], o[:, :, at - 256 * c:at - 256 * c + n]).then_inc(dve_steps, VE.step(f"read m.{6 + c}"))
                    at += n
            o = tile_of(VE, "m.col")
            dve.tensor_copy(a_flat, o[:, 0:16]).then_inc(dve_steps, VE.step("read m.col"))
            dve.wait_ge(dve_steps, VE.n)
            for h in range(ML_HEADS):
                o = tile_of(VE, f"m.G{h}")
                dve.tensor_scalar(decay[:, h, 0:S], o[:, 0:S], a_flat[:, h:h + 1], 0.0, ALU.add, ALU.min).then_inc(dve_steps, VE.step())
                dve.tensor_scalar(decay[:, h, S:S + P], o[:, P:S], a_flat[:, 4 + h:5 + h], 0.0, ALU.add, ALU.min).then_inc(dve_steps, VE.step(f"read m.G{h}"))
                found[f"decay arg{h}"] = (VE.who, VE.n)
                if h:
                    dve_weights(h - 1)
            dve_weights(ML_HEADS - 1)
            attention_softmax(0, lambda h: p0[:, h, :, :], None, 0)
            for h in range(ML_HEADS):
                o = tile_of(VE, f"m.N{h}").rearrange("p (t n) -> p t n", t=TT)
                d = den[:, h, :]
                dve.tensor_copy(d.unsqueeze(2), o[:, :, ML_DH:ML_DH + 1]).then_inc(dve_steps, VE.step())
                dve.wait_ge(dve_steps, VE.n)
                dve.scalar_tensor_tensor(d, d, -1.0, d, ALU.mult, ALU.max).then_inc(dve_steps, VE.step())
                dve.wait_ge(dve_steps, VE.n)
                dve.tensor_tensor(d, d, a_flat[:, 8 + h:16:4], ALU.max).then_inc(dve_steps, VE.step())
                dve.wait_ge(dve_steps, VE.n)
                dve.reciprocal(d, d).then_inc(dve_steps, VE.step())
                dve.wait_ge(dve_steps, VE.n)
                for t in range(TT):
                    dve.tensor_scalar(h_tok[:, t, ML_DH * h:ML_DH * h + ML_DH], o[:, t, 0:ML_DH], d[:, t:t + 1], None, ALU.mult).then_inc(dve_steps, VE.step(f"read m.N{h}"))
            dve.wait_ge(dve_steps, VE.n)
            for t in range(TT):
                for h in range(ML_HEADS):
                    dve.bn_stats(mbn[:, 4 * t + h, :], h_tok[:, t, ML_DH * h:ML_DH * h + ML_DH]).then_inc(dve_steps, VE.step())
            dve.wait_ge(dve_steps, VE.n)
            for n in range(TT * ML_HEADS):
                dve.bn_aggr(mag[:, n, :], mbn[:, n, :]).then_inc(dve_steps, VE.step())
            dve.wait_ge(dve_steps, VE.n)
            dve.tensor_scalar(mrs, mag[:, :, 1], LN_EPS, None, ALU.add).then_inc(dve_steps, VE.step("var mhead"))
            dve.wait_ge(dve_steps, VE.n)
            dve.wait_ge(act_steps, count_of("std mhead"))
            dve.reciprocal(mrs, mrs).then_inc(dve_steps, VE.step())
            dve.wait_ge(dve_steps, VE.n)
            for t in range(TT):
                for h in range(ML_HEADS):
                    v, n = h_tok[:, t, ML_DH * h:ML_DH * h + ML_DH], 4 * t + h
                    dve.tensor_scalar(v, v, mag[:, n, 0:1], mrs[:, n:n + 1], ALU.subtract, ALU.mult).then_inc(dve_steps, VE.step())
            dve.wait_ge(dve_steps, VE.n)
            g = row("mnorm", VE)[:, 0:ML_W]
            for t in range(TT):
                dve.tensor_tensor(h_tok[:, t, :], h_tok[:, t, :], g, ALU.mult).then_inc(dve_steps, VE.step("row mnorm"))
            dve.wait_ge(dve_steps, VE.n)
            dve.wait_ge(act_steps, count_of("read m.11"))
            for t in range(TT):
                dve.tensor_tensor(h_tok[:, t, :], h_tok[:, t, :], o_sig[:, t, :], ALU.mult).then_inc(dve_steps, VE.step("y mlstm"))
            dve_layer_norm(0, "mix", "ln1g0", "ln1b0")

        a_flat = area(7948, 16)

        def dve_weights(h):
            dve.wait_ge(pool_steps, count_of(f"decay {h}"))
            o = tile_of(VE, f"m.S{h}")
            dve.scalar_tensor_tensor(sT[:, h, :], o[:, 0:384], ML_DH ** -0.5, decay[:, h, :], ALU.mult, ALU.mult).then_inc(dve_steps, VE.step(f"read m.S{h}"))
            found[f"sT{h}"] = (VE.who, VE.n)

        u_ring, v_ring = area(0, U_SLOTS, D), area(8192, V_SLOTS, D)
        qT = area(24000, 2, 2, S)
        sc = area(16384, TT, 2 * PR_HEADS * PR_KEYS)
        diag = area(20480, PR_K, P)

        def small(at, slots, *shape):
            n = int(np.prod(shape))
            return [area(at + n * s, *shape) for s in range(slots)]

        sv, si_u, si_f = small(22528, 2, 2, PR_K), small(22592, 2, 2, PR_K), small(22656, 2, 2, PR_K)
        cand, eq = small(22720, 1, PR_K, PR_K)[0], area(22976, 2 * PR_K, PR_K)
        fv, fi = small(23488, 2, PR_K), small(23520, 2, PR_K)
        ab_u, ab_f, ids = area(23552, 2, PR_K), area(23584, 2, PR_K), area(23616, 2, PR_K)
        ix = small(23648, 4, PR_K)
        ex, dots, gel, coef = small(23712, 2, PR_K), small(23744, 2, PR_K), small(23776, 2, PR_K), small(23808, 2, PR_K)
        nmx, sm = small(23840, 2, 1), small(23842, 2, 1)
        NJ = TT * PR_HEADS

        def pe_peer(i):
            wait_transposed(TE, f"xp{i}t")
            for h in range(PR_HEADS + 1):
                if h < PR_HEADS:
                    w = chunk(f"wq{i}.{h}", TE)
                    pe_columns(f"pq{i}.{h}", w, x_fm)
                    release(f"wq{i}.{h}")
                if h:
                    pe.wait_ge(act_steps, count_of(f"read pq{i}.{h - 1}"))
                    o = open_tile(f"ps{i}.{h - 1}")
                    for t in range(TT):
                        for half in range(2):
                            ins = mm(o[:, 256 * t + 128 * half:256 * t + 128 * half + 128], qT[:, (h - 1) % 2, half, 128 * t:128 * t + 128],
                                     skT[:, 2 * i + half, :], True, True)
                    ins.then_inc(pe_steps, TE.step(f"tile ps{i}.{h - 1}"))
            for j in range(NJ):
                t = j // PR_HEADS
                for k in range(PR_K):
                    g = PR_K * (NJ * i + j) + k
                    pe.wait_ge(act_steps, count_of(f"diag {i}.{j}.{k}"))
                    pe.wait_ge(sems[f"v_rows{g % V_SLOTS}"], 16 * (g // V_SLOTS + 1))
                    for half in range(2):
                        ins = mm(acc[:, 2 * t + half, :], diag[:, k, :], v_ring[:, g % V_SLOTS, 512 * half:512 * half + 512],
                                 j % PR_HEADS == 0 and k == 0, j % PR_HEADS == PR_HEADS - 1 and k == PR_K - 1)
                    ins.then_inc(pe_steps, TE.step(f"v used {g}"))
            found[f"acc peer{i}"] = (TE.who, TE.n)

        def act_peer(i):
            def numerators(j):
                b = j % 2
                act.wait_ge(dve_steps, count_of(f"nmax {i}.{j}"))
                act.activation(ex[b], fv[b], ACT.Exp, bias=nmx[b], accum_out=sm[b]).then_inc(act_steps, AC.step(f"ex {i}.{j}"))

            for h in range(PR_HEADS + 1):
                if h < PR_HEADS:
                    o = tile_of(AC, f"pq{i}.{h}")
                    act.copy(qT[:, h % 2, :, :].rearrange("p a b -> p (a b)"), o).then_inc(act_steps, AC.step(f"read pq{i}.{h}"))
                if h:
                    o = tile_of(AC, f"ps{i}.{h - 1}")
                    act.copy(sc[:, :, 256 * h - 256:256 * h], o.rearrange("p (t n) -> p t n", t=TT)).then_inc(
                        act_steps, AC.step(f"read ps{i}.{h - 1}"))
                if h == 4:
                    numerators(0)
            for j in range(NJ + 1):
                if 0 < j < NJ:
                    numerators(j)
                if j:
                    b = (j - 1) % 2
                    act.wait_ge(dve_steps, count_of(f"dots {i}.{j - 1}"))
                    act.activation(gel[b], dots[b], ACT.Gelu).then_inc(act_steps, AC.step(f"gelu {i}.{j - 1}"))
                    act.wait_ge(dve_steps, count_of(f"coef {i}.{j - 1}"))
                    for k in range(PR_K):
                        g = PR_K * (NJ * i + j - 1) + k
                        if j > 1:
                            act.wait_ge(pe_steps, count_of(f"v used {g - PR_K}"))
                        act.activation(diag[:, k, :], ident[:, :], ACT.Copy, scale=coef[b][:, k:k + 1]).then_inc(act_steps, AC.step(f"diag {i}.{j - 1}.{k}"))

        def dve_topk(out_v, out_i, s):
            a, b = slice(0, 8), slice(8, 16)
            dve.max(out_v[:, a], s).then_inc(dve_steps, VE.step())
            dve.wait_ge(dve_steps, VE.n)
            dve.max_index(out_i[:, a], out_v[:, a], s).then_inc(dve_steps, VE.step())
            dve.wait_ge(dve_steps, VE.n)
            dve.match_replace(s, out_v[:, a], s, NEG).then_inc(dve_steps, VE.step())
            dve.wait_ge(dve_steps, VE.n)
            dve.max(out_v[:, b], s).then_inc(dve_steps, VE.step())
            dve.wait_ge(dve_steps, VE.n)
            dve.max_index(out_i[:, b], out_v[:, b], s).then_inc(dve_steps, VE.step())
            dve.wait_ge(dve_steps, VE.n)

        def dve_select(i, j):
            t, h, b = j // PR_HEADS, j % PR_HEADS, j % 2
            if t == 0:
                dve.wait_ge(act_steps, count_of(f"read ps{i}.{h}"))
            for p in range(2):
                dve_topk(sv[b][:, p, :], si_u[b][:, p, :].bitcast(U32), sc[:, t, 256 * h + 128 * p:256 * h + 128 * p + 128])
            dve.tensor_scalar(si_f[b][:, 0, :], si_u[b][:, 0, :].bitcast(U32), float(PR_KEYS * i), None, ALU.add).then_inc(dve_steps, VE.step())
            dve.tensor_copy(si_f[b][:, 1, :], si_u[b][:, 1, :].bitcast(U32)).then_inc(dve_steps, VE.step())
            dve.tensor_tensor(cand, sv[b][:, 0, :].unsqueeze(2).to_broadcast([P, PR_K, PR_K]),
                                     sv[b][:, 1, :].unsqueeze(1).to_broadcast([P, PR_K, PR_K]), ALU.add).then_inc(dve_steps, VE.step())
            dve.wait_ge(dve_steps, VE.n)
            if j >= 2:
                dve.wait_ge(act_steps, count_of(f"ex {i}.{j - 2}"))
            dve_topk(fv[b], fi[b].bitcast(U32), cand.rearrange("p a b -> p (a b)"))
            dve.tensor_scalar(nmx[b], fv[b][:, 0:1], -1.0, None, ALU.mult).then_inc(dve_steps, VE.step(f"nmax {i}.{j}"))
            dve.tensor_scalar(ab_u[:, 0, :].bitcast(U32), fi[b].bitcast(U32), 4, None, ALU.logical_shift_right).then_inc(dve_steps, VE.step())
            dve.tensor_scalar(ab_u[:, 1, :].bitcast(U32), fi[b].bitcast(U32), 15, None, ALU.bitwise_and).then_inc(dve_steps, VE.step())
            dve.wait_ge(dve_steps, VE.n)
            dve.tensor_copy(ab_f, ab_u.bitcast(U32)).then_inc(dve_steps, VE.step())
            dve.wait_ge(dve_steps, VE.n)
            dve.tensor_tensor(eq, ab_f.rearrange("p a b -> p (a b)").unsqueeze(2).to_broadcast([P, 2 * PR_K, PR_K]),
                                     iota16[:, :].unsqueeze(1).to_broadcast([P, 2 * PR_K, PR_K]), ALU.is_equal).then_inc(dve_steps, VE.step())
            dve.wait_ge(dve_steps, VE.n)
            eq4 = eq.rearrange("p (a b) c -> p a b c", a=2)
            dve.tensor_tensor(eq4, eq4, si_f[b].unsqueeze(2).to_broadcast([P, 2, PR_K, PR_K]), ALU.mult).then_inc(dve_steps, VE.step())
            dve.wait_ge(dve_steps, VE.n)
            dve.tensor_reduce(ids.rearrange("p a b -> p (a b)"), eq, AX, ALU.add).then_inc(dve_steps, VE.step())
            dve.wait_ge(dve_steps, VE.n)
            if j >= 4:
                dve.wait_ge(pe_steps, count_of(f"v used {PR_K * (NJ * i + j - 4) + PR_K - 1}"))
            dve.scalar_tensor_tensor(ix[j % 4].bitcast(U32), ids[:, 0, :], float(PR_KEYS), ids[:, 1, :], ALU.mult, ALU.add).then_inc(dve_steps, VE.step(f"ix {i}.{j}"))
            dve.wait_ge(dve_steps, VE.n)

        def dve_dots(i, j, k0, k1):
            t, b = j // PR_HEADS, j % 2
            if k0 == 0 and j >= 2:
                dve.wait_ge(act_steps, count_of(f"gelu {i}.{j - 2}"))
            for k in range(k0, k1):
                g = PR_K * (NJ * i + j) + k
                dve.wait_ge(sems[f"u_rows{g % U_SLOTS}"], 16 * (g // U_SLOTS + 1))
                r = u_ring[:, g % U_SLOTS, :]
                dve.tensor_tensor_reduce(r, r, x_tok[:, t, :], 1.0, 0.0, ALU.mult, ALU.add, dots[b][:, k:k + 1]).then_inc(dve_steps, VE.step(f"u used {g}"))
            if k1 == PR_K:
                found[f"dots {i}.{j}"] = (VE.who, VE.n)

        def dve_coef(i, j):
            b = j % 2
            dve.wait_ge(act_steps, count_of(f"ex {i}.{j}"))
            dve.reciprocal(sm[b], sm[b]).then_inc(dve_steps, VE.step())
            dve.wait_ge(dve_steps, VE.n)
            dve.wait_ge(act_steps, count_of(f"gelu {i}.{j}"))
            if j >= 2:
                dve.wait_ge(act_steps, count_of(f"diag {i}.{j - 2}.{PR_K - 1}"))
            dve.scalar_tensor_tensor(coef[b], ex[b], sm[b], gel[b], ALU.mult, ALU.mult).then_inc(dve_steps, VE.step(f"coef {i}.{j}"))
            dve.wait_ge(dve_steps, VE.n)

        def dve_peer(i):
            dve_select(i, 0)
            for j in range(NJ):
                dve_dots(i, j, 0, 4)
                if j:
                    dve_coef(i, j - 1)
                dve_dots(i, j, 4, 8)
                if j + 1 < NJ:
                    dve_select(i, j + 1)
                dve_dots(i, j, 8, PR_K)
            dve_coef(i, NJ - 1)
            dve_layer_norm(i, "peer", f"ln2g{i}", f"ln2b{i}")

        u_table, v_table = (A[n].rearrange("l e d -> (l e) d") for n in ("peer_u", "peer_v"))

        def pool_peer(i):
            def gather(j, k, ring_, sem_, slots, used, table):
                g = PR_K * (NJ * i + j) + k
                if g >= slots:
                    pool.wait_ge(*by(f"{used} used {g - slots}"))
                pool.indirect_dma_start(ring_[:, g % slots, :], None, table,
                                                  bass.IndirectOffsetOnAxis(ix[j % 4][:, k:k + 1].bitcast(U32), 0),
                                                  element_offset=0).then_inc(sems[f"{sem_}{g % slots}"], landed(f"{sem_}{g % slots}", f"{sem_} {g}"))

            for j in range(NJ + 1):
                if j < NJ:
                    pool.wait_ge(dve_steps, count_of(f"ix {i}.{j}"))
                for k in range(PR_K):
                    if j < NJ:
                        gather(j, k, u_ring, "u_rows", U_SLOTS, "u", u_table)
                    if j:
                        gather(j - 1, k, v_ring, "v_rows", V_SLOTS, "v", v_table)

        x_pad = area(0, RG_B, S + RG_CONV - 1)
        xc, r_g, i_g, a_t, th, l1, gg = (area(2072 + 2048 * n, RG_B, S) for n in range(7))
        xq1, p1, pT1 = area(16408, 2, S), area(16920, XA_HEADS, TT, S), area(18968, XA_HEADS, 2, S)
        sp_c = area(21016, 4, RG_B)

        def pe_rglru():
            wait_transposed(TE, "xrt")
            for c in range(4):
                w = chunk(f"r.x{c}", TE)
                pe_columns(f"r.x{c}", w, x_fm, RG_D)
                release(f"r.x{c}")
            wa, wi = chunk("r.a", TE), chunk("r.i", TE)
            for b in range(RG_B):
                pe.wait_ge(dve_steps, count_of(f"xc {b}"))
                o = open_tile(f"r.g{b}.ri")
                mm(o[0:RG_D, 0:S], wa[:, b, :], xc[0:RG_D, b, :], True, True)
                mm(o[0:RG_D, S:2 * S], wi[:, b, :], xc[0:RG_D, b, :], True, True).then_inc(pe_steps, TE.step(f"tile r.g{b}.ri"))
            release("r.a")
            release("r.i")
            w = chunk("r.q", TE)
            pe_columns("r.xq", w, x_fm)
            release("r.q")
            for c in range(4):
                w = chunk(f"r.g{c}", TE)
                pe_columns(f"r.gate{c}", w, x_fm, RG_D)
                release(f"r.g{c}")
            pe_attention(1, xq1, lambda h: p1[:, h, :, :], lambda h: pT1[:, h, :, :], RG_B)
            pe.wait_ge(act_steps, count_of("xa1 ready"))
            pe.wait_ge(dve_steps, count_of("y rglru"))
            pe.wait_ge(dve_steps, count_of("acc peer0 read"))
            pe_into_acc("mix1", [f"wout1.{c}" for c in range(RG_B // 2)] + ["wout1.x"],
                        lambda k: mix_fm[0:RG_D, k, :] if k < RG_B else mix_fm[:, k, :])

        def act_rglru():
            R = slice(0, RG_D)
            act.wait_ge(dve_steps, count_of("abs lam"))
            act.activation(sp_c[R, 1, :], sp_c[R, 1, :], ACT.Exp, scale=-1.0).then_inc(act_steps, AC.step())
            act.wait_ge(act_steps, AC.n)
            act.activation(sp_c[R, 1, :], sp_c[R, 1, :], ACT.Ln, bias=1.0).then_inc(act_steps, AC.step("log1p lam"))
            for b in range(RG_B):
                o = tile_of(AC, f"r.g{b}.ri")
                act.activation(r_g[R, b, :], o[R, 0:S], ACT.Sigmoid, bias=col_rg[:, RG_BA + b:RG_BA + b + 1]).then_inc(act_steps, AC.step())
                act.activation(i_g[R, b, :], o[R, S:2 * S], ACT.Sigmoid, bias=col_rg[:, RG_BX + b:RG_BX + b + 1]).then_inc(act_steps, AC.step(f"read r.g{b}.ri"))
            act.wait_ge(act_steps, AC.n)
            act.wait_ge(dve_steps, count_of("softplus lam"))
            for b in range(RG_B):
                act.activation(a_t[R, b, :], r_g[R, b, :], ACT.Exp, scale=sp_c[R, 2, b:b + 1]).then_inc(act_steps, AC.step())
                act.activation(th[R, b, :], r_g[R, b, :], ACT.Tanh, scale=sp_c[R, 3, b:b + 1]).then_inc(act_steps, AC.step())
            act.wait_ge(act_steps, AC.n)
            act.activation(l1[R, :, :], th[R, :, :], ACT.Ln, bias=1.0).then_inc(act_steps, AC.step())
            act.wait_ge(act_steps, AC.n)
            act.activation(l1[R, :, :], l1[R, :, :], ACT.Exp, scale=-0.5).then_inc(act_steps, AC.step())
            act.wait_ge(act_steps, AC.n)
            act.activation(th[R, :, :], th[R, :, :], ACT.Sqrt, scale=2.0).then_inc(act_steps, AC.step("sqrt parts"))
            o = tile_of(AC, "r.xq")
            act.copy(xq1.rearrange("p a b -> p (a b)"), o).then_inc(act_steps, AC.step("read r.xq"))
            found["xq1 ready"] = (AC.who, AC.n)
            for c in range(4):
                o = tile_of(AC, f"r.gate{c}")
                act.activation(gg[R, 2 * c:2 * c + 2, :].rearrange("p a b -> p (a b)"), o[R, :], ACT.Gelu).then_inc(act_steps, AC.step(f"read r.gate{c}"))
            act_attention(1, lambda h: p1[:, h, :, :], lambda h: pT1[:, h, :, :], RG_B)

        def dve_rglru():
            R = slice(0, RG_D)
            lam = col_rg[:, RG_LAM:RG_LAM + RG_B]
            dve.tensor_scalar(sp_c[R, 0, :], lam, -1.0, None, ALU.mult).then_inc(dve_steps, VE.step())
            dve.wait_ge(dve_steps, VE.n)
            dve.tensor_tensor(sp_c[R, 1, :], sp_c[R, 0, :], lam, ALU.max).then_inc(dve_steps, VE.step("abs lam"))
            dve.wait_ge(dve_steps, VE.n)
            dve.memset(x_pad[R, :, 0:RG_CONV - 1], 0.0).then_inc(dve_steps, VE.step())
            for c in range(4):
                o = tile_of(VE, f"r.x{c}")
                dve.tensor_copy(x_pad[R, 2 * c:2 * c + 2, RG_CONV - 1:], o[R, :].rearrange("p (a b) -> p a b", a=2)).then_inc(dve_steps, VE.step(f"read r.x{c}"))
                dve.wait_ge(dve_steps, VE.n)
                for b in (2 * c, 2 * c + 1):
                    def tap(k):
                        return col_rg[:, RG_B * k + b:RG_B * k + b + 1]
                    dve.tensor_scalar(xc[R, b, :], x_pad[R, b, 0:S], tap(0), col_rg[:, RG_CB + b:RG_CB + b + 1], ALU.mult, ALU.add).then_inc(dve_steps, VE.step())
                    dve.wait_ge(dve_steps, VE.n)
                    for k in range(1, RG_CONV):
                        dve.scalar_tensor_tensor(xc[R, b, :], x_pad[R, b, k:k + S], tap(k), xc[R, b, :], ALU.mult, ALU.add).then_inc(dve_steps, VE.step(f"xc {b}"))
                        dve.wait_ge(dve_steps, VE.n)
            dve.wait_ge(act_steps, count_of("log1p lam"))
            dve.scalar_tensor_tensor(sp_c[R, 1, :], sp_c[R, 0, :], 0.0, sp_c[R, 1, :], ALU.max, ALU.add).then_inc(dve_steps, VE.step())
            dve.wait_ge(dve_steps, VE.n)
            dve.tensor_scalar(sp_c[R, 2, :], sp_c[R, 1, :], -RG_C, None, ALU.mult).then_inc(dve_steps, VE.step())
            dve.tensor_scalar(sp_c[R, 3, :], sp_c[R, 1, :], RG_C, None, ALU.mult).then_inc(dve_steps, VE.step("softplus lam"))
            dve.wait_ge(dve_steps, VE.n)
            dve.wait_ge(act_steps, count_of(f"read r.g{RG_B - 1}.ri"))
            dve.tensor_tensor(i_g[R, :, :], i_g[R, :, :], xc[R, :, :], ALU.mult).then_inc(dve_steps, VE.step())
            dve.wait_ge(dve_steps, VE.n)
            dve.wait_ge(act_steps, count_of("sqrt parts"))
            dve.tensor_tensor(i_g[R, :, :], i_g[R, :, :], l1[R, :, :], ALU.mult).then_inc(dve_steps, VE.step())
            dve.wait_ge(dve_steps, VE.n)
            dve.tensor_tensor(i_g[R, :, :], i_g[R, :, :], th[R, :, :], ALU.mult).then_inc(dve_steps, VE.step())
            dve.wait_ge(dve_steps, VE.n)
            for b in range(RG_B):
                dve.tensor_tensor_scan(r_g[R, b, :], a_t[R, b, :], i_g[R, b, :], 0.0, ALU.mult, ALU.add).then_inc(dve_steps, VE.step())
            dve.wait_ge(dve_steps, VE.n)
            attention_softmax(1, lambda h: p1[:, h, :, :], None, 0)
            for c in range(4):
                dve.wait_ge(act_steps, count_of(f"read r.gate{c}"))
            dve.tensor_tensor(mix_fm[R, 0:RG_B, :], r_g[R, :, :], gg[R, :, :], ALU.mult).then_inc(dve_steps, VE.step("y rglru"))
            dve_layer_norm(1, "mix", "ln1g1", "ln1b1")

        hn = area(0, TT, D)
        ssq, psq = stat[:, 32:34], stat[:, 34:36]

        def act_pre(n, split=False):
            if split:
                names = ffn_chunks(n[3], n[4])
                for name in names[early_of(n):EARLY]:
                    act_split(name)
            for t in range(TT):
                act.wait_ge(dve_steps, count_of(f"x {n}.{t}"))
                act.activation(junk2[:, t, :], x_tok[:, t, :], ACT.Square, accum_out=ssq[:, t:t + 1]).then_inc(act_steps, AC.step(f"ssq {n}.{t}"))
            for t in range(TT):
                act.wait_ge(dve_steps, count_of(f"var {n}.{t}"))
                act.sqrt(ssq[:, t:t + 1], ssq[:, t:t + 1]).then_inc(act_steps, AC.step(f"std {n}.{t}"))
            if not split:
                x_transposed(n + "t", AC, x_fm, pre_scale(n))
                return
            for name in names[EARLY:HI_SLOTS - 1]:
                act_split(name)
            for c in range(KD // 2):
                o = tile_of(AC, f"{n}t.{c}")
                for k in range(2):
                    act.activation(x_hi[:, 2 * c + k, :], o[:, S * k:S * k + S], ACT.Copy,
                                   scale=pre_scale(n)[:, 2 * c + k:2 * c + k + 1]).then_inc(act_steps, AC.step(f"x hi {n}.{c}"))
            act_split(names[HI_SLOTS - 1])

        def early_of(n):
            return 0 if n == "ffn00" else EARLY

        def pre_scale(n):
            l, s = int(n[3]), int(n[4])
            at = COL_PRE + 8 * (3 * l + s)
            return col[:, at:at + 8]

        def dve_pre(n, split=False):
            if split:
                names = ffn_chunks(n[3], n[4])
            for t in range(TT):
                dve.wait_ge(act_steps, count_of(f"ssq {n}.{t}"))
                dve.tensor_scalar(ssq[:, t:t + 1], ssq[:, t:t + 1], 1.0 / D, RMS_EPS, ALU.mult, ALU.add).then_inc(dve_steps, VE.step(f"var {n}.{t}"))
            if split and not early_of(n):
                dve_split(names[0])
            for t in range(TT):
                dve.wait_ge(act_steps, count_of(f"std {n}.{t}"))
                dve.reciprocal(ssq[:, t:t + 1], ssq[:, t:t + 1]).then_inc(dve_steps, VE.step())
                dve.wait_ge(dve_steps, VE.n)
                dve.tensor_scalar(hn[:, t, :], x_tok[:, t, :], ssq[:, t:t + 1], None, ALU.mult).then_inc(dve_steps, VE.step(f"hn {n}"))
            if not split:
                x_transposed(n + "t", VE, x_fm, pre_scale(n))
                return
            for name in names[early_of(n) or 1:HI_SLOTS - 1]:
                dve_split(name)
            for c in range(KD // 2):
                o = tile_of(VE, f"{n}t.{c}")
                dve.wait_ge(act_steps, count_of(f"x hi {n}.{c}"))
                for k in range(2):
                    m = 2 * c + k
                    dve.scalar_tensor_tensor(x_lo[:, m, :], o[:, S * k:S * k + S], pre_scale(n)[:, m:m + 1], x_hi[:, m, :].bitcast(F32),
                                             ALU.mult, ALU.subtract).then_inc(dve_steps, VE.step(f"read {n}t.{c}"))
            dve_split(names[HI_SLOTS - 1])

        def pe_pre(n):
            pe.wait_ge(dve_steps, count_of(f"hn {n}"))
            pe_transposes(n + "t", lambda t, k: hn[:, t, 128 * k:128 * k + 128])
            wait_transposed(TE, n + "t")

        def act_post(n, src):
            act.sqrt(spare, spare).then_inc(act_steps, AC.step())
            act.wait_ge(pe_steps, count_of(f"acc {n}"))
            for t in range(TT):
                if t:
                    act.wait_ge(dve_steps, count_of(f"gain {n}.{t}"))
                act.activation(junk2[:, t, :], src(t), ACT.Square, accum_out=psq[:, t:t + 1]).then_inc(act_steps, AC.step(f"psq {n}.{t}"))
            for t in range(TT):
                act.wait_ge(dve_steps, count_of(f"pvar {n}.{t}"))
                act.sqrt(psq[:, t:t + 1], psq[:, t:t + 1]).then_inc(act_steps, AC.step(f"pstd {n}.{t}"))

        spare = stat[:, 36:37]

        junk2 = area(13824, TT, D)

        def acc_rows(t):
            return acc[:, 2 * t:2 * t + 2, :].rearrange("p a b -> p (a b)")

        def dve_post(n, src, gain, tmp, last):
            g = row("post" + n[3:], VE)
            dve.wait_ge(pe_steps, count_of(f"acc {n}"))
            for t in reversed(range(TT)):
                if t == 0:
                    dve.wait_ge(act_steps, count_of(f"psq {n}.0"))
                dve.tensor_tensor(tmp[:, t, :], src(t), g, ALU.mult).then_inc(dve_steps, VE.step(f"gain {n}.{t}"))
            found[f"row post{n[3:]}"] = (VE.who, VE.n)
            for t in range(TT):
                dve.wait_ge(act_steps, count_of(f"psq {n}.{t}"))
                dve.tensor_scalar(psq[:, t:t + 1], psq[:, t:t + 1], 1.0 / (D * gain ** 2), RMS_EPS / gain ** 2, ALU.mult, ALU.add).then_inc(
                    dve_steps, VE.step(f"pvar {n}.{t}"))
            dve.wait_ge(act_steps, count_of(f"psq {n}.{TT - 1}"))
            found[f"acc {n} read"] = (VE.who, VE.n)
            for t in range(TT):
                dve.wait_ge(act_steps, count_of(f"pstd {n}.{t}"))
                dve.wait_ge(dve_steps, count_of(f"pvar {n}.{t}"))
                dve.reciprocal(psq[:, t:t + 1], psq[:, t:t + 1]).then_inc(dve_steps, VE.step())
                dve.wait_ge(dve_steps, VE.n)
                dve.scalar_tensor_tensor(x_tok[:, t, :], tmp[:, t, :], psq[:, t:t + 1], x_tok[:, t, :], ALU.mult, ALU.add).then_inc(
                    dve_steps, VE.step(f"x {last}.{t}"))
            dve.wait_ge(dve_steps, VE.n)
            found[f"x {last}"] = (VE.who, VE.n)

        sg = area(2048, 2, S)
        a_hi, a_lo = over("a_hi", "arena", 2560, FF_T, S), over("a_lo", "arena", 8192, FF_T, S)
        a_f = area(8192, FF_T, S)
        tmp_f = area(0, TT, D)
        EARLY = 2

        def ffn_chunks(l, s):
            up = [f"{w}.{l}{s}.{c}" for c in range(FF_T // 2) for w in ("w1", "w3")]
            return up + [f"w2.{l}{s}.{c}" for c in range(FF_T // 2)]

        def pe_ffn(l, s, before):
            n = f"ffn{l}{s}"
            pe_pre(n)
            for c in range(FF_T // 2):
                w1, w3 = split_chunk(f"w1.{l}{s}.{c}"), split_chunk(f"w3.{l}{s}.{c}")
                for f in range(2):
                    o = open_tile(f"{n}.{2 * c + f}")
                    for half, w in ((0, w1), (1, w3)):
                        for k in range(KD):
                            i = mm3(o[:, S * half:S * half + S], [v[:, k, P * f:P * f + P] for v in w],
                                    (x_hi[:, k, :], x_lo[:, k, :]), k == 0, k == KD - 1)
                    i.then_inc(pe_steps, TE.step(f"tile {n}.{2 * c + f}"))
                release(f"w1.{l}{s}.{c}")
                release(f"w3.{l}{s}.{c}")
            pe.wait_ge(dve_steps, count_of(f"acc {before} read"))
            for c in range(FF_T // 2):
                w = split_chunk(f"w2.{l}{s}.{c}")
                pe.wait_ge(dve_steps, count_of(f"gated {n}.{2 * c + 1}"))
                for k in (2 * c, 2 * c + 1):
                    for t in range(TT):
                        for half in range(2):
                            i = mm3(acc[:, 2 * t + half, :], [v[:, k, P * t:P * t + P] for v in (a_hi, a_lo)],
                                    [v[:, k - 2 * c, 512 * half:512 * half + 512] for v in w], k == 0, k == FF_T - 1)
                i.then_inc(pe_steps, TE.step(f"used w2.{l}{s}.{c}"))
            found[f"acc {n}"] = (TE.who, TE.n)

        def act_ffn(l, s, after=()):
            n = f"ffn{l}{s}"
            names = ffn_chunks(l, s)
            act_pre(n, True)
            for f in range(FF_T):
                act_split(names[HI_SLOTS + f])
                o = tile_of(AC, f"{n}.{f}")
                if f >= 2:
                    act.wait_ge(dve_steps, count_of(f"read {n}.{f - 2}"))
                act.activation(sg[:, f % 2, :], o[:, 0:S], ACT.Silu).then_inc(act_steps, AC.step(f"silu {n}.{f}"))
            for name in names[HI_SLOTS + FF_T:] + list(after):
                act_split(name)
            act_post(n, acc_rows)

        def dve_ffn(l, s, last, after=()):
            n = f"ffn{l}{s}"
            names = ffn_chunks(l, s)
            dve_pre(n, True)
            for f in range(FF_T):
                dve_split(names[HI_SLOTS + f])
                dve.wait_ge(act_steps, count_of(f"silu {n}.{f}"))
                o = tile_of(VE, f"{n}.{f}")
                dve.tensor_tensor(a_f[:, f, :], sg[:, f % 2, :], o[:, S:2 * S], ALU.mult).then_inc(dve_steps, VE.step(f"read {n}.{f}"))
                dve.wait_ge(dve_steps, VE.n)
                dve.tensor_copy(a_hi[:, f, :], a_f[:, f, :]).then_inc(dve_steps, VE.step())
                dve.wait_ge(dve_steps, VE.n)
                dve.tensor_tensor(a_lo[:, f, :], a_f[:, f, :], a_hi[:, f, :].bitcast(F32), ALU.subtract).then_inc(dve_steps, VE.step(f"gated {n}.{f}"))
            for name in names[HI_SLOTS + FF_T:] + list(after):
                dve_split(name)
            dve_post(n, acc_rows, 0.5, tmp_f, last)

        u_fm, y_fm = area(2048, KD, S), area(4096, KD, S)
        b_T = area(6144, 2, KD, P)
        c_z = area(8192, 3, S5_J, 32)
        cs = area(11264, 2, 4, 2, S)
        turn = area(15360, 2, 4, S)
        w_t1, w_t2 = area(17408, 2, 2, S), area(18432, 2, 2, S)
        w_in, w_sc = area(19456, 2, 2, S), area(20480, 2, 2, S)
        w_q1, w_q2 = area(21504, 2, 2, S), area(22528, 2, 2, S)
        s5v = area(23552, 12, S5_J)
        b_raw = area(19456, 2, S5_J, 16)
        c_raw = area(20480, 2, KD, P)
        bb = area(23936, 2, S5_J, 16)
        b_tmp = area(24960, 2, S5_J, 16)
        bbz = area(17408, 2, S5_J, 32)
        TWO_PI = 6.2831850

        def pool_s5_loads():
            for n, name in enumerate(("s5_b_re_2", "s5_b_im_2")):
                for two in range(2):
                    pool.dma_start(b_raw[64 * two:64 * two + 64, n, :, :],
                                            A[name][0].rearrange("(j two) p h -> two p j h", two=2)[two]).then_inc(s5_b, landed("s5_b", "s5 b loaded"))
            for n, name in enumerate(("s5_c_re_2", "s5_c_im_2")):
                for two in range(2):
                    pool.dma_start(c_raw[:, n, :, 64 * two:64 * two + 64],
                                            A[name][0].rearrange("(m g) h p -> (g h) m p", g=8)).then_inc(s5_c, landed("s5_c", "s5 c loaded"))

        def pe_s5():
            n = "mid01"
            pe_pre(n)
            for c in range(4):
                w = chunk(f"s.in{c}", TE)
                pe_columns(f"s.u{c}", w, x_fm)
                release(f"s.in{c}")
            pe.wait_ge(s5_c, count_of("s5 c loaded"))
            for part in range(2):
                for m in range(0, KD, 4):
                    o = open_tile(f"s.c{part}{m}")
                    for q in range(4):
                        i = pe.transpose(o[:, 128 * q:128 * q + 128], c_raw[:, part, m + q, :], ident[:, :])
                    i.then_inc(pe_steps, TE.step(f"tile s.c{part}{m}"))
            pe.wait_ge(dve_steps, count_of("bbz"))
            for part in range(2):
                for m in range(0, KD, 4):
                    o = open_tile(f"s.b{part}{m}")
                    for q in range(4):
                        i = pe.transpose(o[:, 128 * q:128 * q + 128],
                                         bbz[:, part, 4 * (m + q):4 * (m + q) + 4, :].rearrange("p a b -> p (a b)"), ident[:, :])
                    i.then_inc(pe_steps, TE.step(f"tile s.b{part}{m}"))
            for part in range(2):
                for m in range(0, KD, 4):
                    pe.wait_ge(act_steps, count_of(f"read s.b{part}{m}"))
                    pe.wait_ge(dve_steps, count_of(f"read s.c{part}{m}"))
            for c in range(4):
                pe.wait_ge(act_steps, count_of(f"read s.u{c}"))

            def drive(j):
                o = open_tile(f"s.bu{j}")
                r = slice(32 * (j % 4), 32 * (j % 4) + 32)
                for part in range(2):
                    i = mm(o[:, S * part:S * part + S], b_T[r, part, j // 4, :], u_fm[r, j // 4, :], True, True)
                i.then_inc(pe_steps, TE.step(f"tile s.bu{j}"))

            pe.wait_ge(dve_steps, count_of("acc ffn00 read"))
            for j in range(3):
                drive(j)
            for j in range(S5_J):
                if j + 3 < S5_J:
                    drive(j + 3)
                if j % 4 == 0:
                    if j >= 8:
                        pe.wait_ge(act_steps, count_of(f"read s.y{j // 4 - 2}"))
                o = acc[:, (j // 4) % 2, 0:S]
                r = slice(32 * (j % 4), 32 * (j % 4) + 32)
                pe.wait_ge(dve_steps, count_of(f"s.q1 {j}"))
                pe.wait_ge(pool_steps, count_of(f"s.q2 {j}"))
                for q, (sign, src) in enumerate(((0, w_q1[:, j % 2, 0, :]), (1, w_q1[:, j % 2, 1, :]),
                                                 (2, w_q2[:, j % 2, 0, :]), (2, w_q2[:, j % 2, 1, :]))):
                    i = mm(o[r, :], c_z[:, sign, j, :], src, q == 0, q == 3)
                i.then_inc(pe_steps, TE.step(f"s.y used {j}"))
            for c in range(4):
                w = chunk(f"s.glu{c}", TE)
                if c == 0:
                    pe.wait_ge(act_steps, count_of("s5 y"))
                pe_columns(f"s.g{c}", w, y_fm)
                release(f"s.glu{c}")
            for c in range(4):
                pe.wait_ge(dve_steps, count_of(f"s.z{c}"))
            pe.wait_ge(act_steps, count_of("read s.y7"))
            pe_into_acc(n, [f"s.out{c}" for c in range(4)], lambda k: u_fm[:, k, :])

        def act_s5():
            n = "mid01"
            act_pre(n)
            act.wait_ge(dve_steps, count_of("log dt"))
            act.activation(s5v[:, 0, :], col_s5[:, 64:96], ACT.Exp).then_inc(act_steps, AC.step("dt"))
            act.wait_ge(act_steps, AC.n)
            act.wait_ge(dve_steps, count_of("dt re"))
            act.activation(s5v[:, 1, :], s5v[:, 1, :], ACT.Exp).then_inc(act_steps, AC.step("mag"))
            act.wait_ge(dve_steps, count_of("angle"))
            act.activation(s5v[:, 4, :], s5v[:, 3, :], ACT.Sin, scale=TWO_PI).then_inc(act_steps, AC.step())
            act.activation(s5v[:, 5, :], s5v[:, 3, :], ACT.Sin, scale=TWO_PI / 2).then_inc(act_steps, AC.step("sines"))
            act_s5_whole(0)
            act_s5_whole(1)
            act_s5_cs(0)
            for c in range(4):
                o = tile_of(AC, f"s.u{c}")
                act.copy(u_fm[:, 2 * c:2 * c + 2, :].rearrange("p a b -> p (a b)"), o).then_inc(act_steps, AC.step(f"read s.u{c}"))
            for part in range(2):
                for m in range(0, KD, 4):
                    o = tile_of(AC, f"s.b{part}{m}")
                    act.copy(b_T[:, part, m:m + 4, :].rearrange("p a b -> p (a b)"), o).then_inc(act_steps, AC.step(f"read s.b{part}{m}"))
            for q in range(8):
                if q:
                    act_s5_cs(q)
                if q + 2 < 8:
                    act_s5_whole(q + 2)
                if q >= 1:
                    act_s5_y(q - 1)
            act_s5_y(7)
            for m in range(KD):
                act.wait_ge(dve_steps, count_of(f"y sum {m}"))
                act.activation(y_fm[:, m, :], y_fm[:, m, :], ACT.Gelu_apprx_tanh).then_inc(act_steps, AC.step("s5 y"))
            for c in range(4):
                o = tile_of(AC, f"s.g{c}")
                for k in range(2):
                    m = 2 * c + k
                    act.activation(u_fm[:, m, :], o[:, S * k:S * k + S], ACT.Sigmoid, bias=col[:, COL_GLU + m:COL_GLU + m + 1]).then_inc(act_steps, AC.step(f"read s.g{c}"))
            for name in ffn_chunks(0, 2)[:EARLY]:
                act_split(name)
            act_post(n, acc_rows)

        def act_s5_y(m):
            act.wait_ge(pe_steps, count_of(f"s.y used {4 * m + 3}"))
            act.copy(y_fm[:, m, :], acc[:, m % 2, 0:S]).then_inc(act_steps, AC.step(f"read s.y{m}"))

        def act_s5_cs(q):
            act.wait_ge(dve_steps, count_of(f"turn {q}"))
            if q >= 2:
                act.wait_ge(dve_steps, count_of(f"s.q1 {4 * q - 5}"))
                act.wait_ge(pool_steps, count_of(f"s.q2 {4 * q - 5}"))
            b = q % 2
            act.activation(cs[:, b, :, 1, :], turn[:, b, :, :], ACT.Sin, scale=TWO_PI / 2).then_inc(act_steps, AC.step())
            act.wait_ge(act_steps, AC.n)
            act.activation(cs[:, b, :, 1, :], cs[:, b, :, 1, :], ACT.Square).then_inc(act_steps, AC.step())
            act.wait_ge(act_steps, AC.n)
            act.activation(cs[:, b, :, 0, :], cs[:, b, :, 1, :], ACT.Copy, scale=-2.0, bias=1.0).then_inc(act_steps, AC.step())
            act.wait_ge(act_steps, AC.n)
            act.activation(cs[:, b, :, 1, :], turn[:, b, :, :], ACT.Sin, scale=TWO_PI).then_inc(act_steps, AC.step(f"cs {q}"))
            act.wait_ge(act_steps, AC.n)

        def act_s5_whole(q):
            b = q % 2
            for k in range(4):
                act.activation(turn[:, b, k, :], t_row[:, :], ACT.Copy, scale=s5v[:, 3, 4 * q + k:4 * q + k + 1],
                               bias=ROUND).then_inc(act_steps, AC.step())
            act.wait_ge(act_steps, AC.n)
            act.activation(turn[:, b, :, :], turn[:, b, :, :], ACT.Copy, bias=-ROUND).then_inc(act_steps, AC.step(f"whole {q}"))

        def dve_s5_turn(j):
            q, k = j // 4, j % 4
            v = turn[:, q % 2, k, :]
            dve.wait_ge(act_steps, count_of(f"whole {q}"))
            dve.scalar_tensor_tensor(v, t_row[:, :], s5v[:, 3, j:j + 1], v, ALU.mult, ALU.subtract).then_inc(dve_steps, VE.step(f"turn {q}"))

        def swapped(v):
            return bass.AP(v.tensor, v.offset + S, [list(v.ap[0]), [-S, 2], [1, S]])

        def pool_s5():
            pool.wait_ge(dve_steps, count_of("x mid01"))
            pool_s5_loads()
            for j in range(S5_J + 1):
                b = j % 2
                if j < S5_J:
                    if j >= 2:
                        pool.wait_ge(dve_steps, count_of(f"scan {j - 2}"))
                    pool.wait_ge(dve_steps, count_of(f"t1 {j}"))
                    pool.tensor_tensor(w_in[:, b, 0, :], w_t1[:, b, 0, :], w_t1[:, b, 1, :], ALU.add).then_inc(pool_steps, PO.step(f"in re {j}"))
                    pool.wait_ge(dve_steps, count_of(f"read s.bu{j}"))
                    pool.tensor_tensor(w_in[:, b, 1, :], w_t2[:, b, 1, :], w_t2[:, b, 0, :], ALU.subtract).then_inc(pool_steps, PO.step(f"in im {j}"))
                if j:
                    pool.wait_ge(dve_steps, count_of(f"scan {j - 1}"))
                    if j >= 3:
                        pool.wait_ge(pe_steps, count_of(f"s.y used {j - 3}"))
                    v = cs[:, ((j - 1) // 4) % 2, (j - 1) % 4, :, :]
                    pool.tensor_tensor(w_q2[:, 1 - b, :, :], w_sc[:, 1 - b, :, :], swapped(v), ALU.mult).then_inc(pool_steps, PO.step(f"s.q2 {j - 1}"))

        def dve_s5():
            n = "mid01"
            dve_pre(n)
            re, im = col_s5[:, 0:32], col_s5[:, 32:64]
            V = lambda k: s5v[:, k, :]
            dve.tensor_copy(V(2), col_s5[:, 64:96]).then_inc(dve_steps, VE.step("log dt"))
            dve.wait_ge(act_steps, count_of("dt"))
            dve.tensor_tensor(V(1), V(0), re, ALU.mult).then_inc(dve_steps, VE.step("dt re"))
            dve.tensor_tensor(V(3), V(0), im, ALU.mult).then_inc(dve_steps, VE.step())
            dve.wait_ge(dve_steps, VE.n)
            dve.tensor_scalar(V(3), V(3), 1.0 / (2.0 * np.pi), None, ALU.mult).then_inc(dve_steps, VE.step())
            dve.wait_ge(dve_steps, VE.n)
            dve.tensor_scalar(V(2), V(3), ROUND, None, ALU.add).then_inc(dve_steps, VE.step())
            dve.wait_ge(dve_steps, VE.n)
            dve.tensor_scalar(V(2), V(2), ROUND, None, ALU.subtract).then_inc(dve_steps, VE.step())
            dve.wait_ge(dve_steps, VE.n)
            dve.tensor_tensor(V(3), V(3), V(2), ALU.subtract).then_inc(dve_steps, VE.step("angle"))
            dve.wait_ge(dve_steps, VE.n)
            dve.wait_ge(act_steps, count_of("sines"))
            dve.wait_ge(act_steps, count_of("mag"))
            for j in range(8):
                dve_s5_turn(j)
            dve.tensor_tensor(V(5), V(5), V(5), ALU.mult).then_inc(dve_steps, VE.step())
            dve.wait_ge(dve_steps, VE.n)
            dve.tensor_scalar(V(5), V(5), -2.0, 1.0, ALU.mult, ALU.add).then_inc(dve_steps, VE.step())
            dve.wait_ge(dve_steps, VE.n)
            dve.tensor_tensor(V(5), V(5), V(1), ALU.mult).then_inc(dve_steps, VE.step())
            dve.wait_ge(dve_steps, VE.n)
            dve.tensor_scalar(V(5), V(5), 1.0, None, ALU.subtract).then_inc(dve_steps, VE.step())
            dve.wait_ge(dve_steps, VE.n)
            dve.tensor_tensor(V(4), V(4), V(1), ALU.mult).then_inc(dve_steps, VE.step())
            dve.wait_ge(dve_steps, VE.n)
            dve.tensor_tensor(V(6), re, re, ALU.mult).then_inc(dve_steps, VE.step())
            dve.wait_ge(dve_steps, VE.n)
            dve.tensor_tensor(V(7), im, im, ALU.mult).then_inc(dve_steps, VE.step())
            dve.wait_ge(dve_steps, VE.n)
            dve.tensor_tensor(V(6), V(6), V(7), ALU.add).then_inc(dve_steps, VE.step())
            dve.wait_ge(dve_steps, VE.n)
            dve.reciprocal(V(6), V(6)).then_inc(dve_steps, VE.step())
            dve.wait_ge(dve_steps, VE.n)
            dve.tensor_tensor(V(7), V(5), re, ALU.mult).then_inc(dve_steps, VE.step())
            dve.wait_ge(dve_steps, VE.n)
            dve.tensor_tensor(V(8), V(4), im, ALU.mult).then_inc(dve_steps, VE.step())
            dve.wait_ge(dve_steps, VE.n)
            dve.tensor_tensor(V(7), V(7), V(8), ALU.add).then_inc(dve_steps, VE.step())
            dve.wait_ge(dve_steps, VE.n)
            dve.tensor_tensor(V(7), V(7), V(6), ALU.mult).then_inc(dve_steps, VE.step())
            dve.wait_ge(dve_steps, VE.n)
            dve.tensor_tensor(V(8), V(4), re, ALU.mult).then_inc(dve_steps, VE.step())
            dve.wait_ge(dve_steps, VE.n)
            dve.tensor_tensor(V(9), V(5), im, ALU.mult).then_inc(dve_steps, VE.step())
            dve.wait_ge(dve_steps, VE.n)
            dve.tensor_tensor(V(8), V(8), V(9), ALU.subtract).then_inc(dve_steps, VE.step())
            dve.wait_ge(dve_steps, VE.n)
            dve.tensor_tensor(V(8), V(8), V(6), ALU.mult).then_inc(dve_steps, VE.step())
            dve.wait_ge(dve_steps, VE.n)
            fr, fi_ = (V(k).unsqueeze(2).to_broadcast([P, S5_J, 16]) for k in (7, 8))
            dve.wait_ge(s5_b, count_of("s5 b loaded"))
            dve.tensor_tensor(bb[:, 0, :, :], b_raw[:, 0, :, :], fr, ALU.mult).then_inc(dve_steps, VE.step())
            dve.tensor_tensor(b_tmp[:, 0, :, :], b_raw[:, 1, :, :], fi_, ALU.mult).then_inc(dve_steps, VE.step())
            dve.tensor_tensor(bb[:, 1, :, :], b_raw[:, 1, :, :], fr, ALU.mult).then_inc(dve_steps, VE.step())
            dve.tensor_tensor(b_tmp[:, 1, :, :], b_raw[:, 0, :, :], fi_, ALU.mult).then_inc(dve_steps, VE.step())
            dve.wait_ge(dve_steps, VE.n)
            dve.tensor_tensor(bb[:, 0, :, :], bb[:, 0, :, :], b_tmp[:, 0, :, :], ALU.subtract).then_inc(dve_steps, VE.step())
            dve.tensor_tensor(bb[:, 1, :, :], bb[:, 1, :, :], b_tmp[:, 1, :, :], ALU.add).then_inc(dve_steps, VE.step())
            dve.wait_ge(dve_steps, VE.n)
            mk = mask32[:, :].rearrange("p (a b) -> p a b", a=2).unsqueeze(1).to_broadcast([P, S5_J, 2, 16])
            for part in range(2):
                dve.tensor_tensor(bbz[:, part, :, :].rearrange("p j (a b) -> p j a b", a=2),
                                          bb[:, part, :, :].unsqueeze(2).to_broadcast([P, S5_J, 2, 16]), mk, ALU.mult).then_inc(dve_steps, VE.step("bbz"))
            mk = mask32[:, :].unsqueeze(1).to_broadcast([P, 16, 32])
            for part in range(2):
                for m in range(0, KD, 4):
                    o = tile_of(VE, f"s.c{part}{m}").rearrange("p (a b) -> p a b", a=16)
                    js = slice(4 * m, 4 * m + 16)
                    if part == 0:
                        dve.tensor_tensor(c_z[:, 0, js, :], o, mk, ALU.mult).then_inc(dve_steps, VE.step())
                        dve.wait_ge(dve_steps, VE.n)
                        dve.tensor_scalar(c_z[:, 1, js, :], c_z[:, 0, js, :], -1.0, None, ALU.mult).then_inc(dve_steps, VE.step())
                    else:
                        dve.scalar_tensor_tensor(c_z[:, 2, js, :], o, -1.0, mk, ALU.mult, ALU.mult).then_inc(dve_steps, VE.step())
                    found[f"read s.c{part}{m}"] = (VE.who, VE.n)
            dve.wait_ge(dve_steps, VE.n)
            for part in range(2):
                for m in range(0, KD, 4):
                    dve.wait_ge(act_steps, count_of(f"read s.b{part}{m}"))
            for j in range(S5_J + 1):
                b = j % 2
                if j < S5_J:
                    if j % 4 == 0:
                        dve.wait_ge(act_steps, count_of(f"cs {j // 4}"))
                    v = cs[:, (j // 4) % 2, j % 4, :, :]
                    o = tile_of(VE, f"s.bu{j}").rearrange("p (a b) -> p a b", a=2)
                    if j >= 2:
                        dve.wait_ge(pool_steps, count_of(f"in im {j - 2}"))
                    dve.tensor_tensor(w_t1[:, b, :, :], o, v, ALU.mult).then_inc(dve_steps, VE.step(f"t1 {j}"))
                    dve.tensor_tensor(w_t2[:, b, :, :], o, swapped(v), ALU.mult).then_inc(dve_steps, VE.step(f"read s.bu{j}"))
                if j:
                    v = cs[:, ((j - 1) // 4) % 2, (j - 1) % 4, :, :]
                    dve.wait_ge(dve_steps, count_of(f"scan {j - 1}"))
                    if j >= 3:
                        dve.wait_ge(pe_steps, count_of(f"s.y used {j - 3}"))
                    dve.tensor_tensor(w_q1[:, 1 - b, :, :], w_sc[:, 1 - b, :, :], v, ALU.mult).then_inc(dve_steps, VE.step(f"s.q1 {j - 1}"))
                if j < S5_J:
                    if j + 8 < S5_J:
                        dve_s5_turn(j + 8)
                    if j >= 2:
                        dve.wait_ge(pool_steps, count_of(f"s.q2 {j - 2}"))
                    for part in range(2):
                        dve.wait_ge(pool_steps, count_of(f"in {('re', 'im')[part]} {j}"))
                        dve.tensor_tensor_scan(w_sc[:, b, part, :], s5v[:, 1, j:j + 1].to_broadcast([P, S]), w_in[:, b, part, :], 0.0,
                                               ALU.mult, ALU.add).then_inc(dve_steps, VE.step(f"scan {j}"))
            for m in range(KD):
                dve.wait_ge(act_steps, count_of(f"read s.y{m}"))
                dve.scalar_tensor_tensor(y_fm[:, m, :], u_fm[:, m, :], col[:, COL_D + m:COL_D + m + 1], y_fm[:, m, :],
                                                 ALU.mult, ALU.add).then_inc(dve_steps, VE.step(f"y sum {m}"))
            for c in range(4):
                dve.wait_ge(act_steps, count_of(f"read s.g{c}"))
                dve.tensor_tensor(u_fm[:, 2 * c:2 * c + 2, :], u_fm[:, 2 * c:2 * c + 2, :], y_fm[:, 2 * c:2 * c + 2, :], ALU.mult).then_inc(dve_steps, VE.step(f"s.z{c}"))
            for name in ffn_chunks(0, 2)[:EARLY]:
                dve_split(name)
            dve_post(n, acc_rows, 1.0, tmp_s5, "ffn02")

        tmp_s5 = area(11264, TT, D)

        CP = CV_TAPS - 1
        z_pad = area(2048, KD, S + CP)
        c_acc = area(4352, KD, S)
        c_sg = area(6400, 2, S)
        c_sq = area(6912, KD, S)
        c_mean, c_rstd = area(8960, S), area(9216, S)
        ones_d = area(9472, P)
        tmp_c = area(9600, TT, D)
        c_odd = area(11648, S)
        c_diag = area(11904, 15, P)
        PE_TAPS = (1, 4, 7)
        TAPS_AFTER = {3: (0,), 7: (1, 2)}

        def pe_conv():
            n = "mid11"
            pe_pre(n)
            for c in range(4):
                wa, wg = chunk(f"c.a{c}", TE), chunk(f"c.g{c}", TE)
                for f in range(2):
                    o = open_tile(f"c.{2 * c + f}")
                    for half, w in ((0, wa), (1, wg)):
                        for k in range(KD):
                            i = mm(o[:, S * half:S * half + S], w[:, k, P * f:P * f + P], x_fm[:, k, :], k == 0, k == KD - 1)
                    i.then_inc(pe_steps, TE.step(f"tile c.{2 * c + f}"))
                release(f"c.a{c}")
                release(f"c.g{c}")
                for n_f in TAPS_AFTER.get(2 * c + 1, ()):
                    f = PE_TAPS[n_f]
                    pe.wait_ge(dve_steps, count_of("acc ffn10 read"))
                    pe.wait_ge(dve_steps, count_of(f"read c.{f}"))
                    for k in range(CV_TAPS):
                        pe.wait_ge(act_steps, count_of(f"tap {f}.{k}"))
                        mm(acc[:, n_f, 0:S], c_diag[:, (CV_TAPS * n_f + k) % 15, :], z_pad[:, f, k:k + S], k == 0, k == CV_TAPS - 1).then_inc(
                            pe_steps, TE.step(f"tap used {CV_TAPS * n_f + k}"))
            for f in PE_TAPS:
                pe.wait_ge(act_steps, count_of(f"taps read {f}"))
            for name, src in (("mean", c_acc), ("var", c_sq)):
                pe.wait_ge(*by(f"{name} terms"))
                o = open_tile(f"c.{name}")
                for k in range(KD):
                    i = mm(o[:, 0:S], ones_d, src[:, k, :], k == 0, k == KD - 1)
                i.then_inc(pe_steps, TE.step(f"tile c.{name}"))
            pe.wait_ge(act_steps, count_of("c silu"))
            pe.wait_ge(dve_steps, count_of("acc ffn10 read"))
            pe_into_acc(n, [f"c.out{c}" for c in range(4)], lambda k: c_acc[:, k, :])

        def tap_of(f, k):
            i = KD * k + f
            return col_dw[:, i // 124, i % 124:i % 124 + 1]

        def act_conv():
            n = "mid11"
            act_pre(n)
            for f in range(KD):
                o = tile_of(AC, f"c.{f}")
                if f >= 2:
                    act.wait_ge(dve_steps, count_of(f"read c.{f - 2}"))
                act.activation(c_sg[:, f % 2, :], o[:, S:2 * S], ACT.Sigmoid, bias=col[:, COL_BIN + 8 + f:COL_BIN + 9 + f]).then_inc(act_steps, AC.step(f"sg {f}"))
                for n_f in TAPS_AFTER.get(f, ()):
                    g = PE_TAPS[n_f]
                    for k in range(CV_TAPS):
                        i = CV_TAPS * n_f + k
                        if i >= 15:
                            act.wait_ge(pe_steps, count_of(f"tap used {i - 15}"))
                        act.activation(c_diag[:, i % 15, :], ident[:, :], ACT.Copy, scale=tap_of(g, k)).then_inc(act_steps, AC.step(f"tap {g}.{k}"))
            for n_f, f in enumerate(PE_TAPS):
                act.wait_ge(pe_steps, count_of(f"tap used {CV_TAPS * n_f + CV_TAPS - 1}"))
                act.activation(c_acc[:, f, :], acc[:, n_f, 0:S], ACT.Identity, bias=col[:, COL_DWB + f:COL_DWB + f + 1]).then_inc(
                    act_steps, AC.step(f"taps read {f}"))
            act.wait_ge(dve_steps, count_of("centred"))
            act.activation(c_sq, c_acc, ACT.Square).then_inc(act_steps, AC.step("var terms"))
            act.wait_ge(dve_steps, count_of("var c"))
            act.sqrt(c_rstd, c_rstd).then_inc(act_steps, AC.step("std c"))
            act.wait_ge(dve_steps, count_of("normed c"))
            for k in range(KD):
                act.activation(c_acc[:, k, :], c_acc[:, k, :], ACT.Silu, bias=col[:, COL_LNB + k:COL_LNB + k + 1],
                                       scale=col[:, COL_LNG + k:COL_LNG + k + 1]).then_inc(act_steps, AC.step("c silu"))
            for name in ffn_chunks(1, 2)[:EARLY]:
                act_split(name)
            act.wait_ge(dve_steps, count_of("c out"))
            act_post(n, lambda t: tmp_c[:, t, :])

        def dve_conv():
            n = "mid11"
            dve_pre(n)
            dve.memset(z_pad[:, :, 0:CP], 0.0).then_inc(dve_steps, VE.step())
            dve.memset(ones_d, 1.0 / D).then_inc(dve_steps, VE.step())

            def gated(f):
                dve.wait_ge(act_steps, count_of(f"sg {f}"))
                o = tile_of(VE, f"c.{f}")
                dve.scalar_tensor_tensor(z_pad[:, f, CP:], o[:, 0:S], col[:, COL_BIN + f:COL_BIN + f + 1], c_sg[:, f % 2, :],
                                         ALU.add, ALU.mult).then_inc(dve_steps, VE.step(f"read c.{f}"))

            gated(0)
            for f in range(KD):
                if f + 1 < KD:
                    gated(f + 1)
                if f in PE_TAPS:
                    continue
                dve.wait_ge(dve_steps, count_of(f"read c.{f}"))
                for k in range(CV_TAPS):
                    to = c_odd if k % 2 else c_acc[:, f, :]
                    if k >= 2:
                        dve.wait_ge(dve_steps, VE.n - 1)
                    if k == 0:
                        ins = dve.tensor_scalar(to, z_pad[:, f, 0:S], tap_of(f, 0), col[:, COL_DWB + f:COL_DWB + f + 1], ALU.mult, ALU.add)
                    elif k == 1:
                        ins = dve.tensor_scalar(to, z_pad[:, f, 1:1 + S], tap_of(f, 1), None, ALU.mult)
                    else:
                        ins = dve.scalar_tensor_tensor(to, z_pad[:, f, k:k + S], tap_of(f, k), to, ALU.mult, ALU.add)
                    ins.then_inc(dve_steps, VE.step())
                dve.wait_ge(dve_steps, VE.n)
                dve.tensor_tensor(c_acc[:, f, :], c_acc[:, f, :], c_odd, ALU.add).then_inc(dve_steps, VE.step("mean terms"))
                dve.wait_ge(dve_steps, VE.n)
            o = tile_of(VE, "c.mean")
            dve.tensor_copy(c_mean, o[:, 0:S]).then_inc(dve_steps, VE.step("read c.mean"))
            dve.wait_ge(dve_steps, VE.n)
            dve.tensor_tensor(c_acc, c_acc, c_mean.unsqueeze(1).to_broadcast([P, KD, S]), ALU.subtract).then_inc(dve_steps, VE.step("centred"))
            dve.wait_ge(dve_steps, VE.n)
            o = tile_of(VE, "c.var")
            dve.tensor_scalar(c_rstd, o[:, 0:S], RMS_EPS, None, ALU.add).then_inc(dve_steps, VE.step("read c.var"))
            dve.wait_ge(dve_steps, VE.n)
            found["var c"] = (VE.who, VE.n)
            dve.wait_ge(act_steps, count_of("std c"))
            dve.reciprocal(c_rstd, c_rstd).then_inc(dve_steps, VE.step())
            dve.wait_ge(dve_steps, VE.n)
            dve.tensor_tensor(c_acc, c_acc, c_rstd.unsqueeze(1).to_broadcast([P, KD, S]), ALU.mult).then_inc(dve_steps, VE.step("normed c"))
            dve.wait_ge(dve_steps, VE.n)
            for name in ffn_chunks(1, 2)[:EARLY]:
                dve_split(name)
            dve.wait_ge(pe_steps, count_of("acc mid11"))
            g = row("cvbout", VE)
            for t in range(TT):
                dve.tensor_tensor(tmp_c[:, t, :], acc_rows(t), g, ALU.add).then_inc(dve_steps, VE.step("c out"))
            dve.wait_ge(dve_steps, VE.n)
            found["row cvbout"] = (VE.who, VE.n)
            dve_post(n, lambda t: tmp_c[:, t, :], 1.0, area(0, TT, D), "ffn12")

        def pool_rows(a, b):
            plan = row_plan(A)
            for i in range(a, b):
                name, src = plan[i]
                if i >= ROWS:
                    pool.wait_ge(dve_steps, count_of("row " + plan[i - ROWS][0]))
                w = src.shape[0]
                pool.dma_start(rowb[:, i % ROWS, 0:w], src.partition_broadcast(P)).then_inc(sems[f"rows{i % ROWS}"], landed(f"rows{i % ROWS}", f"row loaded {name}"))

        @block.tensor
        def _(_):
            pe_setup()
            pe_memory()
            pe.wait_ge(tokens, count_of("x loaded"))
            pe_transposes("x0", x_tile)
            pe_params()
            pe_mlstm()
            for i in range(DEPTH):
                pe.wait_ge(dve_steps, count_of(f"x mix{i}"))
                pe_transposes(f"xp{i}t", x_tile)
                pe_peer(i)
                if i == 0:
                    pe.wait_ge(dve_steps, count_of("x peer0"))
                    pe_transposes("xrt", x_tile)
                    pe_rglru()
            pe_ffn(0, 0, "peer1")
            pe_s5()
            pe_ffn(0, 2, "mid01")
            pe_ffn(1, 0, "ffn02")
            pe_conv()
            pe_ffn(1, 2, "mid11")

        @block.scalar
        def _(_):
            act_param_loads()
            x_transposed("mem", AC, mem_fm)
            act_memory()
            x_transposed("x0", AC, x_fm)
            for i in range(DEPTH):
                if i == 0:
                    act_mlstm()
                else:
                    x_transposed("xrt", AC, x_fm)
                    act_rglru()
                act_sqrt(f"mix{i}", stat[:, 28:30])
                x_transposed(f"xp{i}t", AC, x_fm)
                act_peer(i)
                act_sqrt(f"peer{i}", stat[:, 28:30])
            act_ffn(0, 0)
            act_s5()
            act_ffn(0, 2, ffn_chunks(1, 0)[:EARLY])
            act_ffn(1, 0)
            act_conv()
            act_ffn(1, 2)

        @block.vector
        def _(_):
            x_transposed("mem", VE, mem_fm)
            x_transposed("x0", VE, x_fm)
            dve_setup()
            for i in range(DEPTH):
                if i == 0:
                    dve_mlstm()
                else:
                    x_transposed("xrt", VE, x_fm)
                    dve_rglru()
                x_transposed(f"xp{i}t", VE, x_fm)
                dve_peer(i)
            dve_ffn(0, 0, "mid01")
            dve_s5()
            dve_ffn(0, 2, "ffn10", ffn_chunks(1, 0)[:EARLY])
            dve_ffn(1, 0, "mid11")
            dve_conv()
            dve_ffn(1, 2, "end")

        @block.gpsimd
        def _(_):
            pool_setup()
            pool.wait_ge(pe_steps, count_of("tile kv0.k"))
            pool_rows(0, 4)
            pool_mlstm()
            pool_rows(4, 5)
            pool_peer(0)
            pool_rows(5, 9)
            pool_peer(1)
            pool_rows(9, 12)
            pool_s5()
            pool_rows(12, 16)

        @block.sync
        def _(sync):
            sp_inputs()
            sp_weights()
            sync.wait_ge(dve_steps, count_of("x end"))
            for t in range(TT):
                sync.dma_start(out[0, P * t:P * t + P, :], x_tok[:, t, :]).then_inc(stored, landed("stored", "stored"))
            sync.wait_ge(stored, 16 * TT)
    return found


_INS = ["x", "mem", "mlstm_w_in", "mlstm_b_gates", "mlstm_norm_g", "rglru_w_in", "rglru_conv_w", "rglru_conv_b", "rglru_w_a",
        "rglru_b_a", "rglru_w_x", "rglru_b_x", "rglru_lam", "xattn_w_kv", "w_out", "ln1_g", "ln1_b", "peer_w_q", "peer_subkeys",
        "peer_u", "peer_v", "ln2_g", "ln2_b", "norm_pre_2", "norm_post_2", "ffn_w1_2", "ffn_w3_2", "ffn_w2_2", "s5_w_in_2",
        "s5_a_re_2", "s5_a_im_2", "s5_log_dt_2", "s5_b_re_2", "s5_b_im_2", "s5_c_re_2", "s5_c_im_2", "s5_d_2", "s5_w_glu_2",
        "s5_b_glu_2", "s5_w_out_2", "cv_w_in_2", "cv_b_in_2", "cv_dw_2", "cv_dw_b_2", "cv_ln_g_2", "cv_ln_b_2", "cv_w_out_2",
        "cv_b_out_2"]


def kernel(**inputs):
    import concourse.bacc as bacc
    from concourse.bass_utils import run_bass_kernel_spmd

    def program(known):
        nc = bacc.Bacc("TRN2", target_bir_lowering=False, num_devices=1)
        A = {n: nc.dram_tensor(f"in_{n}", inputs[n].shape, F32, kind="ExternalInput").ap() for n in _INS}
        out = nc.dram_tensor("out", (1, S, D), F32, kind="ExternalOutput").ap()
        return nc, build(nc, A, out, known)

    _, counts = program(None)
    nc, again = program(counts)
    assert counts == again
    arrays = {f"in_{n}": np.ascontiguousarray(inputs[n]) for n in _INS}
    return run_bass_kernel_spmd(nc, [arrays], core_ids=[0]).results[0]["out"]
```
